# Optimizing a Trainium2 kernel written in Bass

```python
import math
import jax, jax.numpy as jnp
from jax import lax
import numpy as np

D_MODEL = 1024
BATCH = 1
SEQ = 256
DEPTH = 1

N_HEADS_A = 8
HEAD_DIM = 64
WIDTH_A = N_HEADS_A * HEAD_DIM
IDX_HEADS = 8
IDX_DIM = 64
TOPK_MAX = 256
N_HEADS_B = 8
WIDTH_B = N_HEADS_B * HEAD_DIM
N_BUCKETS = 32
MAX_DISTANCE = 128
PEER_HEADS = 8
N_KEYS = 128
N_EXPERTS = N_KEYS * N_KEYS
PEER_QDIM = 256
PEER_HALF = PEER_QDIM // 2
PEER_TOPK = 16
Q_BLOCK = 128
TOK_CHUNK = 128
EPS = 1e-6
IN_SPLIT_SIZES = (WIDTH_A, WIDTH_A, WIDTH_A,
                  IDX_HEADS * IDX_DIM, IDX_DIM, IDX_HEADS,
                  WIDTH_B, WIDTH_B, WIDTH_B,
                  D_MODEL, D_MODEL)
IN_WIDTH = 3 * WIDTH_A + IDX_HEADS * IDX_DIM + IDX_DIM + IDX_HEADS + 3 * WIDTH_B + 2 * D_MODEL


def rmsnorm(x, g):
    xf = x.astype(jnp.float32)
    y = xf * lax.rsqrt(jnp.mean(xf * xf, axis=-1, keepdims=True) + EPS)
    return (y * g.astype(jnp.float32)).astype(x.dtype)

def modulate(h, shift, scale):
    return h * (1 + scale[:, None, :]) + shift[:, None, :]

def t5_bucket(n):
    max_exact = N_BUCKETS // 2
    nf = jnp.maximum(n, 1).astype(jnp.float32)
    large = max_exact + (jnp.log(nf / max_exact) / math.log(MAX_DISTANCE / max_exact)
                         * (N_BUCKETS - max_exact)).astype(jnp.int32)
    large = jnp.minimum(large, N_BUCKETS - 1)
    return jnp.where(n < max_exact, n, large)

def to_blocks(a, nblk):
    b = a.shape[0]
    return a.reshape(b, nblk, Q_BLOCK, *a.shape[2:]).swapaxes(0, 1)

def dsa_attention(q, k, v, qi, ki, wi, rel_bias):
    b, s, h, dh = q.shape
    topk = min(TOPK_MAX, s // 4)
    nblk = s // Q_BLOCK
    key_pos = jnp.arange(s)
    idx_scale = (IDX_DIM ** -0.5) * (IDX_HEADS ** -0.5)

    def one_block(args):
        blk, qb, qib, wib = args
        q_pos = blk * Q_BLOCK + jnp.arange(Q_BLOCK)
        rel = jax.nn.relu(jnp.einsum('bthd,bsd->bths', qib, ki))
        score = jnp.einsum('bths,bth->bts', rel, wib).astype(jnp.float32) * idx_scale
        causal = key_pos[None, :] <= q_pos[:, None]
        score = jnp.where(causal[None], score, -jnp.inf)
        top_score, idx = lax.top_k(score, topk)
        valid = jnp.isfinite(top_score)
        kg = jax.vmap(lambda kk, ii: kk[ii])(k, idx)
        vg = jax.vmap(lambda vv, ii: vv[ii])(v, idx)
        logits = jnp.einsum('bthd,btkhd->bhtk', qb, kg).astype(jnp.float32) * (dh ** -0.5)
        bias = rel_bias[t5_bucket(q_pos[None, :, None] - idx)].astype(jnp.float32)
        logits = logits + jnp.moveaxis(bias, -1, 1)
        logits = jnp.where(valid[:, None], logits, -jnp.inf)
        p = jax.nn.softmax(logits, axis=-1).astype(v.dtype)
        return jnp.einsum('bhtk,btkhd->bthd', p, vg)

    out = lax.map(one_block, (jnp.arange(nblk), to_blocks(q, nblk), to_blocks(qi, nblk), to_blocks(wi, nblk)))
    return out.swapaxes(0, 1).reshape(b, s, h * dh)

def stick_breaking_attention(q, k, v):
    b, s, h, dh = q.shape
    nblk = s // Q_BLOCK
    key_pos = jnp.arange(s)

    def one_block(args):
        blk, qb = args
        q_pos = blk * Q_BLOCK + jnp.arange(Q_BLOCK)
        z = jnp.einsum('bthd,bshd->bhts', qb, k).astype(jnp.float32) * (dh ** -0.5)
        strict = (key_pos[None, :] < q_pos[:, None])[None, None]
        log_beta = jax.nn.log_sigmoid(z)
        log_one_minus = jnp.where(strict, log_beta - z, 0.0)
        suffix = lax.cumsum(log_one_minus, axis=3, reverse=True) - log_one_minus
        a = jnp.where(strict, jnp.exp(log_beta + suffix), 0.0).astype(v.dtype)
        return jnp.einsum('bhts,bshd->bthd', a, v)

    out = lax.map(one_block, (jnp.arange(nblk), to_blocks(q, nblk)))
    return out.swapaxes(0, 1).reshape(b, s, h * dh)

def peer_ffn(h, w_q, sub_keys, u, v):
    t, d = h.shape
    qh = (h @ w_q).reshape(t, PEER_HEADS, 2, PEER_HALF)
    s = jnp.einsum('thcd,hcnd->thcn', qh, sub_keys).astype(jnp.float32)
    s1, i1 = lax.top_k(s[:, :, 0], PEER_TOPK)
    s2, i2 = lax.top_k(s[:, :, 1], PEER_TOPK)
    cand = (s1[..., :, None] + s2[..., None, :]).reshape(t, PEER_HEADS, PEER_TOPK * PEER_TOPK)
    cand_idx = (i1[..., :, None] * N_KEYS + i2[..., None, :]).reshape(t, PEER_HEADS, PEER_TOPK * PEER_TOPK)
    top_s, pos = lax.top_k(cand, PEER_TOPK)
    eidx = jnp.take_along_axis(cand_idx, pos, axis=-1)
    g = jax.nn.softmax(top_s, axis=-1)
    nchunk = t // TOK_CHUNK

    def one_chunk(args):
        hc, ec, gc = args
        pre = jnp.einsum('cd,chkd->chk', hc, u[ec]).astype(jnp.float32)
        coef = (gc * jax.nn.gelu(pre, approximate=False)).astype(h.dtype)
        return jnp.einsum('chk,chkd->cd', coef, v[ec])

    out = lax.map(one_chunk, (h.reshape(nchunk, TOK_CHUNK, d),
                              eidx.reshape(nchunk, TOK_CHUNK, PEER_HEADS, PEER_TOPK),
                              g.reshape(nchunk, TOK_CHUNK, PEER_HEADS, PEER_TOPK)))
    return out.reshape(t, d)

def first_inputs(seed: int = 0) -> dict:
    key = jax.random.key(seed)
    ks = jax.random.split(key, 20)
    D = D_MODEL
    nrm = jax.random.normal
    x = nrm(ks[0], (BATCH, SEQ, D), jnp.float32)
    c = nrm(ks[1], (BATCH, D), jnp.float32)
    w_ada = nrm(ks[2], (DEPTH, D, 6 * D), jnp.float32) * (0.5 * D ** -0.5)
    b_ada = nrm(ks[3], (DEPTH, 6 * D), jnp.float32) * 0.01
    norm1_g = 1.0 + 0.05 * nrm(ks[4], (DEPTH, D), jnp.float32)
    norm2_g = 1.0 + 0.05 * nrm(ks[5], (DEPTH, D), jnp.float32)
    w_in = nrm(ks[6], (DEPTH, D, IN_WIDTH), jnp.float32) * D ** -0.5
    rel_bias = nrm(ks[7], (N_BUCKETS, N_HEADS_A), jnp.float32) * 0.5
    w_proj_a = nrm(ks[8], (DEPTH, WIDTH_A, D), jnp.float32) * WIDTH_A ** -0.5
    w_proj_b = nrm(ks[9], (DEPTH, WIDTH_B, D), jnp.float32) * WIDTH_B ** -0.5
    w_out = nrm(ks[10], (DEPTH, D, D), jnp.float32) * D ** -0.5
    peer_wq = nrm(ks[11], (DEPTH, D, PEER_HEADS * PEER_QDIM), jnp.float32) * D ** -0.5
    peer_sub_keys = nrm(ks[12], (DEPTH, PEER_HEADS, 2, N_KEYS, PEER_HALF), jnp.float32) * PEER_HALF ** -0.5
    peer_u = nrm(ks[13], (DEPTH, N_EXPERTS, D), jnp.float32) * D ** -0.5
    peer_v = nrm(ks[14], (DEPTH, N_EXPERTS, D), jnp.float32) * PEER_HEADS ** -0.5
    final_g = 1.0 + 0.05 * nrm(ks[15], (D,), jnp.float32)
    return {"x": x, "c": c, "w_ada": w_ada, "b_ada": b_ada, "norm1_g": norm1_g, "norm2_g": norm2_g,
            "w_in": w_in, "rel_bias": rel_bias, "w_proj_a": w_proj_a, "w_proj_b": w_proj_b,
            "w_out": w_out, "peer_wq": peer_wq, "peer_sub_keys": peer_sub_keys, "peer_u": peer_u,
            "peer_v": peer_v, "final_g": final_g}

def first_block(x, c, w_ada, b_ada, norm1_g, norm2_g, w_in, rel_bias, w_proj_a, w_proj_b, w_out,
              peer_wq, peer_sub_keys, peer_u, peer_v, final_g):
    b, s, d = x.shape
    offsets = []
    acc = 0
    for size in IN_SPLIT_SIZES[:-1]:
        acc += size
        offsets.append(acc)
    cond = jax.nn.silu(c)
    for l in range(DEPTH):
        mod = (cond @ w_ada[l] + b_ada[l]).reshape(b, 6, d)
        shift1, scale1, gate1, shift2, scale2, gate2 = [mod[:, i] for i in range(6)]

        hn = modulate(rmsnorm(x, norm1_g[l]), shift1, scale1)
        proj = hn @ w_in[l]
        qa, ka, va, qi, ki, wi, qb, kb, vb, ga, gb = jnp.split(proj, offsets, axis=-1)
        hd = (b, s, -1, HEAD_DIM)
        ya = dsa_attention(qa.reshape(hd), ka.reshape(hd), va.reshape(hd),
                           qi.reshape(b, s, IDX_HEADS, IDX_DIM), ki, wi, rel_bias)
        yb = stick_breaking_attention(qb.reshape(hd), kb.reshape(hd), vb.reshape(hd))
        merged = jax.nn.sigmoid(ga) * (ya @ w_proj_a[l]) + jax.nn.sigmoid(gb) * (yb @ w_proj_b[l])
        x = x + gate1[:, None, :] * (merged @ w_out[l])

        hn2 = modulate(rmsnorm(x, norm2_g[l]), shift2, scale2)
        f = peer_ffn(hn2.reshape(b * s, d), peer_wq[l], peer_sub_keys[l], peer_u[l], peer_v[l]).reshape(b, s, d)
        x = x + gate2[:, None, :] * f
    return rmsnorm(x, final_g)


MEM_LEN = 256
CONV_CH = D_MODEL // 4
MOBA_WIDTH = D_MODEL // 2
N_MOBA_HEADS = MOBA_WIDTH // HEAD_DIM
GLA_WIDTH = D_MODEL // 4
N_GLA_HEADS = 4
GLA_DV = GLA_WIDTH // N_GLA_HEADS
GLA_DK = GLA_DV // 2
GLA_KEY_WIDTH = N_GLA_HEADS * GLA_DK
GLA_GATE_RANK = 16
GLA_GATE_NORMALIZER = 16.0
GLA_CHUNK = 64
MOBA_BLOCK = 256
MOBA_TOPK = 3
MOBA_QCHUNK = 32
CONV_K = 3
N_XATTN_HEADS = 4
XATTN_WIDTH = N_XATTN_HEADS * HEAD_DIM
D_FF = 2752
IN_SPLITS = (CONV_CH, CONV_CH, CONV_CH,
             MOBA_WIDTH, MOBA_WIDTH, MOBA_WIDTH,
             GLA_KEY_WIDTH, GLA_KEY_WIDTH, GLA_WIDTH, GLA_WIDTH, GLA_GATE_RANK)
IN_PROJ_WIDTH = sum(IN_SPLITS)
MIX_WIDTH = CONV_CH + MOBA_WIDTH + GLA_WIDTH


def rmsnorm_2(x, g):
    xf = x.astype(jnp.float32)
    xf = xf * lax.rsqrt(jnp.mean(xf * xf, axis=-1, keepdims=True) + EPS)
    return xf.astype(x.dtype) * g

def causal_dwconv(u, w, b):
    T = u.shape[1]
    up = jnp.pad(u, ((0, 0), (CONV_K - 1, 0), (0, 0)))
    return sum(up[:, j:j + T] * w[j] for j in range(CONV_K)) + b

def alibi_slopes(n_heads):
    return jnp.asarray(2.0 ** (-8.0 * np.arange(1, n_heads + 1) / n_heads), dtype=jnp.float32)

def moba_attention(q, k, v, slopes):
    Bsz, T, H, hd = q.shape
    nblk = -(-T // MOBA_BLOCK)
    Tp = nblk * MOBA_BLOCK
    pad = ((0, 0), (0, Tp - T), (0, 0), (0, 0))
    q = jnp.pad(q, pad).transpose(0, 2, 1, 3) * (hd ** -0.5)
    k = jnp.pad(k, pad).transpose(0, 2, 1, 3)
    v = jnp.pad(v, pad).transpose(0, 2, 1, 3)
    kb = k.reshape(Bsz, H, nblk, MOBA_BLOCK, hd)
    vb = v.reshape(Bsz, H, nblk, MOBA_BLOCK, hd)
    kmean = jnp.mean(kb.astype(jnp.float32), axis=3)
    gate = jnp.einsum('bhtd,bhnd->bhtn', q.astype(jnp.float32), kmean)
    qblk = jnp.arange(Tp) // MOBA_BLOCK
    past = jnp.arange(nblk)[None, :] < qblk[:, None]
    gate = jnp.where(past, gate, -jnp.inf)
    topk = min(MOBA_TOPK, nblk)
    _, gidx = lax.top_k(gate, topk)
    bi = jnp.arange(Bsz)[:, None, None, None]
    hi = jnp.arange(H)[None, :, None, None]
    sl = slopes[None, :, None, None]

    def chunk(c):
        s0 = c * MOBA_QCHUNK
        qc = lax.dynamic_slice_in_dim(q, s0, MOBA_QCHUNK, axis=2)
        idx = lax.dynamic_slice_in_dim(gidx, s0, MOBA_QCHUNK, axis=2)
        qpos = s0 + jnp.arange(MOBA_QCHUNK)
        valid = jnp.arange(topk)[None, :] < (qpos // MOBA_BLOCK)[:, None]
        ksel = kb[bi, hi, idx]
        vsel = vb[bi, hi, idx]
        kpos_sel = idx[..., None] * MOBA_BLOCK + jnp.arange(MOBA_BLOCK)
        s_sel = jnp.einsum('bhqd,bhqnkd->bhqnk', qc, ksel).astype(jnp.float32)
        s_sel = s_sel - sl[..., None] * (qpos[:, None, None] - kpos_sel).astype(jnp.float32)
        s_sel = jnp.where(valid[None, None, :, :, None], s_sel, -jnp.inf)
        own = s0 // MOBA_BLOCK
        kown = lax.dynamic_slice_in_dim(k, own * MOBA_BLOCK, MOBA_BLOCK, axis=2)
        vown = lax.dynamic_slice_in_dim(v, own * MOBA_BLOCK, MOBA_BLOCK, axis=2)
        kpos_own = own * MOBA_BLOCK + jnp.arange(MOBA_BLOCK)
        rel = (qpos[:, None] - kpos_own[None, :])
        s_own = jnp.einsum('bhqd,bhkd->bhqk', qc, kown).astype(jnp.float32)
        s_own = s_own - sl * rel.astype(jnp.float32)
        s_own = jnp.where(rel >= 0, s_own, -jnp.inf)
        scores = jnp.concatenate(
            [s_sel.reshape(Bsz, H, MOBA_QCHUNK, topk * MOBA_BLOCK), s_own], axis=-1)
        p = jax.nn.softmax(scores, axis=-1).astype(v.dtype)
        p_sel = p[..., :topk * MOBA_BLOCK].reshape(Bsz, H, MOBA_QCHUNK, topk, MOBA_BLOCK)
        p_own = p[..., topk * MOBA_BLOCK:]
        return (jnp.einsum('bhqnk,bhqnkd->bhqd', p_sel, vsel)
                + jnp.einsum('bhqk,bhkd->bhqd', p_own, vown))

    nqc = Tp // MOBA_QCHUNK
    out = lax.map(chunk, jnp.arange(nqc))
    out = out.transpose(1, 0, 3, 2, 4).reshape(Bsz, Tp, H * hd)
    return out[:, :T]

def gla_attention(q, k, v, log_a):
    Bsz, T, H, dk = q.shape
    dv = v.shape[-1]
    n = T // GLA_CHUNK

    def to_chunks(a):
        return a.reshape(Bsz, n, GLA_CHUNK, H, a.shape[-1]).transpose(0, 3, 1, 2, 4)

    q = to_chunks(q) * (dk ** -0.5)
    k = to_chunks(k)
    vc = to_chunks(v)
    b = jnp.cumsum(to_chunks(log_a).astype(jnp.float32), axis=3)
    b_last = b[:, :, :, -1:, :]
    qd = q * jnp.exp(b)
    kd = k * jnp.exp(-b)
    kend = k * jnp.exp(b_last - b)
    causal = jnp.tril(jnp.ones((GLA_CHUNK, GLA_CHUNK), dtype=bool))
    A = jnp.where(causal, jnp.einsum('bhncd,bhnsd->bhncs', qd, kd), 0.0)
    o_intra = jnp.einsum('bhncs,bhnse->bhnce', A, vc)
    U = jnp.einsum('bhnsd,bhnse->bhnde', kend, vc)
    decay = jnp.exp(b_last[:, :, :, 0, :])

    def step(S, xs):
        g, u = xs
        return g[..., None] * S + u, S

    S0 = jnp.zeros((Bsz, H, dk, dv), dtype=U.dtype)
    _, S_prev = lax.scan(step, S0, (decay.transpose(2, 0, 1, 3), U.transpose(2, 0, 1, 3, 4)))
    S_prev = S_prev.transpose(1, 2, 0, 3, 4)
    o_inter = jnp.einsum('bhncd,bhnde->bhnce', qd, S_prev)
    o = (o_intra + o_inter).transpose(0, 2, 3, 1, 4).reshape(Bsz, T, H, dv)
    return o.astype(v.dtype)

def hybrid_mixer(h, w_in, sc_conv_w, sc_conv_b, gla_w_gate, gla_b_gate, gla_norm_g, w_out, slopes):
    Bsz, T, _ = h.shape
    proj = h @ w_in
    points = tuple(int(p) for p in np.cumsum(IN_SPLITS)[:-1])
    (c_b, c_c, c_h, m_q, m_k, m_v, g_q, g_k, g_v, g_o, g_lr) = jnp.split(proj, points, axis=-1)
    y_conv = c_b * causal_dwconv(c_c * c_h, sc_conv_w, sc_conv_b)
    hs = lambda a, nh: a.reshape(Bsz, T, nh, -1)
    y_moba = moba_attention(hs(m_q, N_MOBA_HEADS), hs(m_k, N_MOBA_HEADS), hs(m_v, N_MOBA_HEADS), slopes)
    log_a = jax.nn.log_sigmoid((g_lr @ gla_w_gate + gla_b_gate).astype(jnp.float32)) / GLA_GATE_NORMALIZER
    o = gla_attention(hs(g_q, N_GLA_HEADS), hs(g_k, N_GLA_HEADS), hs(g_v, N_GLA_HEADS),
                      hs(log_a, N_GLA_HEADS))
    y_gla = rmsnorm_2(o, gla_norm_g).reshape(Bsz, T, GLA_WIDTH) * jax.nn.silu(g_o)
    return jnp.concatenate([y_conv, y_moba, y_gla], axis=-1) @ w_out

def memory_cross_attention(h, mem_n, wq, wkv, wo):
    Bsz, T, _ = h.shape
    q = (h @ wq).reshape(Bsz, T, N_XATTN_HEADS, HEAD_DIM)
    k, v = jnp.split(mem_n @ wkv, 2, axis=-1)
    k = k.reshape(Bsz, -1, N_XATTN_HEADS, HEAD_DIM)
    v = v.reshape(Bsz, -1, N_XATTN_HEADS, HEAD_DIM)
    s = jnp.einsum('bthd,bmhd->bhtm', q, k).astype(jnp.float32) * (HEAD_DIM ** -0.5)
    p = jax.nn.softmax(s, axis=-1).astype(v.dtype)
    o = jnp.einsum('bhtm,bmhd->bthd', p, v).reshape(Bsz, T, XATTN_WIDTH)
    return o @ wo

def conv_ffn(h, w_up, conv_w, conv_b, w_down):
    u = causal_dwconv(h @ w_up, conv_w, conv_b)
    a, g = jnp.split(u, 2, axis=-1)
    return (jax.nn.silu(a) * g) @ w_down

def second_inputs(seed: int = 0) -> dict:
    key = jax.random.key(seed)
    ks = jax.random.split(key, 24)
    f32 = jnp.float32

    def w(k, shape, fan_in):
        return jax.random.normal(k, shape, f32) * (fan_in ** -0.5)

    def gain(k, shape):
        return 1.0 + 0.05 * jax.random.normal(k, shape, f32)

    def bias(k, shape):
        return 0.02 * jax.random.normal(k, shape, f32)

    L = DEPTH
    return {
        "x": jax.random.normal(ks[0], (BATCH, SEQ, D_MODEL), f32),
        "mem": jax.random.normal(ks[1], (BATCH, MEM_LEN, D_MODEL), f32),
        "norm_mix_g": gain(ks[2], (L, D_MODEL)),
        "w_in": w(ks[3], (L, D_MODEL, IN_PROJ_WIDTH), D_MODEL),
        "sc_conv_w": w(ks[4], (L, CONV_K, CONV_CH), CONV_K),
        "sc_conv_b": bias(ks[5], (L, CONV_CH)),
        "gla_w_gate": w(ks[6], (L, GLA_GATE_RANK, GLA_KEY_WIDTH), GLA_GATE_RANK),
        "gla_b_gate": bias(ks[7], (L, GLA_KEY_WIDTH)),
        "gla_norm_g": gain(ks[8], (L, GLA_DV)),
        "w_out": w(ks[9], (L, MIX_WIDTH, D_MODEL), MIX_WIDTH),
        "norm_xattn_g": gain(ks[10], (L, D_MODEL)),
        "norm_mem_g": gain(ks[11], (L, D_MODEL)),
        "xattn_wq": w(ks[12], (L, D_MODEL, XATTN_WIDTH), D_MODEL),
        "xattn_wkv": w(ks[13], (L, D_MODEL, 2 * XATTN_WIDTH), D_MODEL),
        "xattn_wo": w(ks[14], (L, XATTN_WIDTH, D_MODEL), XATTN_WIDTH),
        "norm_ffn_g": gain(ks[15], (L, D_MODEL)),
        "ffn_w_up": w(ks[16], (L, D_MODEL, 2 * D_FF), D_MODEL),
        "ffn_conv_w": w(ks[17], (L, CONV_K, 2 * D_FF), CONV_K),
        "ffn_conv_b": bias(ks[18], (L, 2 * D_FF)),
        "ffn_w_down": w(ks[19], (L, D_FF, D_MODEL), D_FF),
        "final_norm_g": gain(ks[20], (D_MODEL,)),
    }

def second_block(x, mem, norm_mix_g, w_in, sc_conv_w, sc_conv_b, gla_w_gate, gla_b_gate, gla_norm_g,
              w_out, norm_xattn_g, norm_mem_g, xattn_wq, xattn_wkv, xattn_wo, norm_ffn_g,
              ffn_w_up, ffn_conv_w, ffn_conv_b, ffn_w_down, final_norm_g):
    slopes = alibi_slopes(N_MOBA_HEADS)
    for l in range(DEPTH):
        h = rmsnorm_2(x, norm_mix_g[l])
        x = x + hybrid_mixer(h, w_in[l], sc_conv_w[l], sc_conv_b[l], gla_w_gate[l], gla_b_gate[l],
                             gla_norm_g[l], w_out[l], slopes)
        h = rmsnorm_2(x, norm_xattn_g[l])
        x = x + memory_cross_attention(h, rmsnorm_2(mem, norm_mem_g[l]), xattn_wq[l], xattn_wkv[l], xattn_wo[l])
        h = rmsnorm_2(x, norm_ffn_g[l])
        x = x + conv_ffn(h, ffn_w_up[l], ffn_conv_w[l], ffn_conv_b[l], ffn_w_down[l])
    return rmsnorm_2(x, final_norm_g)


def setup_inputs(seed=0):
    out = dict(first_inputs(seed))
    for name, value in second_inputs(seed + 1).items():
        if name != "x":
            out[name + "_2"] = value
    return out


def reference(
    x, c, w_ada, b_ada, norm1_g, norm2_g, w_in, rel_bias, w_proj_a, w_proj_b, w_out, peer_wq,
    peer_sub_keys, peer_u, peer_v, final_g, mem_2, norm_mix_g_2, w_in_2, sc_conv_w_2,
    sc_conv_b_2, gla_w_gate_2, gla_b_gate_2, gla_norm_g_2, w_out_2, norm_xattn_g_2,
    norm_mem_g_2, xattn_wq_2, xattn_wkv_2, xattn_wo_2, norm_ffn_g_2, ffn_w_up_2, ffn_conv_w_2,
    ffn_conv_b_2, ffn_w_down_2, final_norm_g_2,
):
    x = first_block(
        x, c, w_ada, b_ada, norm1_g, norm2_g, w_in, rel_bias, w_proj_a, w_proj_b, w_out,
        peer_wq, peer_sub_keys, peer_u, peer_v, final_g,
    )
    return second_block(
        x, mem_2, norm_mix_g_2, w_in_2, sc_conv_w_2, sc_conv_b_2, gla_w_gate_2, gla_b_gate_2,
        gla_norm_g_2, w_out_2, norm_xattn_g_2, norm_mem_g_2, xattn_wq_2, xattn_wkv_2,
        xattn_wo_2, norm_ffn_g_2, ffn_w_up_2, ffn_conv_w_2, ffn_conv_b_2, ffn_w_down_2,
        final_norm_g_2,
    )


_drawn_inputs = setup_inputs


def setup_inputs(seed=0):
    import zlib

    import numpy as np

    out = dict(_drawn_inputs(seed))
    spreads = {}
    factors = {'b_ada': 3.869,
     'norm1_g': 3.13,
     'norm2_g': 2.907,
     'sc_conv_b_2': 6.102,
     'gla_b_gate_2': 8.0,
     'gla_norm_g_2': 4.015,
     'norm_xattn_g_2': 8.0,
     'norm_mem_g_2': 7.302,
     'ffn_conv_b_2': 23.552,
     'norm_ffn_g_2': 8.0}
    for name, (base, spread) in spreads.items():
        noise = np.random.default_rng([zlib.crc32(name.encode()), seed]).standard_normal(out[name].shape)
        drawn = base * np.exp(spread * noise) if base else spread * noise
        out[name] = __import__('jax').numpy.asarray(drawn.astype(out[name].dtype))
    for name, factor in factors.items():
        out[name] = (out[name] * factor).astype(out[name].dtype)
    return out
```

```python
import math
from contextlib import ExitStack

import numpy as np

import concourse.bass as bass
from concourse import mybir
from concourse.alu_op_type import AluOpType as ALU

ACT = mybir.ActivationFunctionType
F32 = mybir.dt.float32
U32 = mybir.dt.uint32
AX = mybir.AxisListType.X

T = 256
NC = 2048
NEG = -1.0e30
LOW = -3.0e38
GONE = -3.4e38
EPS = 1e-6
BASE_SLOTS = 5


class Queues:

    def __init__(self, nc, ctx):
        self.nc = nc
        self.ctx = ctx
        self.names = ["tensor", "vector", "scalar", "gpsimd", "sync"]
        self.items = {n: [] for n in self.names}
        self.sems = {n: ctx.enter_context(nc.semaphore(f"done_{n}")) for n in self.names}
        self.count = {n: 0 for n in self.names}
        self.nload = 0

    def do(self, eng, fn, *after, inc=True, apart=False):
        if eng != "tensor" and not apart:
            after = after + ((eng, self.sems[eng], self.count[eng]),)
        self.items[eng].append((after, fn, self.sems[eng] if inc else None, 1))
        if inc:
            self.count[eng] += 1
        return (eng, self.sems[eng], self.count[eng])

    def load(self, eng, out, in_, *after):
        self.nload += 1
        sem = self.ctx.enter_context(self.nc.semaphore(f"dma{self.nload}"))
        return self.dma(eng, out, in_, sem, 1, *after)

    def dma(self, eng, out, in_, sem, nth, *after):
        e = self.engine(eng)
        self.items[eng].append((after, lambda: e.dma_start(out, in_), sem, 16))
        return (f"dma {id(sem)}", sem, 16 * nth)

    def engine(self, n):
        return {"tensor": self.nc.tensor, "vector": self.nc.vector, "scalar": self.nc.scalar,
                "gpsimd": self.nc.gpsimd, "sync": self.nc.sync}[n]

    def emit(self, eng, handle):
        seen = {}
        for after, fn, sem, by in self.items[eng]:
            for m in after:
                if m is None:
                    continue
                who, s, v = m
                if v > 0 and seen.get(who, 0) < v:
                    handle.wait_ge(s, v)
                    seen[who] = v
            ins = fn()
            if sem is not None:
                ins.then_inc(sem, by)


def build(nc, A, out, scratch):
    with ExitStack() as ctx:
        q = Queues(nc, ctx)
        V, S, G, TE = nc.vector, nc.scalar, nc.gpsimd, nc.tensor

        def sb(name, shape, dt=F32):
            return ctx.enter_context(nc.sbuf_tensor(name, shape, dt))

        PR = sb("PR", [128, 128 * 256])
        ringb = sb("ringb", [128, BASE_SLOTS * NC])
        xT = sb("xT", [128, 8, T])
        hT = sb("hT", [128, 8, T])
        AB = sb("AB", [128, 2048])
        cst = sb("cst", [128, 768])
        vecs = sb("vecs", [128, A["vecs"].shape[1]])
        mod = sb("mod", [128, 48])
        sm = sb("sm", [128, 256])
        cond = sb("cond", [128, 8])
        rT = sb("rT", [128, 2, T])
        banks = [ctx.enter_context(nc.psum_tensor(f"bank{i}", [128, 512], F32)) for i in range(8)]
        bank_free = [None] * 8
        bank_at = [0]

        held = set()

        def take(hold=False):
            while bank_at[0] % 8 in held:
                bank_at[0] += 1
            i = bank_at[0] % 8
            bank_at[0] += 1
            if hold:
                held.add(i)
            return i

        ident = cst[:, 0:128]
        ones = cst[:, 128:256]
        tri_gt = cst[:, 256:384]
        up_strict = cst[:, 384:512]
        bd64 = cst[:, 512:640]
        iota = cst[:, 640:768]

        def dve(fn, *after, **k):
            return q.do("vector", fn, *after, **k)

        def act(fn, *after, **k):
            return q.do("scalar", fn, *after, **k)

        def pool(fn, *after, **k):
            return q.do("gpsimd", fn, *after, **k)

        def pe(fn, *after, **k):
            return q.do("tensor", fn, *after, **k)

        def mm(o, l, r, start, stop, *after, inc=False):
            return pe(lambda: TE.matmul(o, l, r, start=start, stop=stop, skip_group_check=True), *after, inc=inc)

        slots = [ringb[:, i * NC:(i + 1) * NC] for i in range(BASE_SLOTS)]
        far = [PR[:, 32768 - (i + 1) * NC:32768 - i * NC] for i in range(4)]
        slot_ap = slots + far
        slot_sem = [ctx.enter_context(nc.semaphore(f"slot{i}")) for i in range(len(slot_ap))]
        slot_uses = [0] * len(slot_ap)
        slot_free = [None] * len(slot_ap)
        order = {"n": 0, "live": list(range(len(slot_ap)))}
        queue = []
        issued = []

        def plan(name, n, phase, width=NC):
            for i in range(n):
                queue.append((name, i, width, phase))

        def issue_next():
            name, i, width, phase = queue[len(issued)]
            live = order["live"] = list(range(len(slot_ap))) if phase == "wide" else list(range(BASE_SLOTS))
            s = live[order["n"] % len(live)]
            order["n"] += 1
            slot_uses[s] += 1
            m = q.dma("sync", slot_ap[s][:, 0:width], A[name][i], slot_sem[s], slot_uses[s], slot_free[s])
            slot_free[s] = "used"
            issued.append((s, m))

        taken = [0]

        def chunk(name):
            n = taken[0]
            taken[0] += 1
            assert queue[n][0] == name, (queue[n], name)
            issue_next()
            assert len(issued) == n + 1
            s, m = issued[n]
            return slot_ap[s], m, s

        def release(s, mark):
            slot_free[s] = mark

        l_cst = q.load("scalar", cst[:, :], A["cst"])
        l_vecs = q.load("scalar", vecs[:, :], A["vecs"])
        l_x = q.load("scalar", xT[:, :, :], A["xT"])
        VO = A["voff"]

        def vec(name, j, n=1):
            o = VO[name] + j
            return vecs[:, o:o + n]

        off = [0]

        def scr(n):
            a = off[0]
            off[0] += n
            return PR[:, a:a + n]

        def tri3(ap, n):
            return ap.rearrange("p (a b) -> p a b", a=n)

        m = act(lambda: S.activation(sm[:, 0:8], vec("c", 0, 8), ACT.Exp, scale=-1.0), l_vecs)
        m = dve(lambda: V.tensor_scalar(sm[:, 8:16], sm[:, 0:8], 1.0, None, ALU.add), m)
        m = dve(lambda: V.reciprocal(sm[:, 16:24], sm[:, 8:16]), m)
        m_cond = dve(lambda: V.tensor_tensor(cond[:, :], vec("c", 0, 8), sm[:, 16:24], ALU.mult), m)

        def ada(c0, c1):
            b = take()
            for c in range(c0, c1):
                w, lw, s = chunk("w_ada")
                for j in range(2):
                    for k in range(8):
                        col = 2 * (c - c0) + j
                        last = mm(banks[b][:, col:col + 1], w[:, j * 1024 + k * 128:j * 1024 + (k + 1) * 128],
                                  cond[:, k:k + 1], k == 0, k == 7, lw, m_cond, bank_free[b], inc=(k == 7))
                release(s, last)
            n = 2 * (c1 - c0)
            a = 2 * c0
            m = dve(lambda: V.tensor_tensor(mod[:, a:a + n], banks[b][:, 0:n], vec("b_ada", a, n), ALU.add), last)
            bank_free[b] = m
            return m

        def norm(src, dst, sq, gname, m_src, m_free, scale_col=None, shift=None):
            b = take()
            m = act(lambda: S.activation(sq, src[:, :, :].rearrange("p a b -> p (a b)"), ACT.Square), *m_src, *m_free)
            for k in range(8):
                last = mm(banks[b][:, 0:T], ones, sq[:, k * T:(k + 1) * T], k == 0, k == 7,
                          m, l_cst, bank_free[b], inc=(k == 7))
            ms, r = rT[:, 0, :], rT[:, 1, :]
            t0 = sq[:, 0:T]
            t1 = sq[:, T:2 * T]
            a = dve(lambda: V.tensor_scalar(ms, banks[b][:, 0:T], 1.0 / 1024, EPS, ALU.mult, ALU.add), last, *m_free)
            bank_free[b] = a
            m = act(lambda: S.activation(t0, ms, ACT.Sqrt), a)
            m = dve(lambda: V.reciprocal(r, t0), m)
            m = newton(r, ms, t1, m)
            outs = []
            for j in range(8):
                gc = scale_col(j) if scale_col else vec(gname, j)
                n = dve(lambda j=j, gc=gc: V.scalar_tensor_tensor(out=dst[:, j, :], in0=src[:, j, :], scalar=gc, in1=r,
                                                                   op0=ALU.mult, op1=ALU.mult), m, l_vecs)
                if shift:
                    n = act(lambda j=j: S.activation(dst[:, j, :], dst[:, j, :], ACT.Identity, bias=shift(j)), n)
                outs.append(n)
            return outs

        def newton(r, ms, t, m):
            m = dve(lambda: V.tensor_tensor(t, r, r, ALU.mult), m)
            m = dve(lambda: V.tensor_tensor(t, t, ms, ALU.mult), m)
            m = dve(lambda: V.tensor_scalar(t, t, -0.5, 1.5, ALU.mult, ALU.add), m)
            return dve(lambda: V.tensor_tensor(r, r, t, ALU.mult), m)

        def lin(name, nchunks, rhs, m_rhs, evac, kt=8, c0=0):
            per = NC // (kt * 128)
            for c in range(c0, nchunks):
                w, lw, s = chunk(name)
                for h in range(per // 2):
                    b = take()
                    for j in range(2):
                        for k in range(kt):
                            o = (2 * h + j) * kt * 128 + k * 128
                            last = mm(banks[b][:, j * T:(j + 1) * T], w[:, o:o + 128], rhs(k),
                                      k == 0, k == kt - 1, lw, m_rhs(k), bank_free[b], inc=(k == kt - 1))
                    bank_free[b] = evac(c * (per // 2) + h, banks[b], last)
                release(s, last)

        def lin_nat(name, lhs, m_lhs, width, evac):
            b2 = [take(), take()]
            kk = NC // width
            for c in range(8 // kk):
                w, lw, s = chunk(name)
                for ki in range(kk):
                    k = c * kk + ki
                    for t in range(2):
                        last = mm(banks[b2[t]][:, 0:width], lhs(k, t), w[:, ki * width:(ki + 1) * width],
                                  k == 0, k == 7, lw, m_lhs(k), bank_free[b2[t]], inc=True)
                release(s, last)
            for t in range(2):
                bank_free[b2[t]] = evac(t, banks[b2[t]], last)

        hk = lambda k: hT[:, k, :]
        hkt = lambda k, t: hT[:, k, t * 128:(t + 1) * 128]

        def copy_to(dst, store, eng="act"):
            def evac(c, bank, m):
                d = dst[:, c * 512:(c + 1) * 512]
                if eng == "act":
                    n = act(lambda: S.copy(d, bank[:, :]), m)
                else:
                    n = dve(lambda: V.tensor_copy(d, bank[:, :]), m)
                store.append(n)
                return n
            return evac

        def attend(heads, qT, kT, vN, vw, yT, marks, bm, m_bm, W_of, ps, scale, sc, m_free):
            ybank = {}
            ydone = []
            L = [sc[:, i * 512:(i + 1) * 512] for i in range(3)]
            PT = [sc[:, 1536 + i * 512:1536 + (i + 1) * 512] for i in range(3)]
            lfree = [m_free] * 3
            ptfree = [m_free] * 3
            n = 0
            for pair in range(heads // 4):
                yb = [take(True), take(True)]
                fr = [bank_free[yb[0]], bank_free[yb[1]]]
                for t in range(2):
                    nk = W_of(t)
                    W = 128 * nk
                    for par in range(2):
                        hs = [4 * pair + par, 4 * pair + par + 2]
                        rows = slice(64 * par, 64 * par + 64)
                        b = take()
                        for i, h in enumerate(hs):
                            last = mm(banks[b][:, i * 256:i * 256 + W], qT[rows, h // 2, t * 128:(t + 1) * 128],
                                      kT[rows, h // 2, 0:W], True, True, *marks, bank_free[b], inc=(i == 1))
                        z = n % 3
                        n += 1
                        Lz = tri3(L[z], 2)[:, :, 0:W]
                        bz = tri3(banks[b][:, :], 2)[:, :, 0:W]
                        st = ps[:, 8 * z:8 * z + 8]
                        if bm:
                            m = dve(lambda Lz=Lz, bz=bz, h=hs[0], t=t, W=W: V.scalar_tensor_tensor(
                                out=Lz, in0=bz, scalar=scale, in1=bm(h, t, W), op0=ALU.mult, op1=ALU.add),
                                last, lfree[z], *m_bm)
                            bank_free[b] = m
                            m = dve(lambda Lz=Lz, st=st: V.tensor_reduce(st[:, 0:2], Lz, AX, ALU.max, negate=True), m)
                            src, esc = Lz, 1.0
                        else:
                            m = dve(lambda bz=bz, st=st: V.tensor_reduce(st[:, 2:4], bz, AX, ALU.max), last, lfree[z])
                            m = dve(lambda st=st: V.tensor_scalar(st[:, 0:2], st[:, 2:4], -scale, None, ALU.mult), m)
                            src, esc = bz, scale
                        for i in range(2):
                            e = act(lambda i=i, src=src, Lz=Lz, st=st, esc=esc: S.activation(
                                Lz[:, i, :], src[:, i, :], ACT.Exp, bias=st[:, i:i + 1], scale=esc,
                                accum_out=st[:, 4 + i:5 + i]), m, lfree[z])
                        if not bm:
                            bank_free[b] = e
                        m = dve(lambda st=st: V.reciprocal(st[:, 6:8], st[:, 4:6]), e)
                        for i in range(2):
                            x = pool(lambda i=i, Lz=Lz, st=st: G.tensor_scalar(Lz[:, i, :], Lz[:, i, :], st[:, 6 + i:7 + i],
                                                                               None, ALU.mult), m)
                        b = take()
                        for i in range(2):
                            for k in range(nk):
                                last = pe(lambda i=i, k=k, b=b, Lz=Lz: TE.transpose(
                                    banks[b][:, i * 256 + k * 128:i * 256 + k * 128 + 128],
                                    Lz[:, i, k * 128:(k + 1) * 128], ident), x, bank_free[b])
                        lfree[z] = last
                        PTz = tri3(PT[z], 2)[:, :, 0:W]
                        bz = tri3(banks[b][:, :], 2)[:, :, 0:W]
                        m = act(lambda PTz=PTz, bz=bz: S.copy(PTz, bz), last, ptfree[z])
                        bank_free[b] = m
                        for i, h in enumerate(hs):
                            for k in range(nk):
                                last = mm(banks[yb[i]][64 * par:64 * par + 64, t * 128:(t + 1) * 128],
                                          vN[:, k, 64 * h:64 * h + 64], tri3(PT[z], 2)[:, i, k * 128:(k + 1) * 128],
                                          (k == 0), k == nk - 1, m, fr[i], inc=True)
                        ptfree[z] = last
                for i in range(2):
                    j = 2 * pair + i
                    m = act(lambda i=i, j=j, yb=yb: S.copy(yT[:, j, :], banks[yb[i]][:, 0:T]), last)
                    bank_free[yb[i]] = m
                    held.discard(yb[i])
                    ydone.append(m)
            return ydone

        plan("w_ada", 8, "wide")
        for nm, k in (("w_qi", 2), ("w_ki", 1), ("w_qa", 2), ("w_ka", 2), ("w_va", 2), ("w_qb", 2), ("w_kb", 2),
                      ("w_vb", 2)):
            plan(nm, k, "wide", 1024 if nm == "w_ki" else NC)
        plan("w_ada", 16, "wide")
        plan("w_g", 8, "wide")
        plan("w_pa", 2, "wide")
        plan("w_pb", 2, "wide")
        plan("w_o", 4, "wide")
        plan("w_pq", 8, "near")
        plan("u", 64, "near")
        plan("v", 64, "near")
        for nm, k in (("w2_mq", 2), ("w2_mk", 2), ("w2_mv", 2), ("w2_cc", 1), ("w2_ch", 1), ("w2_cb", 1), ("w2_gk", 1),
                      ("w2_go", 1), ("w2_gv", 1), ("w2_lr", 1), ("w2_xk", 1), ("w2_xv", 1), ("w2_o", 4),
                      ("w2_xq", 1), ("w2_xo", 1)):
            plan(nm, k, "wide", {"w2_lr": 128}.get(nm, NC))
        plan("w_up", 22, "wide")
        plan("w_dn", 16, "wide", 1408)
        counts = {}
        for i, (nm, _, w, ph) in enumerate(queue):
            counts[nm] = counts.get(nm, -1) + 1
            queue[i] = (nm, counts[nm], w, ph)

        sq = scr(2048)
        qiT, kiT = tri3(scr(1024), 4), scr(256)
        qaT, kaT, va = scr(1024), scr(1024), scr(1024)
        qbT, kbT, vb = scr(1024), scr(1024), scr(1024)
        yaT, ybT = tri3(scr(1024), 4), tri3(scr(1024), 4)
        sg = tri3(scr(4096), 16)
        mg = tri3(sq, 8)
        bm = tri3(scr(3072), 8)
        madd = scr(384)
        sc_a = scr(3072)
        relb = sc_a[:, 0:2048]
        wk = scr(512)
        wk2 = scr(256)
        wiw = scr(64)
        assert off[0] <= 32768 - 4 * NC, off[0]

        m_mod1 = ada(0, 8)
        m = dve(lambda: V.tensor_scalar(sm[:, 32:40], mod[:, 8:16], 1.0, None, ALU.add), m_mod1)
        m_A1 = dve(lambda: V.tensor_tensor(sm[:, 24:32], sm[:, 32:40], vec("norm1_g", 0, 8), ALU.mult), m)

        l_oh = q.load("scalar", AB[0:32, 0:384], A["oh"])
        l_rb = q.load("scalar", AB[0:32, 384:392], A["rel_bias"])
        l_wi = q.load("scalar", wiw, A["w_wi"])
        reps, stores, l_bm = [], [], []
        rbs = sg.rearrange("p a b -> p (a b)")
        for h in range(8):
            o = 512 + 128 * h
            reps.append(dve(lambda h=h, o=o: V.tensor_copy(AB[0:32, o:o + 128],
                                                           AB[0:32, 384 + h:385 + h].broadcast_to((32, 128))), l_rb))
        for h in range(8):
            o = 512 + 128 * h
            b = take()
            rb = rbs[:, 384 * h:384 * h + 384]
            m = mm(banks[b][:, 0:384], AB[0:32, o:o + 128], AB[0:32, 0:384], True, True, reps[h], l_oh, bank_free[b], inc=True)
            w = dve(lambda b=b, rb=rb: V.tensor_copy(rb, banks[b][:, 0:384]), m)
            bank_free[b] = w
            stores.append(q.load("gpsimd", scratch[h], rb, w))
        for h in range(8):
            flat = scratch[h].rearrange("p n -> (p n)")
            src = flat[127:127 + 128 * 383].rearrange("(p n) -> p n", n=383)
            l_bm.append(q.load("gpsimd", bm[:, h, 128:384], src[:, 0:256], stores[h]))

        h1 = norm(xT, hT, sq, None, [l_x], [m_A1], scale_col=lambda j: sm[:, 24 + j:25 + j], shift=lambda j: mod[:, j:j + 1])
        mh = lambda k: h1[k]

        qi_m = []
        lin("w_qi", 2, hk, mh, copy_to(qiT.rearrange("p a b -> p (a b)"), qi_m))
        b = take()
        w, lw, s = chunk("w_ki")
        for k in range(8):
            last = mm(banks[b][:, 0:T], w[:, k * 128:(k + 1) * 128], hk(k), k == 0, k == 7, lw, bank_free[b], inc=(k == 7))
        release(s, last)
        m_ki = act(lambda b=b: S.copy(kiT, banks[b][:, 0:T]), last)
        bank_free[b] = m_ki
        b = take()
        for t in range(2):
            for k in range(8):
                last = mm(banks[b][:, 8 * t:8 * t + 8], hkt(k, t), wiw[:, 8 * k:8 * k + 8], k == 0, k == 7, l_wi,
                          bank_free[b], inc=(k == 7))
        m_wi = dve(lambda b=b: V.tensor_scalar(sm[:, 48:64], banks[b][:, 0:16], (64 ** -0.5) * (8 ** -0.5), None, ALU.mult), last)
        bank_free[b] = m_wi

        m_rel_free = None
        for t in range(2):
            W = 128 * (t + 1)
            rel = relb.rearrange("p (a b) -> p a b", a=8)[:, :, 0:W]
            mr = []
            for par in range(2):
                for g in range(2):
                    b = take()
                    hs = [par + 4 * g, par + 4 * g + 2]
                    rows = slice(64 * par, 64 * par + 64)
                    for i, h in enumerate(hs):
                        last = mm(banks[b][:, i * 256:i * 256 + W], qiT[rows, h // 2, t * 128:(t + 1) * 128],
                                  kiT[rows, 0:W], True, True, qi_m[-1], m_ki, bank_free[b], inc=(i == 1))
                    m = act(lambda b=b, h=hs[0], rel=rel, W=W: S.activation(
                        rel[:, h:h + 3:2, :], tri3(banks[b][:, :], 2)[:, :, 0:W], ACT.Relu), last, m_rel_free)
                    bank_free[b] = m
                    mr.append(m)
            acc = wk[:, 0:W]
            m = dve(lambda rel=rel, acc=acc, t=t: V.tensor_scalar(acc, rel[:, 0, :], sm[:, 48 + 8 * t:49 + 8 * t], None, ALU.mult),
                    mr[-1], m_wi)
            for h in range(1, 8):
                m = dve(lambda rel=rel, acc=acc, t=t, h=h: V.scalar_tensor_tensor(
                    out=acc, in0=rel[:, h, :], scalar=sm[:, 48 + 8 * t + h:49 + 8 * t + h], in1=acc,
                    op0=ALU.mult, op1=ALU.add), m)
            m_rel_free = m
            m = pool(lambda acc=acc, W=W, t=t: G.affine_select(out=acc, in_=acc, compare_op=ALU.is_ge, fill=LOW, base=128 * t,
                                                              pattern=[[-1, W]], channel_multiplier=1), m)
            for r in range(8):
                m = dve(lambda acc=acc: V.max(sm[:, 64:72], acc), m)
                m = dve(lambda acc=acc: V.match_replace(acc, sm[:, 64:72], acc, GONE), m)
            a, e = (0, 128) if t == 0 else (128, 384)
            md = madd[:, a:e]
            m = dve(lambda acc=acc, md=md: V.tensor_scalar(md, acc, -3.2e38, NEG, ALU.is_gt, ALU.mult), m)
            m = pool(lambda md=md, W=W, t=t: G.affine_select(out=md, in_=md, compare_op=ALU.is_ge, fill=NEG, base=128 * t,
                                                            pattern=[[-1, W]], channel_multiplier=1), m)
            m_madd = m
        m0 = pool(lambda: G.tensor_tensor(bm[:, :, 0:128], bm[:, :, 256:384],
                                          madd[:, 0:128].rearrange("p (a b) -> p a b", a=1).broadcast_to((128, 8, 128)), ALU.add),
                  m_madd, *l_bm)
        m_bm = pool(lambda: G.tensor_tensor(bm[:, :, 128:384], bm[:, :, 128:384],
                                            madd[:, 128:384].rearrange("p (a b) -> p a b", a=1).broadcast_to((128, 8, 256)), ALU.add), m0)

        qa_m, ka_m, va_m, qb_m, kb_m, vb_m = [], [], [], [], [], []

        def nat_to(dst, width, store, eng="act"):
            def evac(t, bank, m):
                n = act(lambda: S.copy(dst[:, t * width:(t + 1) * width], bank[:, 0:width]), m)
                store.append(n)
                return n
            return evac

        lin("w_qa", 2, hk, mh, copy_to(qaT, qa_m))
        lin("w_ka", 2, hk, mh, copy_to(kaT, ka_m))
        lin_nat("w_va", hkt, mh, 512, nat_to(va, 512, va_m))
        lin("w_qb", 2, hk, mh, copy_to(qbT, qb_m))
        lin("w_kb", 2, hk, mh, copy_to(kbT, kb_m))
        lin_nat("w_vb", hkt, mh, 512, nat_to(vb, 512, vb_m))
        m_mod2 = ada(8, 24)

        sg_m = []

        def gate(c, bank, m):
            d = sg[:, 2 * c:2 * c + 2, :].rearrange("p a b -> p (a b)")
            e = act(lambda: S.activation(d, bank[:, :], ACT.Exp, scale=-1.0), m, *stores)
            x = dve(lambda: V.tensor_scalar(d, d, 1.0, None, ALU.add), e)
            sg_m.append(dve(lambda: V.reciprocal(d, d), x))
            return e

        lin("w_g", 8, hk, mh, gate)

        qb3, kb3, vb3 = tri3(qbT, 4), tri3(kbT, 4), tri3(vb, 2)
        m_yb = []
        bufs = [[sq[:, 0:384], sq[:, 384:768], sq[:, 768:1152]], [sc_a[:, 0:384], sc_a[:, 384:768], sc_a[:, 768:1152]]]
        buf_free = [None, None]
        yb_bank = None
        for h in range(8):
            rows = slice(64 * (h % 2), 64 * (h % 2) + 64)
            z0, z1, z2 = bufs[h % 2]
            b = take()
            mm(banks[b][:, 0:256], kb3[rows, h // 2, 0:128], qb3[rows, h // 2, :], True, True,
               qb_m[-1], kb_m[-1], bank_free[b])
            last = mm(banks[b][:, 256:384], kb3[rows, h // 2, 128:256], qb3[rows, h // 2, 128:256], True, True, inc=True)
            zp = banks[b][:, 0:384]
            free = buf_free[h % 2]
            if h == 1:
                free = m_rel_free
            mab = m = act(lambda zp=zp, z0=z0: S.activation(z0, zp, ACT.Abs, scale=0.125), last, free)
            m = act(lambda z0=z0: S.activation(z0, z0, ACT.Exp, scale=-1.0), m)
            m = act(lambda z0=z0: S.activation(z0, z0, ACT.Ln, bias=1.0), m)
            n = dve(lambda zp=zp, z1=z1: V.tensor_scalar(z1, zp, 0.125, 0.0, ALU.mult, ALU.min), mab, free)
            n = dve(lambda z0=z0, z1=z1: V.tensor_tensor(z1, z1, z0, ALU.subtract), n, m)
            m = dve(lambda zp=zp, z1=z1, z2=z2: V.scalar_tensor_tensor(out=z2, in0=zp, scalar=-0.125, in1=z1,
                                                                      op0=ALU.mult, op1=ALU.add), n)
            bank_free[b] = m
            m = pool(lambda z2=z2: G.tensor_tensor(z2[:, 0:128], z2[:, 0:128], up_strict, ALU.mult), m, l_cst)
            m = pool(lambda z2=z2: G.tensor_tensor(z2[:, 256:384], z2[:, 256:384], up_strict, ALU.mult), m)
            b = take()
            mm(banks[b][:, 0:256], tri_gt, z2[:, 0:256], True, False, m, bank_free[b])
            mm(banks[b][:, 128:256], ones, z2[:, 256:384], False, True)
            last = mm(banks[b][:, 256:384], tri_gt, z2[:, 256:384], False, True, inc=True)
            m = dve(lambda b=b, z1=z1: V.tensor_tensor(z1, z1, banks[b][:, 0:384], ALU.add), last)
            bank_free[b] = m
            m = act(lambda z1=z1: S.activation(z1, z1, ACT.Exp), m)
            m = pool(lambda z1=z1: G.tensor_tensor(z1[:, 0:128], z1[:, 0:128], up_strict, ALU.mult), m)
            m = pool(lambda z1=z1: G.tensor_tensor(z1[:, 256:384], z1[:, 256:384], up_strict, ALU.mult), m)
            if h % 2 == 0:
                yb_bank = take(True)
            o = banks[yb_bank][64 * (h % 2):64 * (h % 2) + 64, :]
            mm(o[:, 0:256], vb3[:, 0, 64 * h:64 * h + 64], z1[:, 0:256], True, False, m, vb_m[-1], bank_free[yb_bank])
            last = mm(o[:, 128:256], vb3[:, 1, 64 * h:64 * h + 64], z1[:, 256:384], False, True, inc=True)
            buf_free[h % 2] = last
            if h % 2 == 1:
                m = act(lambda b=yb_bank, h=h: S.copy(ybT[:, h // 2, :], banks[b][:, 0:256]), last)
                bank_free[yb_bank] = m
                held.discard(yb_bank)
                m_yb.append(m)
        m_scfree = last

        def bm_a(h, t, W):
            a = 0 if t == 0 else 128
            return bm[:, h:h + 3:2, a:a + W]

        m_ya = attend(8, tri3(qaT, 4), tri3(kaT, 4), tri3(va, 2), 512, yaT, [qa_m[-1], ka_m[-1], va_m[-1]],
                      bm_a, [m_bm], lambda t: t + 1, sm[:, 80:104], 0.125, sc_a, m_scfree)

        m_mg = [None] * 4

        def merge_a(c, bank, m):
            d = mg[:, 2 * c:2 * c + 2, :].rearrange("p a b -> p (a b)")
            g = sg[:, 2 * c:2 * c + 2, :].rearrange("p a b -> p (a b)")
            m_mg[c] = dve(lambda: V.tensor_tensor(d, bank[:, :], g, ALU.mult), m, sg_m[-1])
            return m_mg[c]

        def merge_b(c, bank, m):
            d = mg[:, 2 * c:2 * c + 2, :].rearrange("p a b -> p (a b)")
            g = sg[:, 8 + 2 * c:8 + 2 * c + 2, :].rearrange("p a b -> p (a b)")
            x = dve(lambda: V.tensor_tensor(g, bank[:, :], g, ALU.mult), m)
            m_mg[c] = dve(lambda: V.tensor_tensor(d, d, g, ALU.add), x)
            return x

        lin("w_pa", 2, lambda k: yaT[:, k, :], lambda k: m_ya[k], merge_a, kt=4)
        lin("w_pb", 2, lambda k: ybT[:, k, :], lambda k: m_yb[k], merge_b, kt=4)

        m_x = []

        def resid(col):
            def evac(c, bank, m):
                for j in range(2):
                    i = 2 * c + j
                    if col is None:
                        n = dve(lambda i=i, j=j: V.tensor_tensor(xT[:, i, :], bank[:, j * T:(j + 1) * T], xT[:, i, :], ALU.add), m)
                    else:
                        n = dve(lambda i=i, j=j: V.scalar_tensor_tensor(out=xT[:, i, :], in0=bank[:, j * T:(j + 1) * T],
                                                                        scalar=mod[:, col + i:col + i + 1], in1=xT[:, i, :],
                                                                        op0=ALU.mult, op1=ALU.add), m)
                m_x.append(n)
                return n
            return evac

        lin("w_o", 4, lambda k: mg[:, k, :], lambda k: m_mg[k // 2], resid(16))

        m = dve(lambda: V.tensor_scalar(sm[:, 32:40], mod[:, 32:40], 1.0, None, ALU.add), m_mod2)
        m_A2 = dve(lambda: V.tensor_tensor(sm[:, 24:32], sm[:, 32:40], vec("norm2_g", 0, 8), ALU.mult), m)
        h2 = norm(xT, hT, sq, None, [m_x[-1]], [m_A2], scale_col=lambda j: sm[:, 24 + j:25 + j],
                  shift=lambda j: mod[:, 24 + j:25 + j])
        mh2 = lambda k: h2[k]

        o96 = 96 * 256
        SC = PR[:, o96:o96 + 4096].rearrange("p (t c n) -> p t c n", t=2, c=16)
        o = o96 + 4096
        cand = PR[:, o:o + 256]
        qh = [AB[:, 0:512], AB[:, 512:1024]]
        tv = PR[:, o + 512:o + 1024].rearrange("p (t c k) -> p t c k", t=2, c=16)
        ti = PR[:, o + 1024:o + 1536].rearrange("p (t c k) -> p t c k", t=2, c=16)
        tf = PR[:, o + 1536:o + 2048].rearrange("p (t c k) -> p t c k", t=2, c=16)
        eq = PR[:, o + 2048:o + 4096]
        cv2 = sb("cv", [128, 2, 128])
        cp2 = sb("cp", [128, 2, 128], U32)
        cpa = sb("cpa", [128, 128], U32)
        cpf = sb("cpf", [128, 2, 128])
        rt = sb("rt", [128, 3, 256])
        skt = PR[:, 80 * 256:80 * 256 + 2048]
        l_sk = q.load("scalar", skt, A["sub_keys"], m_x[-1])

        qh_free = [m_x[-1], m_x[-1]]
        m_s = []

        def peer_q(c, bank, m):
            z = qh[c % 2]
            e = act(lambda: S.copy(z, bank[:, :]), m, qh_free[c % 2])
            b = take()
            for t in range(2):
                for j in range(2):
                    last = mm(banks[b][:, (2 * t + j) * 128:(2 * t + j + 1) * 128],
                              z[:, j * T + t * 128:j * T + (t + 1) * 128],
                              skt[:, (2 * c + j) * 128:(2 * c + j + 1) * 128], True, True, e, l_sk, bank_free[b], inc=True)
            qh_free[c % 2] = last
            x = act(lambda: S.copy(SC[:, :, 2 * c:2 * c + 2, :], banks[b][:, :].rearrange("p (t j n) -> p t j n", t=2, j=2)), last)
            bank_free[b] = x
            m_s.append(x)
            return e

        lin("w_pq", 8, hk, mh2, peer_q)

        P3 = PR[:, :].rearrange("p (i t) -> p i t", t=T)
        m_gelu = None
        rt_m = []

        def pre(c, bank, m):
            nonlocal m_gelu
            m_gelu = act(lambda: S.activation(P3[:, 2 * c:2 * c + 2, :].rearrange("p a b -> p (a b)"), bank[:, :], ACT.Gelu),
                         m, rt_m[-1] if c >= 40 else None)
            return m_gelu

        lin("u", 32, hk, mh2, pre)

        top_m = []
        for t in range(2):
            cv, cp = cv2[:, t, :], cp2[:, t, :]
            ti_u = ti[:, t, :, :].bitcast(U32)
            for c in range(16):
                s_ = SC[:, t, c, :]
                m = dve(lambda s_=s_, t=t, c=c: V.max(tv[:, t, c, 0:8], s_), m_s[c // 2])
                dve(lambda s_=s_, ti_u=ti_u, t=t, c=c: V.max_index(ti_u[:, c, 0:8], tv[:, t, c, 0:8], s_), m)
                m = dve(lambda s_=s_, t=t, c=c: V.match_replace(s_, tv[:, t, c, 0:8], s_, GONE), m)
                m = dve(lambda s_=s_, t=t, c=c: V.max(tv[:, t, c, 8:16], s_), m)
                m = dve(lambda s_=s_, ti_u=ti_u, t=t, c=c: V.max_index(ti_u[:, c, 8:16], tv[:, t, c, 8:16], s_), m)
            mf = dve(lambda ti_u=ti_u, t=t: V.tensor_copy(tf[:, t, :, :], ti_u), m)
            prev = mf
            for h in range(8):
                a0 = tv[:, t, 2 * h, :].rearrange("p (k o) -> p k o", o=1).broadcast_to((128, 16, 16))
                a1 = tv[:, t, 2 * h + 1, :].rearrange("p (o k) -> p o k", o=1).broadcast_to((128, 16, 16))
                cs = slice(16 * h, 16 * h + 8)
                ct = slice(16 * h + 8, 16 * h + 16)
                m = dve(lambda a0=a0, a1=a1: V.tensor_tensor(cand.rearrange("p (a b) -> p a b", a=16), a0, a1, ALU.add), prev)
                m = dve(lambda cs=cs, cv=cv, cp=cp: V.max(cv[:, cs], cand), m)
                dve(lambda cs=cs, cv=cv, cp=cp: V.max_index(cp[:, cs], cv[:, cs], cand), m)
                m = dve(lambda cs=cs, cv=cv, cp=cp: V.match_replace(cand, cv[:, cs], cand, GONE), m)
                m = dve(lambda ct=ct, cv=cv, cp=cp: V.max(cv[:, ct], cand), m)
                prev = dve(lambda ct=ct, cv=cv, cp=cp: V.max_index(cp[:, ct], cv[:, ct], cand), m)
            top_m.append(prev)
        for t in range(2):
            cv, cp = cv2[:, t, :], cp2[:, t, :]
            prev = top_m[t]
            cv3 = cv[:, :].rearrange("p (h k) -> p h k", h=8)
            g3 = eq[:, 0:128].rearrange("p (h k) -> p h k", h=8)
            m = dve(lambda cv3=cv3, g3=g3: V.tensor_tensor(g3, cv3, cv3[:, :, 0:1].broadcast_to((128, 8, 16)), ALU.subtract), prev)
            m = act(lambda: S.activation(eq[:, 0:128], eq[:, 0:128], ACT.Exp), m)
            m = dve(lambda g3=g3: V.tensor_reduce(sm[:, 104:112], g3, AX, ALU.add), m)
            m = dve(lambda: V.reciprocal(sm[:, 112:120], sm[:, 104:112]), m)
            m = dve(lambda g3=g3, cv3=cv3: V.tensor_tensor(
                cv3, g3, sm[:, 112:120].rearrange("p (h o) -> p h o", o=1).broadcast_to((128, 8, 16)), ALU.mult), m)
            b = take()
            last = pe(lambda b=b, cv=cv: TE.transpose(banks[b][:, 256:384], cv, ident), m, bank_free[b])
            m = dve(lambda cp=cp: V.tensor_scalar(cpa[:, :], cp, 4, None, ALU.logical_shift_right))
            m = dve(lambda: V.tensor_copy(cpf[:, 0, :], cpa[:, :]), m)
            m = dve(lambda cp=cp: V.tensor_scalar(cpa[:, :], cp, 15, None, ALU.bitwise_and), m)
            m = dve(lambda: V.tensor_copy(cpf[:, 1, :], cpa[:, :]), m)
            for s2 in range(2):
                e4 = eq.rearrange("p (h k i) -> p h k i", h=8, k=16)
                e3 = eq.rearrange("p (a i) -> p a i", i=16)
                io = iota[:, 0:16].rearrange("p (o i) -> p o i", o=1).broadcast_to((128, 128, 16))
                ps_ = cpf[:, s2, :].rearrange("p (a o) -> p a o", o=1).broadcast_to((128, 128, 16))
                m = dve(lambda e3=e3, io=io, ps_=ps_: V.tensor_tensor(e3, io, ps_, ALU.is_equal), m)
                for h in range(8):
                    tk = tf[:, t, 2 * h + s2, :].rearrange("p (o i) -> p o i", o=1).broadcast_to((128, 16, 16))
                    mx = dve(lambda e4=e4, h=h, tk=tk: V.tensor_tensor(e4[:, h, :, :], e4[:, h, :, :], tk, ALU.mult), m)
                m = dve(lambda e3=e3, s2=s2: V.tensor_reduce(cpf[:, s2, :], e3, AX, ALU.add), mx)
            for s2 in range(2):
                last = pe(lambda s2=s2, b=b: TE.transpose(banks[b][:, s2 * 128:(s2 + 1) * 128], cpf[:, s2, :], ident), m)
            m = dve(lambda b=b, t=t: V.tensor_copy(rt[:, :, t * 128:(t + 1) * 128],
                                                   banks[b][:, 0:384].rearrange("p (a b) -> p a b", a=3)), last)
            bank_free[b] = m
            rt_m.append(m)

        lin("u", 64, hk, mh2, pre, c0=32)

        tb = [AB[:, 0:1024], AB[:, 1024:2048]]
        tb_free = [None, None]
        m_G = None
        built = {}

        def tables(g):
            z = tb[g % 2]
            for i in range(4):
                t = 4 * g + i
                ma = dve(lambda z=z, i=i, t=t: V.tensor_scalar(z[:, i * 128:(i + 1) * 128], iota, rt[:, 0, t:t + 1],
                                                               rt[:, 2, t:t + 1], ALU.is_equal, ALU.mult), tb_free[g % 2], rt_m[1])
                mb = pool(lambda z=z, i=i, t=t: G.tensor_scalar(z[:, 512 + i * 128:512 + (i + 1) * 128], iota, rt[:, 1, t:t + 1],
                                                                None, ALU.is_equal), tb_free[g % 2], rt_m[1])
                built[g, i] = (ma, mb)

        tables(0)
        for g in range(64):
            z = tb[g % 2]
            b = take()
            for i in range(4):
                last = mm(banks[b][:, i * 128:(i + 1) * 128], z[:, 512 + i * 128:512 + (i + 1) * 128],
                          z[:, i * 128:(i + 1) * 128], True, True, *built[g, i], bank_free[b], inc=True)
            tb_free[g % 2] = last
            if g < 63:
                tables(g + 1)
            d = P3[:, :, 4 * g:4 * g + 4].rearrange("p i t -> p t i")
            m_G = dve(lambda d=d, b=b: V.tensor_tensor(d, banks[b][:, :].rearrange("p (t i) -> p t i", t=4), d, ALU.mult),
                      last, m_gelu)
            bank_free[b] = m_G

        fb = [take() for _ in range(4)]
        for c in range(64):
            w, lw, s = chunk("v")
            for j in range(2):
                i = 2 * c + j
                for t in range(2):
                    for d in range(2):
                        last = mm(banks[fb[2 * t + d]][:, :], P3[:, i, t * 128:(t + 1) * 128],
                                  w[:, j * 1024 + d * 512:j * 1024 + (d + 1) * 512], i == 0, i == 127,
                                  lw, m_G, bank_free[fb[2 * t + d]], inc=(t == 1 and d == 1))
            release(s, last)
        m_pv = last
        for s in range(BASE_SLOTS, len(slot_ap)):
            slot_free[s] = m_pv
        fn = PR[:, 0:2048]
        m_f = []
        for i in range(4):
            m = act(lambda i=i: S.copy(fn[:, i * 512:(i + 1) * 512], banks[fb[i]][:, :]), m_pv)
            bank_free[fb[i]] = m
            m_f.append(m)
        m_x.clear()
        for d in range(4):
            b = take()
            for j in range(2):
                for t in range(2):
                    c = 2 * d + j
                    src = fn[:, t * 1024 + c * 128:t * 1024 + (c + 1) * 128]
                    last = pe(lambda b=b, j=j, t=t, src=src: TE.transpose(
                        banks[b][:, j * T + t * 128:j * T + (t + 1) * 128], src, ident), m_f[-1], bank_free[b])
            bank_free[b] = resid(40)(d, banks[b], last)

        off[0] = 2048
        sq2 = scr(2048)
        mqT, mkT, mv = scr(1024), scr(1024), scr(1024)
        ccT = scr(512)
        uT = scr(2 * 258)
        cbT = scr(512)
        gqk = scr(512)
        goT = scr(512)
        gv = scr(512)
        lrT = scr(256)
        memT = tri3(scr(2048), 8)
        xkT, xv = scr(512), scr(512)
        catT = tri3(scr(2048), 8)
        bmm = tri3(scr(3072), 8)
        sc_b = scr(3072)
        gt = scr(2560)
        assert off[0] <= 32768 - 4 * NC, off[0]
        x3 = norm(xT, xT, sq2, "final_g", [m_x[-1]], [])
        l_mem = q.load("scalar", memT, A["memT"], m_x[-1])
        l_bmm = q.load("scalar", bmm, A["bmm"], m_x[-1])
        hm = norm(memT, memT, sq2, "norm_mem_g", [l_mem], [x3[-1]])
        h3 = norm(xT, hT, sq2, "norm_mix_g", [x3[-1]], [hm[-1]])
        mh3 = lambda k: h3[k]

        z_m = []
        lin("w2_mq", 2, hk, mh3, copy_to(mqT, z_m))
        lin("w2_mk", 2, hk, mh3, copy_to(mkT, z_m))
        lin_nat("w2_mv", hkt, mh3, 512, nat_to(mv, 512, z_m))
        m_mo = z_m[-1]
        lin("w2_cc", 1, hk, mh3, copy_to(ccT, z_m))
        uv = uT.rearrange("p (a b) -> p a b", a=2)
        m_z = pool(lambda: G.memset(uv[:, :, 0:2], 0.0), m_pv)
        m_u = []

        def ch(c, bank, m):
            m_u.append(dve(lambda: V.tensor_tensor(uv[:, :, 2:258], tri3(bank[:, :], 2), tri3(ccT, 2), ALU.mult), m, z_m[-1]))
            return m_u[-1]

        lin("w2_ch", 1, hk, mh3, ch)

        def cb(c, bank, m):
            for j in range(2):
                t_ = sq2[:, j * 256:(j + 1) * 256]
                n = dve(lambda j=j, t_=t_: V.tensor_scalar(t_, uv[:, j, 2:258], vec("sc_w", 2 * 2 + j), vec("sc_b", j), ALU.mult, ALU.add),
                        m_u[-1], m_z, h3[-1])
                for tap in (1, 0):
                    n = dve(lambda j=j, t_=t_, tap=tap: V.scalar_tensor_tensor(
                        out=t_, in0=uv[:, j, tap:tap + 256], scalar=vec("sc_w", 2 * tap + j), in1=t_,
                        op0=ALU.mult, op1=ALU.add), n)
            n = dve(lambda: V.tensor_tensor(catT[:, 0:2, :], tri3(bank[:, :], 2), tri3(sq2[:, 0:512], 2), ALU.mult), n, m)
            m_u.append(n)
            return n

        lin("w2_cb", 1, hk, mh3, cb)
        m_conv = m_u[-1]
        g_m = []
        lin("w2_gk", 1, hk, mh3, copy_to(gqk, g_m))

        def go(c, bank, m):
            e = act(lambda: S.activation(gt[:, 0:512], bank[:, :], ACT.Exp, scale=-1.0), m)
            n = dve(lambda: V.tensor_scalar(gt[:, 0:512], gt[:, 0:512], 1.0, None, ALU.add), e)
            n = dve(lambda: V.reciprocal(gt[:, 0:512], gt[:, 0:512]), n)
            n = dve(lambda: V.tensor_tensor(goT, bank[:, :], gt[:, 0:512], ALU.mult), n)
            g_m.append(n)
            return n

        lin("w2_go", 1, hk, mh3, go)
        m_go = g_m[-1]
        lin_nat("w2_gv", hkt, mh3, 256, nat_to(gv, 256, g_m))
        m_gv = g_m[-1]
        b = take()
        w, lw, s = chunk("w2_lr")
        for k in range(8):
            last = mm(banks[b][0:16, 0:T], w[:, k * 16:(k + 1) * 16], hk(k), k == 0, k == 7, lw, bank_free[b], inc=(k == 7))
        release(s, last)
        m_lr = act(lambda b=b: S.copy(lrT[0:16, :], banks[b][0:16, 0:T]), last)
        bank_free[b] = m_lr
        mm_ = lambda k: hm[k]
        x_m = []
        lin("w2_xk", 1, lambda k: memT[:, k, :], mm_, copy_to(xkT, x_m))
        lin_nat("w2_xv", lambda k, t: memT[:, k, t * 128:(t + 1) * 128], mm_, 256, nat_to(xv, 256, x_m))

        l_g = q.load("scalar", gt[0:16, 1280:1408], A["w_gate"], m_x[-1])
        l_gb = q.load("scalar", gt[0:1, 1408:1536], A["b_gate"], m_x[-1])
        l_gc = q.load("scalar", gt[:, 1536:1792], A["gcst"], m_x[-1])
        tri64 = gt[:, 1536:1664]
        hmask = gt[:, 1664:1792]
        la = gt[:, 0:256]
        b = take()
        for t in range(2):
            o_ = banks[b][:, t * 128:(t + 1) * 128]
            mm(o_, lrT[0:16, t * 128:(t + 1) * 128], gt[0:16, 1280:1408], True, False, m_lr, l_g, bank_free[b])
            last = mm(o_, ones[0:1, :], gt[0:1, 1408:1536], False, True, l_gb, inc=True)
        zg = banks[b][:, 0:256]
        mab = m = act(lambda zg=zg: S.activation(la, zg, ACT.Abs), last, m_go)
        m = act(lambda: S.activation(la, la, ACT.Exp, scale=-1.0), m)
        m = act(lambda: S.activation(la, la, ACT.Ln, bias=1.0), m)
        n = dve(lambda zg=zg: V.tensor_scalar(gt[:, 256:512], zg, 0.0, None, ALU.min), mab)
        bank_free[b] = n
        n = dve(lambda: V.tensor_tensor(la, gt[:, 256:512], la, ALU.subtract), n, m)
        n = dve(lambda: V.tensor_scalar(la, la, 1.0 / 16.0, None, ALU.mult), n)
        b = take()
        for t in range(2):
            last = mm(banks[b][:, t * 128:(t + 1) * 128], la[:, t * 128:(t + 1) * 128], tri64, True, True, n, l_gc,
                      bank_free[b], inc=True)
        bT = gt[:, 256:512]
        m = act(lambda b=b: S.copy(bT, banks[b][:, 0:256]), last)
        bank_free[b] = m
        eb, en, kend = gt[:, 512:768], gt[:, 768:1024], gt[:, 1024:1280]
        m1 = act(lambda: S.activation(eb, bT, ACT.Exp), m)
        m2 = act(lambda: S.activation(en, bT, ACT.Exp, scale=-1.0), m)
        for c in range(4):
            m3 = act(lambda c=c: S.activation(kend[:, c * 64:(c + 1) * 64], bT[:, c * 64:(c + 1) * 64], ACT.Exp, scale=-1.0,
                                              bias=bT[:, c * 64 + 63:c * 64 + 64]), m)
        dec = sm[:, 120:124]
        m4 = act(lambda: S.activation(dec, bT[:, 63:256:64], ACT.Exp), m)
        gq, gk = gqk[:, 0:256], gqk[:, 256:512]
        n = dve(lambda: V.scalar_tensor_tensor(out=eb, in0=gq, scalar=32 ** -0.5, in1=eb, op0=ALU.mult, op1=ALU.mult), m1, g_m[0])
        dve(lambda: V.tensor_tensor(en, gk, en, ALU.mult), m2)
        m_qk = dve(lambda: V.tensor_tensor(kend, gk, kend, ALU.mult), m4)
        AT = sc_b[:, 0:1024].rearrange("p (h t c) -> p h t c", h=4, t=2)
        m_at = []
        for h in range(4):
            b = take()
            for t in range(2):
                last = mm(banks[b][:, t * 128:(t + 1) * 128], en[32 * h:32 * h + 32, t * 128:(t + 1) * 128],
                          eb[32 * h:32 * h + 32, t * 128:(t + 1) * 128], True, True, m_qk, bank_free[b], inc=True)
            m = act(lambda b=b, h=h: S.copy(AT[:, h, :, :], banks[b][:, 0:256].rearrange("p (t c) -> p t c", t=2)), last)
            bank_free[b] = m
            m = pool(lambda h=h: G.affine_select(out=AT[:, h, :, :], in_=AT[:, h, :, :], compare_op=ALU.is_ge, fill=0.0,
                                                 base=0, pattern=[[0, 2], [1, 128]], channel_multiplier=-1), m)
            a4 = AT[:, h, :, 64:128]
            m = pool(lambda a4=a4: G.affine_select(out=a4, in_=a4, compare_op=ALU.is_ge, fill=0.0,
                                                   base=-64, pattern=[[0, 2], [0, 64]], channel_multiplier=1), m)
            m_at.append(m)
        b = take()
        for t in range(2):
            last = pe(lambda t=t, b=b: TE.transpose(banks[b][:, t * 128:(t + 1) * 128], kend[:, t * 128:(t + 1) * 128], ident),
                      m_qk, bank_free[b])
        keN = sc_b[:, 1024:1280]
        m_ke = act(lambda b=b: S.copy(keN, banks[b][:, 0:256]), last)
        bank_free[b] = m_ke
        St = sc_b[:, 1280:1280 + 3 * 256].rearrange("p (c e) -> p c e", c=3)
        m_S = []
        hm2 = hmask.rearrange("p (h o) -> p h o", o=1)[:, 0:4, :].broadcast_to((128, 4, 64))
        for c in range(3):
            r = slice(64 * (c % 2), 64 * (c % 2) + 64)
            b = take()
            last = mm(banks[b][:, 0:256], keN[r, (c // 2) * 128:(c // 2) * 128 + 128], gv[r, (c // 2) * 256:(c // 2) * 256 + 256],
                      True, True, m_ke, m_gv, bank_free[b], inc=True)
            m = dve(lambda b=b, c=c: V.tensor_tensor(St[:, c, :].rearrange("p (h e) -> p h e", h=4),
                                                     banks[b][:, 0:256].rearrange("p (h e) -> p h e", h=4), hm2, ALU.mult), last)
            bank_free[b] = m
            if c:
                m = dve(lambda c=c: V.scalar_tensor_tensor(out=St[:, c, :], in0=St[:, c - 1, :], scalar=dec[:, c:c + 1],
                                                           in1=St[:, c, :], op0=ALU.mult, op1=ALU.add), m)
            m_S.append(m)
        oT = sc_b[:, 2048:2560].rearrange("p (a b) -> p a b", a=2)
        sqg = sc_b[:, 2560:3072]
        for pr in range(2):
            b = take()
            for t in range(2):
                for j in range(2):
                    h = 2 * pr + j
                    mm(banks[b][64 * j:64 * j + 64, t * 128:(t + 1) * 128], gv[:, t * 256 + 64 * h:t * 256 + 64 * h + 64],
                       AT[:, h, t, :], t == 0, False, m_at[h], m_gv, bank_free[b])
            for c in range(1, 4):
                last = mm(banks[b][:, c * 64:(c + 1) * 64], St[:, c - 1, pr * 128:(pr + 1) * 128],
                          eb[:, c * 64:(c + 1) * 64], False, True, m_S[c - 1], inc=True)
            m_o = act(lambda b=b, pr=pr: S.copy(oT[:, pr, :], banks[b][:, 0:256]), last)
            bank_free[b] = m_o
        oF = sc_b[:, 2048:2560]
        m = act(lambda: S.activation(sqg, oF, ACT.Square), m_o)
        b = take()
        last = mm(banks[b][:, :], bd64, sqg, True, True, m, bank_free[b], inc=True)
        ms = gt[:, 0:512]
        rr = gt[:, 512:1024]
        m = dve(lambda b=b: V.tensor_scalar(ms, banks[b][:, :], 1.0 / 64, EPS, ALU.mult, ALU.add), last)
        bank_free[b] = m
        m = act(lambda: S.activation(sqg, ms, ACT.Sqrt), m)
        m = dve(lambda: V.reciprocal(rr, sqg), m)
        m = newton(rr, ms, sqg, m)
        m = dve(lambda: V.scalar_tensor_tensor(out=oF, in0=oF, scalar=vec("gla_norm_g", 0), in1=rr, op0=ALU.mult, op1=ALU.mult), m)
        m_gla = dve(lambda: V.tensor_tensor(catT[:, 6:8, :].rearrange("p a b -> p (a b)"), oF, goT, ALU.mult), m, m_go)

        def bm_m(h, t, W):
            a = 0 if t == 0 else 128
            return bmm[:, h:h + 3:2, a:a + W]

        m_mb = attend(8, tri3(mqT, 4), tri3(mkT, 4), tri3(mv, 2), 512, catT[:, 2:6, :], [m_mo],
                      bm_m, [l_bmm], lambda t: t + 1, sm[:, 80:104], 0.125, sc_b, m_gla)
        m_cat = [m_conv, m_conv] + m_mb + [m_gla, m_gla]
        m_x.clear()
        lin("w2_o", 4, lambda k: catT[:, k, :], lambda k: m_cat[k], resid(None))

        h4 = norm(xT, hT, sq2, "norm_xattn_g", [m_x[-1]], [])
        xqT = gt[:, 0:512]
        x_q = []
        lin("w2_xq", 1, hk, lambda k: h4[k], copy_to(xqT, x_q))
        xo = tri3(gt[:, 512:1024], 2)
        m_xo = attend(4, tri3(xqT, 2), tri3(xkT, 2), tri3(xv, 2), 256, xo, [x_q[-1], x_m[-1]],
                      None, [], lambda t: 2, sm[:, 80:104], 0.125, sc_b, m_x[-1])
        m_x.clear()
        w, lw, s = chunk("w2_xo")
        for c in range(4):
            b = take()
            for j in range(2):
                for k in range(2):
                    o = (2 * c + j) * 256 + k * 128
                    last = mm(banks[b][:, j * T:(j + 1) * T], w[:, o:o + 128], xo[:, k, :], k == 0, k == 1, lw, m_xo[k],
                              bank_free[b], inc=(k == 1))
            bank_free[b] = resid(None)(c, banks[b], last)
        release(s, last)

        h5 = norm(xT, hT, sq2, "norm_ffn_g", [m_x[-1]], [])
        off[0] = 2048 + 2048
        act_t = tri3(scr(22 * 256), 22)
        tmp = [scr(1024), scr(1024)]
        m_act = []

        def ffn(c, bank, m):
            a, g = tmp[c % 2][:, 0:256], tmp[c % 2][:, 256:512]
            e = tmp[c % 2][:, 512:768]
            fr = m_act[c - 2] if c >= 2 else m_x[-1]
            marks = []
            for j, d in ((0, a), (1, g)):
                i = 2 * c + j
                z = bank[:, j * T:(j + 1) * T]
                n = act(lambda d=d, z=z, i=i: S.activation(d, z, ACT.Identity, bias=vec("f_b", i), scale=vec("f_w", 2 * 44 + i)), m, fr)
                marks.append(n)
            for j, d in ((0, a), (1, g)):
                i = 2 * c + j
                z = bank[:, j * T:(j + 1) * T]
                n = dve(lambda d=d, z=z, i=i: V.scalar_tensor_tensor(out=d[:, 1:256], in0=z[:, 0:255], scalar=vec("f_w", 44 + i),
                                                                     in1=d[:, 1:256], op0=ALU.mult, op1=ALU.add), marks[-1])
                n = dve(lambda d=d, z=z, i=i: V.scalar_tensor_tensor(out=d[:, 2:256], in0=z[:, 0:254], scalar=vec("f_w", i),
                                                                     in1=d[:, 2:256], op0=ALU.mult, op1=ALU.add), n)
                if j == 0:
                    ea = act(lambda a=a, e=e: S.activation(e, a, ACT.Exp, scale=-1.0), n)
            free = n
            p = dve(lambda a=a, g=g: V.tensor_tensor(g, a, g, ALU.mult), n)
            x = dve(lambda e=e: V.tensor_scalar(e, e, 1.0, None, ALU.add), ea)
            x = dve(lambda e=e: V.reciprocal(e, e), x)
            m_act.append(dve(lambda e=e, g=g, c=c: V.tensor_tensor(act_t[:, c, :], g, e, ALU.mult), x, p))
            return free

        lin("w_up", 22, hk, lambda k: h5[k], ffn)
        m_x.clear()
        for c in range(4):
            b = take()
            for j in range(2):
                for half in range(2):
                    w, lw, s = chunk("w_dn")
                    for kk in range(11):
                        k = half * 11 + kk
                        last = mm(banks[b][:, j * T:(j + 1) * T], w[:, kk * 128:(kk + 1) * 128], act_t[:, k, :],
                                  k == 0, k == 21, lw, m_act[k], bank_free[b], inc=(kk == 10))
                    release(s, last)
            bank_free[b] = resid(None)(c, banks[b], last)
        h6 = norm(xT, hT, sq2, "final_norm_g", [m_x[-1]], [])
        done = []
        for j in range(8):
            done.append(q.load("sync", out[:, j, :], hT[:, j, :], h6[j]))

        block = ctx.enter_context(nc.Block())

        @block.sync
        def _(e):
            q.emit("sync", e)
            for _, s_, v_ in done:
                e.wait_ge(s_, v_)

        @block.tensor
        def _(e):
            q.emit("tensor", e)

        @block.vector
        def _(e):
            q.emit("vector", e)

        @block.scalar
        def _(e):
            q.emit("scalar", e)

        @block.gpsimd
        def _(e):
            q.emit("gpsimd", e)


def bucket(n):
    me = 16
    nf = np.maximum(n, 1).astype(np.float32)
    large = me + (np.log(nf / np.float32(me)) / np.float32(math.log(128 / me)) * np.float32(16)).astype(np.int32)
    return np.where(n < me, n, np.minimum(large, 31))


def constants():
    p = np.arange(128)
    f = np.float32
    cst = np.concatenate([
        np.eye(128), np.ones((128, 128)), (p[:, None] > p[None, :]), (p[None, :] > p[:, None]),
        (p[:, None] // 64 == p[None, :] // 64), np.broadcast_to(p[None, :], (128, 128))], 1).astype(f)
    oh = np.zeros((32, 384), f)
    for col in range(384):
        n = 255 - col
        if n >= 0:
            oh[bucket(np.array(n)), col] = 1.0
    same = (p[:, None] // 64 == p[None, :] // 64) & (p[:, None] <= p[None, :])
    hm = np.zeros((128, 128), f)
    for h in range(4):
        hm[32 * h:32 * h + 32, h] = 1.0
    gc = np.concatenate([same.astype(f), hm], 1)
    bmm = np.full((128, 8, 384), NEG, f)
    for h in range(8):
        slope = f(2.0 ** -(h + 1))
        for t in range(2):
            q_, k_ = 128 * t + p[:, None], np.arange(128 * (t + 1))[None, :]
            v = np.where(q_ >= k_, -(slope * (q_ - k_).astype(f)), NEG)
            bmm[:, h, (0 if t == 0 else 128):(128 if t == 0 else 384)] = v
    return cst, oh, gc, bmm


def tiles(w, kt, per):
    K, N = w.shape
    a = w.reshape(kt, 128, N // 128, 128).transpose(2, 1, 0, 3).reshape(N // 128 // per, per, 128, kt * 128)
    return np.ascontiguousarray(a.transpose(0, 2, 1, 3).reshape(N // 128 // per, 128, per * kt * 128))


def rows(w, width):
    kk = NC // width
    a = w.reshape(8 // kk, kk, 128, width).transpose(0, 2, 1, 3)
    return np.ascontiguousarray(a.reshape(8 // kk, 128, NC))


def cols(v):
    v = v.reshape(-1)
    return v.reshape(-1, 128).T


def lay_out(i):
    f = {k: np.asarray(v) for k, v in i.items()}
    A = {}
    w = f["w_in"][0]
    o = np.cumsum([0, 512, 512, 512, 512, 64, 8, 512, 512, 512, 1024, 1024])
    part = [w[:, o[n]:o[n + 1]] for n in range(11)]
    A["w_ada"] = tiles(f["w_ada"][0], 8, 2)
    A["w_qa"], A["w_ka"], A["w_qi"] = tiles(part[0], 8, 2), tiles(part[1], 8, 2), tiles(part[3], 8, 2)
    A["w_ki"] = tiles(np.concatenate([part[4], part[4]], 1), 8, 1)
    A["w_wi"] = np.ascontiguousarray(part[5].reshape(8, 128, 8).transpose(1, 0, 2).reshape(128, 64))
    A["w_va"], A["w_vb"] = rows(part[2], 512), rows(part[8], 512)
    A["w_qb"], A["w_kb"] = tiles(part[6], 8, 2), tiles(part[7], 8, 2)
    A["w_g"] = tiles(np.concatenate([part[9], part[10]], 1), 8, 2)
    A["w_pa"], A["w_pb"] = tiles(f["w_proj_a"][0], 4, 4), tiles(f["w_proj_b"][0], 4, 4)
    A["w_o"] = tiles(f["w_out"][0], 8, 2)
    A["w_pq"] = tiles(f["peer_wq"][0], 8, 2)
    A["sub_keys"] = np.ascontiguousarray(f["peer_sub_keys"][0].reshape(16, 128, 128).transpose(2, 0, 1).reshape(128, 2048))
    A["u"] = np.ascontiguousarray(
        f["peer_u"][0].reshape(64, 2, 128, 8, 128).transpose(0, 4, 1, 3, 2).reshape(64, 128, 2048))
    A["v"] = np.ascontiguousarray(f["peer_v"][0].reshape(64, 2, 128, 1024).transpose(0, 2, 1, 3).reshape(64, 128, 2048))
    w = f["w_in_2"][0]
    o = np.cumsum([0, 256, 256, 256, 512, 512, 512, 128, 128, 256, 256, 16])
    p2 = [w[:, o[n]:o[n + 1]] for n in range(11)]
    A["w2_cb"], A["w2_cc"], A["w2_ch"] = (tiles(p2[n], 8, 2) for n in range(3))
    A["w2_mq"], A["w2_mk"], A["w2_mv"] = tiles(p2[3], 8, 2), tiles(p2[4], 8, 2), rows(p2[5], 512)
    A["w2_gk"] = tiles(np.concatenate([p2[6], p2[7]], 1), 8, 2)
    A["w2_gv"], A["w2_go"] = rows(p2[8], 256), tiles(p2[9], 8, 2)
    A["w2_lr"] = np.ascontiguousarray(p2[10].reshape(8, 128, 16).transpose(1, 0, 2).reshape(1, 128, 128))
    A["w2_o"] = tiles(f["w_out_2"][0], 8, 2)
    A["w2_xq"] = tiles(f["xattn_wq_2"][0], 8, 2)
    kv = f["xattn_wkv_2"][0]
    A["w2_xk"], A["w2_xv"] = tiles(kv[:, 0:256], 8, 2), rows(kv[:, 256:512], 256)
    A["w2_xo"] = tiles(f["xattn_wo_2"][0], 2, 8)
    pad = lambda a, n: np.concatenate([a, np.zeros((a.shape[0], n - a.shape[1]), a.dtype)], 1)

    def ag(a):
        x, y = pad(a[:, :2752], 2816).reshape(-1, 22, 1, 128), pad(a[:, 2752:], 2816).reshape(-1, 22, 1, 128)
        return np.concatenate([x, y], 2).reshape(a.shape[0], 5632)

    A["w_up"] = tiles(ag(f["ffn_w_up_2"][0]), 8, 2)
    dn = pad(f["ffn_w_down_2"][0].T, 2816).T
    A["w_dn"] = np.ascontiguousarray(dn.reshape(2, 11, 128, 8, 128).transpose(3, 0, 2, 1, 4).reshape(16, 128, 1408))
    A["xT"] = np.ascontiguousarray(f["x"][0].T.reshape(8, 128, 256).transpose(1, 0, 2))
    A["memT"] = np.ascontiguousarray(f["mem_2"][0].T.reshape(8, 128, 256).transpose(1, 0, 2))
    A["rel_bias"] = f["rel_bias"]
    A["w_gate"] = f["gla_w_gate_2"][0]
    A["b_gate"] = f["gla_b_gate_2"]
    parts = [("c", cols(f["c"])), ("b_ada", cols(f["b_ada"])), ("norm1_g", cols(f["norm1_g"])),
             ("norm2_g", cols(f["norm2_g"])), ("final_g", cols(f["final_g"])), ("norm_mix_g", cols(f["norm_mix_g_2"])),
             ("norm_xattn_g", cols(f["norm_xattn_g_2"])), ("norm_mem_g", cols(f["norm_mem_g_2"])),
             ("norm_ffn_g", cols(f["norm_ffn_g_2"])), ("final_norm_g", cols(f["final_norm_g_2"])),
             ("sc_w", cols(f["sc_conv_w_2"])), ("sc_b", cols(f["sc_conv_b_2"])),
             ("gla_norm_g", np.concatenate([f["gla_norm_g_2"], f["gla_norm_g_2"]], 1).T),
             ("f_w", cols(ag(f["ffn_conv_w_2"][0]))), ("f_b", cols(ag(f["ffn_conv_b_2"])))]
    voff, n = {}, 0
    for name, a in parts:
        voff[name] = n
        n += a.shape[1]
    A["vecs"] = np.ascontiguousarray(np.concatenate([a for _, a in parts], 1))
    A["cst"], A["oh"], A["gcst"], A["bmm"] = constants()
    return A, voff


def kernel(**inputs):
    import concourse.bacc as bacc
    from concourse.bass_utils import run_bass_kernel_spmd

    arrays, voff = lay_out(inputs)
    nc = bacc.Bacc("TRN2", target_bir_lowering=False, num_devices=1)
    A, feeds = {}, {}
    for name, a in arrays.items():
        A[name] = nc.dram_tensor(f"in_{name}", a.shape, mybir.dt.from_np(a.dtype), kind="ExternalInput").ap()
        feeds[f"in_{name}"] = a
    A["voff"] = voff
    scratch = nc.dram_tensor("skew", (8, 128, 384), F32, kind="Internal").ap()
    out = nc.dram_tensor("out_0", (128, 8, 256), F32, kind="ExternalOutput").ap()
    build(nc, A, out, scratch)
    r = run_bass_kernel_spmd(nc, [feeds], core_ids=[0])
    y = r.results[0]["out_0"]
    return np.ascontiguousarray(np.asarray(y).transpose(2, 1, 0).reshape(1, 256, 1024))
```

```python
import math
from contextlib import ExitStack

import numpy as np

import concourse.bass as bass
from concourse import mybir
from concourse.alu_op_type import AluOpType as ALU

ACT = mybir.ActivationFunctionType
F32 = mybir.dt.float32
U32 = mybir.dt.uint32
F32R = mybir.dt.float32r
AX = mybir.AxisListType.X

T = 256
NC = 2048
UNIT = 1024
NEG = -1.0e30
LOW = -3.0e38
GONE = -3.4e38
EPS = 1e-6


class Queues:

    def __init__(self, nc, ctx):
        self.nc = nc
        self.ctx = ctx
        self.names = ["tensor", "vector", "scalar", "gpsimd", "sync"]
        self.items = {n: [] for n in self.names}
        self.sems = {n: ctx.enter_context(nc.semaphore(f"done_{n}")) for n in self.names}
        self.count = {n: 0 for n in self.names}
        self.nload = 0

    def do(self, eng, fn, *after, inc=True, apart=False):
        if eng != "tensor" and not apart:
            after = after + ((eng, self.sems[eng], self.count[eng]),)
        self.items[eng].append((after, fn, self.sems[eng] if inc else None, 1))
        if inc:
            self.count[eng] += 1
        return (eng, self.sems[eng], self.count[eng])

    def load(self, eng, out, in_, *after):
        self.nload += 1
        sem = self.ctx.enter_context(self.nc.semaphore(f"dma{self.nload}"))
        return self.dma(eng, out, in_, sem, 1, *after)

    def dma(self, eng, out, in_, sem, nth, *after):
        e = self.engine(eng)
        self.items[eng].append((after, lambda: e.dma_start(out, in_), sem, 16))
        return (f"dma {id(sem)}", sem, 16 * nth)

    def engine(self, n):
        return {"tensor": self.nc.tensor, "vector": self.nc.vector, "scalar": self.nc.scalar,
                "gpsimd": self.nc.gpsimd, "sync": self.nc.sync}[n]

    def emit(self, eng, handle):
        seen = {}
        for after, fn, sem, by in self.items[eng]:
            for m in after:
                if m is None:
                    continue
                who, s, v = m
                if v > 0 and seen.get(who, 0) < v:
                    handle.wait_ge(s, v)
                    seen[who] = v
            ins = fn()
            if sem is not None:
                ins.then_inc(sem, by)


def build(nc, A, out, scratch):
    with ExitStack() as ctx:
        q = Queues(nc, ctx)
        V, S, G, TE = nc.vector, nc.scalar, nc.gpsimd, nc.tensor

        def sb(name, shape, dt=F32, where=ctx):
            return where.enter_context(nc.sbuf_tensor(name, shape, dt))

        ringb = sb("ringb", [128, 4, UNIT])
        split = sb("split", [128, 3, 2, UNIT], F32R)
        xT = sb("xT", [128, 8, T])
        H = sb("H", [128, 2, 8, T], F32R)
        cst = sb("cst", [128, 768])
        vecs = sb("vecs", [128, A["vecs"].shape[1]])
        mod = sb("mod", [128, 48])
        sm = sb("sm", [128, 160])
        cond = sb("cond", [128, 8])
        rT = sb("rT", [128, 5, T])
        banks = [ctx.enter_context(nc.psum_tensor(f"bank{i}", [128, 512], F32)) for i in range(8)]
        bank_free = [None] * 8
        bank_at = [0]
        held = set()

        def take():
            assert len(held) < 8
            while bank_at[0] % 8 in held:
                bank_at[0] += 1
            i = bank_at[0] % 8
            bank_at[0] += 1
            held.add(i)
            return i

        def free(b, mark):
            bank_free[b] = mark
            held.discard(b)

        def room(n=1):
            return 8 - len(held) >= n + 2

        ident = cst[:, 0:128]
        ones = cst[:, 128:256]
        tri_gt = cst[:, 256:384]
        up_strict = cst[:, 384:512]
        bd64 = cst[:, 512:640]
        iota = cst[:, 640:768]

        def dve(fn, *after, **k):
            return q.do("vector", fn, *after, **k)

        def act(fn, *after, **k):
            return q.do("scalar", fn, *after, **k)

        def pool(fn, *after, **k):
            return q.do("gpsimd", fn, *after, **k)

        def pe(fn, *after, **k):
            return q.do("tensor", fn, *after, **k)

        def mm(o, l, r, start, stop, *after, inc=False):
            return pe(lambda: TE.matmul(o, l, r, start=start, stop=stop, skip_group_check=True), *after, inc=inc)

        def mm3(o, l, r, start, stop, *after, inc=False):
            mm(o, l[0], r[0], start, False, *after)
            mm(o, l[0], r[1], False, False)
            return mm(o, l[1], r[0], False, stop, inc=inc)

        jobs = []

        def spawn(gen):
            jobs.append(gen)

        def pump(conc=3):
            for g in list(jobs[:conc]):
                if next(g, "end") == "end":
                    jobs.remove(g)

        def drain():
            while jobs:
                pump()

        slot_ap, slot_sem, slot_uses, slot_free = [], [], [], []
        sets = {}

        def add_slots(name, aps):
            sets[name] = list(range(len(slot_ap), len(slot_ap) + len(aps)))
            for ap in aps:
                slot_sem.append(ctx.enter_context(nc.semaphore(f"slot{len(slot_ap)}")))
                slot_ap.append(ap)
                slot_uses.append(0)
                slot_free.append(())

        add_slots("near", [ringb[:, i, :] for i in range(2)])
        add_slots("ab", [ringb[:, i, :] for i in (2, 3)])
        sets["four"] = sets["near"] + sets["ab"]
        AB = ringb[:, 2:4, :].rearrange("p a b -> p (a b)")
        queue, ready, turn = [], [], {}
        part = {}
        buf_free = [None] * 3
        nsplit = [0]

        def plan(name, n, where, kind="split", width=UNIT):
            for i in range(n):
                j = part.get(name, 0)
                part[name] = j + 1
                queue.append((name, j, width, where, kind))

        def prepare():
            name, j, width, where, kind = queue[len(ready)]
            ss = sets[where]
            s = ss[turn.get(where, 0) % len(ss)]
            turn[where] = turn.get(where, 0) + 1
            slot_uses[s] += 1
            w = A[name].shape[2]
            per = max(w // UNIT, 1)
            src = A[name][j // per][:, (j % per) * UNIT:(j % per) * UNIT + width]
            raw = slot_ap[s][:, 0:width]
            m = q.dma("sync", raw, src, slot_sem[s], slot_uses[s], *slot_free[s])
            slot_free[s] = None
            if kind == "raw":
                ready.append((raw, m, s))
                return
            b = nsplit[0] % 3
            nsplit[0] += 1
            hi, lo = split[:, b, 0, :], split[:, b, 1, :]
            mh = act(lambda: S.copy(hi[:, 0:width], raw), m, buf_free[b], apart=True)
            ml = dve(lambda: V.tensor_tensor(lo[:, 0:width], raw, hi[:, 0:width].bitcast(F32), ALU.subtract),
                     mh, buf_free[b], apart=True)
            slot_free[s] = (ml,)
            ready.append(((hi, lo), ml, b))

        taken = [0]

        def unit(name, conc=3):
            n = taken[0]
            taken[0] += 1
            assert queue[n][0] == name, (queue[n], name)
            while len(ready) < min(n + 3, len(queue)) and (
                    len(ready) <= n or (queue[len(ready)][4] == "split" and queue[n][4] == "split")):
                prepare()
            pump(conc)
            data, m, s = ready[n]

            def done(mark):
                if queue[n][4] == "raw":
                    slot_free[s] = (mark,)
                else:
                    buf_free[s] = mark
            return data, m, done

        l_vecs = q.load("scalar", vecs[:, :], A["vecs"])
        l_cst = q.load("scalar", cst[:, :], A["cst"])
        l_x = q.load("scalar", xT[:, :, :], A["xT"])
        VO = A["voff"]

        def vec(name, j, n=1):
            o = VO[name] + j
            return vecs[:, o:o + n]

        def tri3(ap, n):
            return ap.rearrange("p (a b) -> p a b", a=n)

        def flat(ap):
            return ap.rearrange("p a b -> p (a b)")

        m_cond = act(lambda: S.activation(cond[:, :], vec("c", 0, 8), ACT.Silu), l_vecs)

        def ada(c0, c1):
            b = take()
            for c in range(c0, c1):
                w, lw, done = unit("w_ada")
                for k in range(8):
                    last = mm(banks[b][:, c - c0:c - c0 + 1], w[:, k * 128:(k + 1) * 128],
                              cond[:, k:k + 1], k == 0, k == 7, lw, m_cond, bank_free[b], inc=(k == 7))
                done(last)
            m = dve(lambda: V.tensor_tensor(mod[:, c0:c1], banks[b][:, 0:c1 - c0], vec("b_ada", c0, c1 - c0), ALU.add),
                    last, l_vecs)
            free(b, m)
            return m

        def newton(r, ms, t, m):
            m = dve(lambda: V.tensor_tensor(t, r, r, ALU.mult), m)
            m = dve(lambda: V.tensor_tensor(t, t, ms, ALU.mult), m)
            m = dve(lambda: V.tensor_scalar(t, t, -0.5, 1.5, ALU.mult, ALU.add), m)
            return dve(lambda: V.tensor_tensor(r, r, t, ALU.mult), m)

        t_free = [None, None]

        def sumsq():
            st = {"b": take(), "k": 0}

            def add(src, m):
                k = st["k"]
                st["k"] += 1
                t = rT[:, 2 + k % 2, :]
                m = act(lambda: S.activation(t, src, ACT.Square), m, t_free[k % 2])
                t_free[k % 2] = st["last"] = mm(banks[st["b"]][:, 0:T], ones, t, k == 0, k == 7, m, l_cst,
                                                    bank_free[st["b"]], inc=True)
            st["add"] = add
            return st

        def norm(src, st, gain, m_free=(), shift=None, dst=None, keep=None):
            assert st["k"] == 8
            b = st["b"]
            ms, r, t0 = rT[:, 0, :], rT[:, 1, :], rT[:, 4, :]
            a = dve(lambda: V.tensor_scalar(ms, banks[b][:, 0:T], 1.0 / 1024, EPS, ALU.mult, ALU.add), st["last"], *m_free)
            free(b, a)
            m = act(lambda: S.activation(t0, ms, ACT.Sqrt), a)
            m = dve(lambda: V.reciprocal(r, t0), m)
            m = newton(r, ms, t0, m)
            outs = []
            for j in range(8):
                if keep is not None:
                    outs.append(dve(lambda j=j: V.scalar_tensor_tensor(out=keep[:, j, :], in0=src[:, j, :], scalar=gain(j), in1=r,
                                                                        op0=ALU.mult, op1=ALU.mult), m, l_vecs))
                    continue
                t = rT[:, 2 + j % 2, :]
                n = dve(lambda j=j, t=t: V.scalar_tensor_tensor(out=t, in0=src[:, j, :], scalar=gain(j), in1=r,
                                                                op0=ALU.mult, op1=ALU.mult), m, l_vecs, t_free[j % 2])
                hi, lo = dst[:, 0, j, :], dst[:, 1, j, :]
                if shift:
                    n = act(lambda hi=hi, t=t, j=j: S.activation(hi, t, ACT.Identity, bias=shift(j)), n)
                    n = dve(lambda hi=hi, lo=lo, t=t, j=j: V.scalar_tensor_tensor(
                        out=lo, in0=t, scalar=shift(j), in1=hi.bitcast(F32), op0=ALU.add, op1=ALU.subtract), n)
                else:
                    n = act(lambda hi=hi, t=t: S.copy(hi, t), n)
                    n = dve(lambda hi=hi, lo=lo, t=t: V.tensor_tensor(lo, t, hi.bitcast(F32), ALU.subtract), n)
                t_free[j % 2] = n
                outs.append(n)
            return outs

        def cut(hi, lo, src, *after):
            m = act(lambda: S.copy(hi, src), *after)
            return dve(lambda: V.tensor_tensor(lo, src, hi.bitcast(F32), ALU.subtract), m)

        def lin(name, ncols, rhs, m_rhs, evac, kt=8, conc=3, c0=0):
            at = {"left": 0}
            for p in range(c0 // 2, ncols // 2):
                b = None
                for j in range(2):
                    for k in range(kt):
                        if at["left"] == 0:
                            w, lw, done = unit(name, conc)
                            at.update(w=w, lw=lw, done=done, left=8)
                        if b is None:
                            b = take()
                        o = (8 - at["left"]) * 128
                        at["left"] -= 1
                        wh, wl = at["w"]
                        last = mm3(banks[b][:, j * T:(j + 1) * T], (wh[:, o:o + 128], wl[:, o:o + 128]), rhs(k),
                                   k == 0, k == kt - 1, at["lw"], m_rhs(k), bank_free[b],
                                   inc=(k == kt - 1 or at["left"] == 0))
                        if at["left"] == 0:
                            at["done"](last)
                evac(p, b, last)

        def lin_nat(name, lhs, m_lhs, width, evac):
            b2 = None
            kk = UNIT // width
            for c in range(8 // kk):
                w, lw, done = unit(name)
                b2 = b2 or [take(), take()]
                for ki in range(kk):
                    k = c * kk + ki
                    for t in range(2):
                        last = mm3(banks[b2[t]][:, 0:width], lhs(k, t),
                                   (w[0][:, ki * width:(ki + 1) * width], w[1][:, ki * width:(ki + 1) * width]),
                                   k == 0, k == 7, lw, m_lhs(k), bank_free[b2[t]], inc=True)
                done(last)
            for t in range(2):
                evac(t, b2[t], last)

        def of(X):
            return lambda k: (X[:, 0, k, :], X[:, 1, k, :])

        def of_t(X):
            return lambda k, t: (X[:, 0, k, t * 128:(t + 1) * 128], X[:, 1, k, t * 128:(t + 1) * 128])

        hk, hkt = of(H), of_t(H)

        def copy_to(dst, store):
            def evac(c, b, m):
                n = act(lambda: S.copy(dst[:, c * 512:(c + 1) * 512], banks[b][:, :]), m)
                store.append(n)
                free(b, n)
            return evac

        def nat_to(dst, width, store):
            def evac(t, b, m):
                n = act(lambda: S.copy(dst[:, t * width:(t + 1) * width], banks[b][:, 0:width]), m)
                store.append(n)
                free(b, n)
            return evac

        def attend(heads, qT, kT, vN, Y, y0, marks, bm, m_bm, W_of, st_all, scale, sc, m_free, ydone):
            lfree = [m_free] * 3
            ptfree = [m_free] * 3
            state = {"z": [0, 1, 2], "y": {}, "live": 0}

            def item(pair, t, par):
                while not state["z"] or (pair not in state["y"] and state["live"]):
                    yield
                z = state["z"].pop(0)
                L, PT = sc[:, z * 512:(z + 1) * 512], sc[:, 1536 + z * 512:1536 + (z + 1) * 512]
                nk = W_of(t)
                W = 128 * nk
                hs = [4 * pair + par, 4 * pair + par + 2]
                rows = slice(64 * par, 64 * par + 64)
                while not room(1 if pair in state["y"] else 3):
                    yield
                if pair not in state["y"]:
                    yb = [take(), take()]
                    state["y"][pair] = [yb, [bank_free[i] for i in yb], 0]
                    state["live"] = 1
                b = take()
                for i, h in enumerate(hs):
                    last = mm(banks[b][:, i * 256:i * 256 + W], qT[rows, h // 2, t * 128:(t + 1) * 128],
                              kT[rows, h // 2, 0:W], True, True, *marks(), bank_free[b], inc=(i == 1))
                Lz = tri3(L, 2)[:, :, 0:W]
                bz = tri3(banks[b][:, :], 2)[:, :, 0:W]
                st = st_all[:, 8 * z:8 * z + 8]
                if bm:
                    m = dve(lambda: V.scalar_tensor_tensor(out=Lz, in0=bz, scalar=scale, in1=bm(hs[0], t, W),
                                                           op0=ALU.mult, op1=ALU.add), last, lfree[z], *m_bm())
                    free(b, m)
                    m = dve(lambda: V.tensor_reduce(st[:, 0:2], Lz, AX, ALU.max, negate=True), m)
                    src, esc = Lz, 1.0
                else:
                    m = dve(lambda: V.tensor_reduce(st[:, 2:4], bz, AX, ALU.max), last, lfree[z])
                    m = dve(lambda: V.tensor_scalar(st[:, 0:2], st[:, 2:4], -scale, None, ALU.mult), m)
                    src, esc = bz, scale
                for i in range(2):
                    e = act(lambda i=i: S.activation(Lz[:, i, :], src[:, i, :], ACT.Exp, bias=st[:, i:i + 1], scale=esc,
                                                     accum_out=st[:, 4 + i:5 + i]), m, lfree[z])
                if not bm:
                    free(b, e)
                m = dve(lambda: V.reciprocal(st[:, 6:8], st[:, 4:6]), e)
                for i in range(2):
                    x = dve(lambda i=i: V.tensor_scalar(Lz[:, i, :], Lz[:, i, :], st[:, 6 + i:7 + i], None, ALU.mult), m)
                yield
                while not room(1):
                    yield
                b = take()
                for i in range(2):
                    for k in range(nk):
                        last = pe(lambda i=i, k=k: TE.transpose(
                            banks[b][:, i * 256 + k * 128:i * 256 + k * 128 + 128],
                            Lz[:, i, k * 128:(k + 1) * 128], ident), x, bank_free[b])
                lfree[z] = last
                PTz = tri3(PT, 2)
                m = act(lambda b=b: S.copy(PTz[:, :, 0:W], tri3(banks[b][:, :], 2)[:, :, 0:W]), last, ptfree[z])
                free(b, m)
                yield
                yb, fr, _ = state["y"][pair]
                for i, h in enumerate(hs):
                    for k in range(nk):
                        last = mm(banks[yb[i]][64 * par:64 * par + 64, t * 128:(t + 1) * 128],
                                  vN[:, k, 64 * h:64 * h + 64], PTz[:, i, k * 128:(k + 1) * 128],
                                  (k == 0), k == nk - 1, m, fr[i], inc=True)
                ptfree[z] = last
                state["z"].append(z)
                state["y"][pair][2] += 1
                if state["y"][pair][2] == 4:
                    state["live"] = 0
                    for i in range(2):
                        j = 2 * pair + i
                        m = cut(Y[:, 0, y0 + j, :], Y[:, 1, y0 + j, :], banks[yb[i]][:, 0:T], last)
                        free(yb[i], m)
                        ydone[j] = m

            items = [(pair, t, par) for pair in range(heads // 4) for t in range(2) for par in range(2)]

            def run():
                lanes = []
                left = list(items)
                while left or lanes:
                    if len(lanes) < 3 and left:
                        if not lanes or lanes[-1][1] > 0:
                            lanes.append([item(*left.pop(0)), 0])
                    for ln in list(lanes):
                        ln[1] += 1
                        if next(ln[0], "end") == "end":
                            lanes.remove(ln)
                    yield
            return run()

        def parted(w, where, kind="split", width=UNIT):
            for nm, k in w:
                plan(nm, k, where, kind, width)

        plan("w_ada", 4, "four", "raw")
        plan("w_ada", 12, "far", "raw")
        parted([("w_qi", 4), ("w_ki", 1), ("w_qb", 4), ("w_kb", 4), ("w_vb", 4), ("w_qa", 4), ("w_ka", 4), ("w_va", 4),
                ("w_g", 16)], "far")
        plan("w_ada", 32, "far", "raw")
        parted([("w_pb", 4), ("w_pa", 4), ("w_o", 8)], "far")
        parted([("w_pq", 16), ("u", 128)], "four")
        plan("v", 2, "near")
        plan("v", 126, "four")
        plan("w2_xk", 2, "four")
        plan("w2_xv", 1, "four")
        plan("w2_xv", 1, "far2")
        parted([("w2_mq", 4), ("w2_mk", 4), ("w2_mv", 4), ("w2_gk", 2), ("w2_gv", 2), ("w2_go", 2), ("w2_cc", 2), ("w2_ch", 2),
                ("w2_cb", 2), ("w2_o", 8), ("w2_xq", 2), ("w2_xo", 2)], "far2")
        plan("w_up", 44, "far2")
        plan("w_dn", 22, "far2")

        ph = ExitStack()
        far = sb("far", [128, 6, UNIT], where=ph)
        add_slots("far", [far[:, i, :] for i in range(6)])
        sets["far"] = sets["four"] + sets["far"]
        PA = sb("PA", [128, 20672], where=ph)
        Yb = sb("Yb", [128, 2, 4, T], F32R, where=ph)
        Ya = sb("Ya", [128, 2, 4, T], F32R, where=ph)
        off = [0]
        base = [PA]

        def scr(n):
            a = off[0]
            off[0] += n
            assert off[0] <= base[0].shape[1], off[0]
            return base[0][:, a:a + n]

        qiT, kiT = tri3(scr(1024), 4), scr(256)
        qaT, kaT, va = scr(1024), scr(1024), scr(1024)
        qbT, kbT, vb = scr(1024), scr(1024), scr(1024)
        sg = tri3(scr(4096), 16)
        bm = tri3(scr(3072), 8)
        madd = scr(384)
        relb = scr(2048)
        sc_a = scr(3072)
        wk = scr(256)
        wiw = scr(64)

        sums = sumsq()
        for j in range(8):
            sums["add"](xT[:, j, :], l_x)
        m_mod1 = ada(0, 16)
        m = dve(lambda: V.tensor_scalar(sm[:, 32:40], mod[:, 8:16], 1.0, None, ALU.add), m_mod1)
        m_A1 = dve(lambda: V.tensor_tensor(sm[:, 24:32], sm[:, 32:40], vec("norm1_g", 0, 8), ALU.mult), m)
        h1 = norm(xT, sums, lambda j: sm[:, 24 + j:25 + j], [m_A1], shift=lambda j: mod[:, j:j + 1], dst=H)
        mh = lambda k: h1[k]

        l_wi = q.load("scalar", wiw, A["w_wi"])
        ohs = sc_a[0:32, :]
        l_oh = q.load("scalar", ohs[:, 0:384], A["oh"])
        l_rb = q.load("scalar", ohs[:, 384:392], A["rel_bias"])
        reps, stores, l_bm = [], [], []
        rbs = flat(sg)

        def bias_job():
            for h in range(8):
                o = 512 + 128 * h
                reps.append(dve(lambda h=h, o=o: V.tensor_copy(ohs[:, o:o + 128], ohs[:, 384 + h:385 + h].broadcast_to((32, 128))),
                                l_rb))
            for h in range(8):
                o = 512 + 128 * h
                b = take()
                rb = rbs[:, 384 * h:384 * h + 384]
                m = mm(banks[b][:, 0:384], ohs[:, o:o + 128], ohs[:, 0:384], True, True, reps[h], l_oh, bank_free[b], inc=True)
                w = dve(lambda b=b, rb=rb: V.tensor_copy(rb, banks[b][:, 0:384]), m)
                free(b, w)
                stores.append(q.load("gpsimd", scratch[h], rb, w))
                yield
            for h in range(8):
                fl = scratch[h].rearrange("p n -> (p n)")
                src = fl[127:127 + 128 * 383].rearrange("(p n) -> p n", n=383)
                l_bm.append(q.load("gpsimd", bm[:, h, 128:384], src[:, 0:256], stores[h]))

        spawn(bias_job())

        qi_m = []
        lin("w_qi", 4, hk, mh, copy_to(flat(qiT), qi_m))
        w, lw, done = unit("w_ki")
        b = take()
        for k in range(8):
            last = mm3(banks[b][:, 0:T], (w[0][:, k * 128:(k + 1) * 128], w[1][:, k * 128:(k + 1) * 128]), hk(k),
                       k == 0, k == 7, lw, bank_free[b], inc=(k == 7))
        done(last)
        m_ki = act(lambda b=b: S.copy(kiT, banks[b][:, 0:T]), last)
        free(b, m_ki)
        b = take()
        for t in range(2):
            for k in range(8):
                for s2 in range(2):
                    last = mm(banks[b][:, 8 * t:8 * t + 8], hkt(k, t)[s2].bitcast(F32), wiw[:, 8 * k:8 * k + 8],
                              k == 0 and s2 == 0, k == 7 and s2 == 1, l_wi, bank_free[b], inc=(k == 7 and s2 == 1))
        m_wi = dve(lambda b=b: V.tensor_scalar(sm[:, 48:64], banks[b][:, 0:16], (64 ** -0.5) * (8 ** -0.5), None, ALU.mult), last)
        free(b, m_wi)

        m_bm = []

        def index_job():
            m_rel_free = None
            for t in range(2):
                W = 128 * (t + 1)
                rel = relb.rearrange("p (a b) -> p a b", a=8)[:, :, 0:W]
                for par in range(2):
                    for g in range(2):
                        while not room(1):
                            yield
                        b = take()
                        hs = [par + 4 * g, par + 4 * g + 2]
                        rows = slice(64 * par, 64 * par + 64)
                        for i, h in enumerate(hs):
                            last = mm(banks[b][:, i * 256:i * 256 + W], qiT[rows, h // 2, t * 128:(t + 1) * 128],
                                      kiT[rows, 0:W], True, True, qi_m[-1], m_ki, bank_free[b], inc=(i == 1))
                        mr = act(lambda b=b, h=hs[0], rel=rel, W=W: S.activation(
                            rel[:, h:h + 3:2, :], tri3(banks[b][:, :], 2)[:, :, 0:W], ACT.Relu), last, m_rel_free)
                        free(b, mr)
                yield
                acc = wk[:, 0:W]
                m = dve(lambda rel=rel, acc=acc, t=t: V.tensor_scalar(acc, rel[:, 0, :], sm[:, 48 + 8 * t:49 + 8 * t], None, ALU.mult),
                        mr, m_wi)
                for h in range(1, 8):
                    m = dve(lambda rel=rel, acc=acc, t=t, h=h: V.scalar_tensor_tensor(
                        out=acc, in0=rel[:, h, :], scalar=sm[:, 48 + 8 * t + h:49 + 8 * t + h], in1=acc,
                        op0=ALU.mult, op1=ALU.add), m)
                m_rel_free = m
                m = pool(lambda acc=acc, W=W, t=t: G.affine_select(out=acc, in_=acc, compare_op=ALU.is_ge, fill=LOW, base=128 * t,
                                                                  pattern=[[-1, W]], channel_multiplier=1), m)
                yield
                for r in range(8):
                    m = dve(lambda acc=acc: V.max(sm[:, 64:72], acc), m)
                    m = dve(lambda acc=acc: V.match_replace(acc, sm[:, 64:72], acc, GONE), m)
                    if r % 2:
                        yield
                a, e = (0, 128) if t == 0 else (128, 384)
                md = madd[:, a:e]
                m = dve(lambda acc=acc, md=md: V.tensor_scalar(md, acc, -3.2e38, NEG, ALU.is_gt, ALU.mult), m)
                m_madd = pool(lambda md=md, W=W, t=t: G.affine_select(out=md, in_=md, compare_op=ALU.is_ge, fill=NEG, base=128 * t,
                                                                     pattern=[[-1, W]], channel_multiplier=1), m)
            m0 = pool(lambda: G.tensor_tensor(bm[:, :, 0:128], bm[:, :, 256:384],
                                              madd[:, 0:128].rearrange("p (a b) -> p a b", a=1).broadcast_to((128, 8, 128)), ALU.add),
                      m_madd, *l_bm)
            m_bm.append(pool(lambda: G.tensor_tensor(bm[:, :, 128:384], bm[:, :, 128:384],
                                                     madd[:, 128:384].rearrange("p (a b) -> p a b", a=1).broadcast_to((128, 8, 256)),
                                                     ALU.add), m0))

        spawn(index_job())

        qa_m, ka_m, va_m, qb_m, kb_m, vb_m = [], [], [], [], [], []
        lin("w_qb", 4, hk, mh, copy_to(qbT, qb_m))
        lin("w_kb", 4, hk, mh, copy_to(kbT, kb_m))
        lin_nat("w_vb", hkt, mh, 512, nat_to(vb, 512, vb_m))

        qb3, kb3, vb3 = tri3(qbT, 4), tri3(kbT, 4), tri3(vb, 2)
        yb_done = {}
        zbuf = sb("zbuf", [128, 2, 3, 384], where=ph)

        def stick(h, lane, yb):
            rows = slice(64 * (h % 2), 64 * (h % 2) + 64)
            z0, z1, z2 = (zbuf[:, lane, i, :] for i in range(3))
            while not room(2):
                yield
            b = take()
            mm(banks[b][:, 0:256], kb3[rows, h // 2, 0:128], qb3[rows, h // 2, :], True, True,
               qb_m[-1], kb_m[-1], bank_free[b])
            last = mm(banks[b][:, 256:384], kb3[rows, h // 2, 128:256], qb3[rows, h // 2, 128:256], True, True, inc=True)
            zp = banks[b][:, 0:384]
            fr = stick_free[lane]
            mab = m = act(lambda: S.activation(z0, zp, ACT.Abs, scale=0.125), last, fr)
            m = act(lambda: S.activation(z0, z0, ACT.Exp, scale=-1.0), m)
            m = act(lambda: S.activation(z0, z0, ACT.Ln, bias=1.0), m)
            n = dve(lambda: V.tensor_scalar(z1, zp, 0.125, 0.0, ALU.mult, ALU.min), mab, fr)
            n = dve(lambda: V.tensor_tensor(z1, z1, z0, ALU.subtract), n, m)
            m = dve(lambda: V.scalar_tensor_tensor(out=z2, in0=zp, scalar=-0.125, in1=z1, op0=ALU.mult, op1=ALU.add), n)
            free(b, m)
            m = pool(lambda: G.tensor_tensor(z2[:, 0:128], z2[:, 0:128], up_strict, ALU.mult), m, l_cst)
            m = pool(lambda: G.tensor_tensor(z2[:, 256:384], z2[:, 256:384], up_strict, ALU.mult), m)
            yield
            while not room(1):
                yield
            b = take()
            mm(banks[b][:, 0:256], tri_gt, z2[:, 0:256], True, False, m, bank_free[b])
            mm(banks[b][:, 128:256], ones, z2[:, 256:384], False, True)
            last = mm(banks[b][:, 256:384], tri_gt, z2[:, 256:384], False, True, inc=True)
            m = dve(lambda b=b: V.tensor_tensor(z1, z1, banks[b][:, 0:384], ALU.add), last)
            free(b, m)
            m = act(lambda: S.activation(z1, z1, ACT.Exp), m)
            m = pool(lambda: G.tensor_tensor(z1[:, 0:128], z1[:, 0:128], up_strict, ALU.mult), m)
            m = pool(lambda: G.tensor_tensor(z1[:, 256:384], z1[:, 256:384], up_strict, ALU.mult), m)
            yield
            if yb[0] is None:
                yb[0] = take()
                yb[1] = bank_free[yb[0]]
            o = banks[yb[0]][64 * (h % 2):64 * (h % 2) + 64, :]
            mm(o[:, 0:256], vb3[:, 0, 64 * h:64 * h + 64], z1[:, 0:256], True, False, m, vb_m[-1], yb[1])
            last = mm(o[:, 128:256], vb3[:, 1, 64 * h:64 * h + 64], z1[:, 256:384], False, True, inc=True)
            stick_free[lane] = last
            yb[2] += 1
            if yb[2] == 2:
                m = cut(Yb[:, 0, h // 2, :], Yb[:, 1, h // 2, :], banks[yb[0]][:, 0:256], last)
                free(yb[0], m)
                yb_done[h // 2] = m

        stick_free = [None, None]

        def stick_job():
            for p in range(4):
                yb = [None, None, 0]
                a, c = stick(2 * p, 0, yb), stick(2 * p + 1, 1, yb)
                live = [a]
                while live:
                    for g in list(live):
                        if next(g, "end") == "end":
                            live.remove(g)
                    yield
                    if c:
                        live.append(c)
                        c = None

        spawn(stick_job())

        lin("w_qa", 4, hk, mh, copy_to(qaT, qa_m))
        lin("w_ka", 4, hk, mh, copy_to(kaT, ka_m))
        lin_nat("w_va", hkt, mh, 512, nat_to(va, 512, va_m))

        def bm_a(h, t, W):
            a = 0 if t == 0 else 128
            return bm[:, h:h + 3:2, a:a + W]

        ya_done = {}

        def attend_a():
            while not m_bm:
                yield
            yield from attend(8, tri3(qaT, 4), tri3(kaT, 4), tri3(va, 2), Ya, 0, lambda: [qa_m[-1], ka_m[-1], va_m[-1]],
                              bm_a, lambda: m_bm, lambda t: t + 1, sm[:, 80:104], 0.125, sc_a, m_bm[-1], ya_done)

        spawn(attend_a())

        sg_m = []

        def gate(c, b, m):
            d = flat(sg[:, 2 * c:2 * c + 2, :])
            sg_m.append(act(lambda: S.activation(d, banks[b][:, :], ACT.Sigmoid), m, *stores))
            free(b, sg_m[-1])

        lin("w_g", 16, hk, mh, gate)
        m_mod2 = ada(16, 48)
        drain()

        M = H
        m_mg = [None] * 8

        def merge_b(c, b, m):
            g = flat(sg[:, 8 + 2 * c:8 + 2 * c + 2, :])
            n = dve(lambda: V.tensor_tensor(g, banks[b][:, :], g, ALU.mult), m, sg_m[-1])
            free(b, n)

        def merge_a(c, b, m):
            g = flat(sg[:, 2 * c:2 * c + 2, :])
            gb = flat(sg[:, 8 + 2 * c:8 + 2 * c + 2, :])
            n = dve(lambda: V.tensor_tensor(g, banks[b][:, :], g, ALU.mult), m)
            free(b, n)
            n = dve(lambda: V.tensor_tensor(g, g, gb, ALU.add), n)
            n = cut(flat(M[:, 0, 2 * c:2 * c + 2, :]), flat(M[:, 1, 2 * c:2 * c + 2, :]), g, n)
            m_mg[2 * c] = m_mg[2 * c + 1] = n

        lin("w_pb", 8, of(Yb), lambda k: yb_done[k], merge_b, kt=4)
        lin("w_pa", 8, of(Ya), lambda k: ya_done[k], merge_a, kt=4)

        m_x = []

        def resid(col, sums):
            def evac(c, b, m):
                for j in range(2):
                    i = 2 * c + j
                    if col is None:
                        n = dve(lambda i=i, j=j: V.tensor_tensor(xT[:, i, :], banks[b][:, j * T:(j + 1) * T], xT[:, i, :], ALU.add), m)
                    else:
                        n = dve(lambda i=i, j=j: V.scalar_tensor_tensor(out=xT[:, i, :], in0=banks[b][:, j * T:(j + 1) * T],
                                                                        scalar=mod[:, col + i:col + i + 1], in1=xT[:, i, :],
                                                                        op0=ALU.mult, op1=ALU.add), m)
                    marks[i] = n
                free(b, n)
                m_x.append(n)

                def later():
                    yield
                    for i in (2 * c, 2 * c + 1):
                        sums["add"](xT[:, i, :], marks[i])
                spawn(later())
            marks = {}
            return evac

        sums = sumsq()
        lin("w_o", 8, of(M), lambda k: m_mg[k], resid(16, sums))
        drain()
        ph.close()

        ph = ExitStack()
        PR = sb("PR", [128, 128 * 256], where=ph)
        m = dve(lambda: V.tensor_scalar(sm[:, 32:40], mod[:, 32:40], 1.0, None, ALU.add), m_mod2)
        m_A2 = dve(lambda: V.tensor_tensor(sm[:, 24:32], sm[:, 32:40], vec("norm2_g", 0, 8), ALU.mult), m)
        h2 = norm(xT, sums, lambda j: sm[:, 24 + j:25 + j], [m_A2], shift=lambda j: mod[:, 24 + j:25 + j], dst=H)
        mh2 = lambda k: h2[k]

        o96 = 96 * 256
        SC = PR[:, o96:o96 + 4096].rearrange("p (t c n) -> p t c n", t=2, c=16)
        o = o96 + 4096
        cand = PR[:, o:o + 256]
        tv = PR[:, o + 512:o + 1024].rearrange("p (t c k) -> p t c k", t=2, c=16)
        ti = PR[:, o + 1024:o + 1536].rearrange("p (t c k) -> p t c k", t=2, c=16)
        tf = PR[:, o + 1536:o + 2048].rearrange("p (t c k) -> p t c k", t=2, c=16)
        eq = PR[:, o + 2048:o + 4096]
        qh = [PR[:, 22528 + i * 512:22528 + (i + 1) * 512] for i in range(3)]
        cv2 = PR[:, o + 256:o + 512].rearrange("p (t n) -> p t n", t=2)
        cp2 = sb("cp", [128, 2, 128], U32, where=ph)
        cpa = sb("cpa", [128, 128], U32, where=ph)
        cpf = sb("cpf", [128, 2, 128], where=ph)
        rt = sb("rt", [128, 3, 256], where=ph)
        skt = PR[:, 80 * 256:80 * 256 + 2048]
        l_sk = q.load("scalar", skt, A["sub_keys"], m_x[-1])
        qh_free = [None] * 3
        m_s = {}

        def peer_q(c, b, m):
            z = qh[c % 3]
            e = act(lambda: S.copy(z, banks[b][:, :]), m, qh_free[c % 3])
            free(b, e)

            def later():
                yield
                b = take()
                for t in range(2):
                    for j in range(2):
                        last = mm(banks[b][:, (2 * t + j) * 128:(2 * t + j + 1) * 128],
                                  z[:, j * T + t * 128:j * T + (t + 1) * 128],
                                  skt[:, (2 * c + j) * 128:(2 * c + j + 1) * 128], True, True, e, l_sk, bank_free[b], inc=True)
                qh_free[c % 3] = last
                x = act(lambda: S.copy(SC[:, :, 2 * c:2 * c + 2, :], banks[b][:, :].rearrange("p (t j n) -> p t j n", t=2, j=2)), last)
                free(b, x)
                m_s[c] = x
            spawn(later())

        lin("w_pq", 16, hk, mh2, peer_q)
        drain()
        rt_m = []

        def route_job():
            for t in range(2):
                ti_u = ti[:, t, :, :].bitcast(U32)
                for c in range(16):
                    s_ = SC[:, t, c, :]
                    m = dve(lambda s_=s_, t=t, c=c: V.max(tv[:, t, c, 0:8], s_), m_s[c // 2])
                    dve(lambda s_=s_, ti_u=ti_u, t=t, c=c: V.max_index(ti_u[:, c, 0:8], tv[:, t, c, 0:8], s_), m)
                    m = dve(lambda s_=s_, t=t, c=c: V.match_replace(s_, tv[:, t, c, 0:8], s_, GONE), m)
                    m = dve(lambda s_=s_, t=t, c=c: V.max(tv[:, t, c, 8:16], s_), m)
                    m = dve(lambda s_=s_, ti_u=ti_u, t=t, c=c: V.max_index(ti_u[:, c, 8:16], tv[:, t, c, 8:16], s_), m)
                    yield
                prev = dve(lambda ti_u=ti_u, t=t: V.tensor_copy(tf[:, t, :, :], ti_u), m)
                cv, cp = cv2[:, t, :], cp2[:, t, :]
                for h in range(8):
                    a0 = tv[:, t, 2 * h, :].rearrange("p (k o) -> p k o", o=1).broadcast_to((128, 16, 16))
                    a1 = tv[:, t, 2 * h + 1, :].rearrange("p (o k) -> p o k", o=1).broadcast_to((128, 16, 16))
                    cs = slice(16 * h, 16 * h + 8)
                    ct = slice(16 * h + 8, 16 * h + 16)
                    m = dve(lambda a0=a0, a1=a1: V.tensor_tensor(cand.rearrange("p (a b) -> p a b", a=16), a0, a1, ALU.add), prev)
                    m = dve(lambda cs=cs, cv=cv: V.max(cv[:, cs], cand), m)
                    dve(lambda cs=cs, cv=cv, cp=cp: V.max_index(cp[:, cs], cv[:, cs], cand), m)
                    m = dve(lambda cs=cs, cv=cv: V.match_replace(cand, cv[:, cs], cand, GONE), m)
                    m = dve(lambda ct=ct, cv=cv: V.max(cv[:, ct], cand), m)
                    prev = dve(lambda ct=ct, cv=cv, cp=cp: V.max_index(cp[:, ct], cv[:, ct], cand), m)
                    yield
                cv3 = cv.rearrange("p (h k) -> p h k", h=8)
                g3 = eq[:, 0:128].rearrange("p (h k) -> p h k", h=8)
                m = dve(lambda cv3=cv3, g3=g3: V.tensor_tensor(g3, cv3, cv3[:, :, 0:1].broadcast_to((128, 8, 16)), ALU.subtract), prev)
                m = act(lambda: S.activation(eq[:, 0:128], eq[:, 0:128], ACT.Exp), m)
                yield
                m = dve(lambda g3=g3: V.tensor_reduce(sm[:, 104:112], g3, AX, ALU.add), m)
                m = dve(lambda: V.reciprocal(sm[:, 112:120], sm[:, 104:112]), m)
                mg_ = dve(lambda g3=g3, cv3=cv3: V.tensor_tensor(
                    cv3, g3, sm[:, 112:120].rearrange("p (h o) -> p h o", o=1).broadcast_to((128, 8, 16)), ALU.mult), m)
                m = dve(lambda cp=cp: V.tensor_scalar(cpa[:, :], cp, 4, None, ALU.logical_shift_right), mg_)
                m = dve(lambda: V.tensor_copy(cpf[:, 0, :], cpa[:, :]), m)
                m = dve(lambda cp=cp: V.tensor_scalar(cpa[:, :], cp, 15, None, ALU.bitwise_and), m)
                m = dve(lambda: V.tensor_copy(cpf[:, 1, :], cpa[:, :]), m)
                yield
                e4 = eq.rearrange("p (h k i) -> p h k i", h=8, k=16)
                e3 = eq.rearrange("p (a i) -> p a i", i=16)
                io = iota[:, 0:16].rearrange("p (o i) -> p o i", o=1).broadcast_to((128, 128, 16))
                for s2 in range(2):
                    ps_ = cpf[:, s2, :].rearrange("p (a o) -> p a o", o=1).broadcast_to((128, 128, 16))
                    m = dve(lambda ps_=ps_: V.tensor_tensor(e3, io, ps_, ALU.is_equal), m)
                    yield
                    for h in range(8):
                        tk = tf[:, t, 2 * h + s2, :].rearrange("p (o i) -> p o i", o=1).broadcast_to((128, 16, 16))
                        mx = dve(lambda h=h, tk=tk: V.tensor_tensor(e4[:, h, :, :], e4[:, h, :, :], tk, ALU.mult), m)
                        if h % 4 == 3:
                            yield
                    m = dve(lambda s2=s2: V.tensor_reduce(cpf[:, s2, :], e3, AX, ALU.add), mx)
                    yield
                yield
                b = take()
                pe(lambda b=b, cv=cv: TE.transpose(banks[b][:, 256:384], cv, ident), m, bank_free[b])
                for s2 in range(2):
                    last = pe(lambda s2=s2, b=b: TE.transpose(banks[b][:, s2 * 128:(s2 + 1) * 128], cpf[:, s2, :], ident), m)
                m = dve(lambda b=b, t=t: V.tensor_copy(rt[:, :, t * 128:(t + 1) * 128],
                                                       banks[b][:, 0:384].rearrange("p (a b) -> p a b", a=3)), last)
                free(b, m)
                rt_m.append(m)

        spawn(route_job())

        P3 = PR[:, :].rearrange("p (i t) -> p i t", t=T)
        gelu = {}

        def pre(c, b, m):
            if c >= 48:
                assert len(rt_m) == 2
            gelu["m"] = act(lambda: S.activation(flat(P3[:, 2 * c:2 * c + 2, :]), banks[b][:, :], ACT.Gelu),
                            m, rt_m[-1] if c >= 48 else None)
            free(b, gelu["m"])

        lin("u", 128, hk, mh2, pre)
        drain()

        tb = [AB[:, 0:1024], AB[:, 1024:2048]]
        ab_free = [m for s in sets["ab"] for m in slot_free[s]]
        tb_free = [None, None]
        made = {}

        def tables(g):
            z = tb[g % 2]
            for i in range(4):
                t = 4 * g + i
                dve(lambda z=z, i=i, t=t: V.tensor_scalar(z[:, i * 128:(i + 1) * 128], iota, rt[:, 0, t:t + 1],
                                                          rt[:, 2, t:t + 1], ALU.is_equal, ALU.mult),
                    tb_free[g % 2], *rt_m, *ab_free, apart=True)
                made[g, i] = dve(lambda z=z, i=i, t=t: V.tensor_scalar(z[:, 512 + i * 128:512 + (i + 1) * 128], iota,
                                                                       rt[:, 1, t:t + 1], None, ALU.is_equal),
                                 tb_free[g % 2], apart=True)

        tables(0)
        for g in range(64):
            z = tb[g % 2]
            b = take()
            for i in range(4):
                last = mm(banks[b][:, i * 128:(i + 1) * 128], z[:, 512 + i * 128:512 + (i + 1) * 128],
                          z[:, i * 128:(i + 1) * 128], True, True, made[g, i], bank_free[b], inc=True)
            tb_free[g % 2] = last
            if g < 63:
                tables(g + 1)
            d = P3[:, :, 4 * g:4 * g + 4].rearrange("p i t -> p t i")
            m_G = dve(lambda d=d, b=b: V.tensor_tensor(d, banks[b][:, :].rearrange("p (t i) -> p t i", t=4), d, ALU.mult),
                      last, gelu["m"], apart=True)
            free(b, m_G)
        for s in sets["ab"]:
            slot_free[s] = (last,)

        Hf = H[:, :, :, :].rearrange("p a b c -> p (a b c)")
        cf = [(Hf[:, i * 512:i * 512 + 256], Hf[:, i * 512 + 256:i * 512 + 512]) for i in range(8)]
        cf_free = [None] * 8
        cfm = {}

        def coef(i):
            hi, lo = cf[i % 8]
            m = act(lambda: S.copy(hi, P3[:, i, :]), m_G, cf_free[i % 8], apart=True)
            cfm[i] = dve(lambda: V.tensor_tensor(lo, P3[:, i, :], hi.bitcast(F32), ALU.subtract), m, apart=True)

        fb = [take() for _ in range(4)]
        for i in range(4):
            coef(i)
        for i in range(128):
            w, lw, done = unit("v")
            if i + 4 < 128:
                coef(i + 4)
            hi, lo = cf[i % 8]
            for t in range(2):
                for d in range(2):
                    ts_, ds_ = slice(t * 128, (t + 1) * 128), slice(d * 512, (d + 1) * 512)
                    last = mm3(banks[fb[2 * t + d]][:, :], (hi[:, ts_], lo[:, ts_]), (w[0][:, ds_], w[1][:, ds_]),
                               i == 0, i == 127, lw, cfm[i], bank_free[fb[2 * t + d]], inc=(t == 1 and d == 1))
            cf_free[i % 8] = last
            done(last)
        m_pv = last
        ph.close()

        ph = ExitStack()
        far2 = sb("far2", [128, 6, UNIT], where=ph)
        add_slots("far2", [far2[:, i, :] for i in range(6)])
        for s in sets["far2"]:
            slot_free[s] = (m_pv,)
        sets["far2"] = sets["far2"] + sets["four"]
        ph2 = ExitStack()
        PB = sb("PB", [128, 20480], where=ph2)
        Ym = sb("Ym", [128, 2, 8, T], F32R, where=ph2)
        off[0] = 0
        base[0] = PB
        fn = scr(2048)
        m_f = []
        for i in range(4):
            if i % 2:
                m = act(lambda i=i: S.copy(fn[:, i * 512:(i + 1) * 512], banks[fb[i]][:, :]), m_pv)
            else:
                m = dve(lambda i=i: V.tensor_copy(fn[:, i * 512:(i + 1) * 512], banks[fb[i]][:, :]), m_pv)
            free(fb[i], m)
            m_f.append(m)
        m_x.clear()
        sums = sumsq()
        ev = resid(40, sums)
        for d in range(4):
            b = take()
            for j in range(2):
                for t in range(2):
                    c = 2 * d + j
                    src = fn[:, t * 1024 + c * 128:t * 1024 + (c + 1) * 128]
                    last = pe(lambda b=b, j=j, t=t, src=src: TE.transpose(
                        banks[b][:, j * T + t * 128:j * T + (t + 1) * 128], src, ident), *m_f, bank_free[b])
            ev(d, b, last)
        memT = tri3(scr(2048), 8)
        bmm = tri3(scr(3072), 8)
        l_mem = q.load("scalar", memT, A["memT"], m_pv)
        l_bmm = q.load("scalar", bmm, A["bmm"], m_pv)
        mqT, mkT, mv = scr(1024), scr(1024), scr(1024)
        ccT = scr(512)
        uT = scr(2 * 258)
        ctmp = scr(512)
        gqk = scr(512)
        goT = scr(512)
        gv = scr(512)
        lrT = scr(256)
        xkT, xv = scr(512), scr(512)
        sc_b = scr(3072)
        gt = scr(2560)
        lrw = scr(128)

        drain()
        mem_s = sumsq()
        for j in range(8):
            mem_s["add"](memT[:, j, :], l_mem)
        hm = norm(memT, mem_s, lambda j: vec("norm_mem_g", j), dst=Ym)
        x3 = norm(xT, sums, lambda j: vec("final_g", j), keep=xT)
        x_m = []
        lin("w2_xk", 2, of(Ym), lambda k: hm[k], copy_to(xkT, x_m))
        lin_nat("w2_xv", of_t(Ym), lambda k: hm[k], 256, nat_to(xv, 256, x_m))
        sums = sumsq()
        for j in range(8):
            sums["add"](xT[:, j, :], x3[j])
        h3 = norm(xT, sums, lambda j: vec("norm_mix_g", j), dst=H)
        mh3 = lambda k: h3[k]
        l_lr = q.load("scalar", lrw, A["w2_lr"][0], m_pv)
        l_g = q.load("scalar", gt[0:16, 1280:1408], A["w_gate"], m_pv)
        l_gb = q.load("scalar", gt[0:1, 1408:1536], A["b_gate"], m_pv)
        l_gc = q.load("scalar", gt[:, 1536:1792], A["gcst"], m_pv)

        z_m = []
        lin("w2_mq", 4, hk, mh3, copy_to(mqT, z_m))
        lin("w2_mk", 4, hk, mh3, copy_to(mkT, z_m))
        lin_nat("w2_mv", hkt, mh3, 512, nat_to(mv, 512, z_m))
        m_mo = z_m[-1]

        def bm_m(h, t, W):
            a = 0 if t == 0 else 128
            return bmm[:, h:h + 3:2, a:a + W]

        mb_done = {}
        spawn(attend(8, tri3(mqT, 4), tri3(mkT, 4), tri3(mv, 2), Ym, 2, lambda: [m_mo],
                     bm_m, lambda: [l_bmm], lambda t: t + 1, sm[:, 80:104], 0.125, sc_b, m_mo, mb_done))

        g_m = []
        lin("w2_gk", 2, hk, mh3, copy_to(gqk, g_m))
        lin_nat("w2_gv", hkt, mh3, 256, nat_to(gv, 256, g_m))
        m_gv = g_m[-1]
        b = take()
        for k in range(8):
            for s2 in range(2):
                last = mm(banks[b][0:16, 0:T], lrw[:, k * 16:(k + 1) * 16], hk(k)[s2].bitcast(F32), k == 0 and s2 == 0,
                          k == 7 and s2 == 1, l_lr, bank_free[b], inc=(k == 7 and s2 == 1))
        m_lr = act(lambda b=b: S.copy(lrT[0:16, :], banks[b][0:16, 0:T]), last)
        free(b, m_lr)

        def go(c, b, m):
            n = act(lambda: S.activation(goT, banks[b][:, :], ACT.Silu), m)
            free(b, n)
            g_m.append(n)

        lin("w2_go", 2, hk, mh3, go)
        m_go = g_m[-1]
        gla_m = []
        sc_g = sb("sc_g", [128, 1792], where=ph2)

        def gla_job():
            tri64 = gt[:, 1536:1664]
            hmask = gt[:, 1664:1792]
            la = gt[:, 0:256]
            while not room(1):
                yield
            b = take()
            for t in range(2):
                o_ = banks[b][:, t * 128:(t + 1) * 128]
                mm(o_, lrT[0:16, t * 128:(t + 1) * 128], gt[0:16, 1280:1408], True, False, m_lr, l_g, bank_free[b])
                last = mm(o_, ones[0:1, :], gt[0:1, 1408:1536], False, True, l_gb, inc=True)
            zg = banks[b][:, 0:256]
            mab = m = act(lambda: S.activation(la, zg, ACT.Abs), last)
            m = act(lambda: S.activation(la, la, ACT.Exp, scale=-1.0), m)
            m = act(lambda: S.activation(la, la, ACT.Ln, bias=1.0), m)
            n = dve(lambda: V.tensor_scalar(gt[:, 256:512], zg, 0.0, None, ALU.min), mab)
            free(b, n)
            n = dve(lambda: V.tensor_tensor(la, gt[:, 256:512], la, ALU.subtract), n, m)
            n = dve(lambda: V.tensor_scalar(la, la, 1.0 / 16.0, None, ALU.mult), n)
            yield
            while not room(1):
                yield
            b = take()
            for t in range(2):
                last = mm(banks[b][:, t * 128:(t + 1) * 128], la[:, t * 128:(t + 1) * 128], tri64, True, True, n, l_gc,
                          bank_free[b], inc=True)
            bT = gt[:, 256:512]
            m = act(lambda b=b: S.copy(bT, banks[b][:, 0:256]), last)
            free(b, m)
            eb, en, kend = gt[:, 512:768], gt[:, 768:1024], gt[:, 1024:1280]
            m1 = act(lambda: S.activation(eb, bT, ACT.Exp), m)
            m2 = act(lambda: S.activation(en, bT, ACT.Exp, scale=-1.0), m)
            for c in range(4):
                act(lambda c=c: S.activation(kend[:, c * 64:(c + 1) * 64], bT[:, c * 64:(c + 1) * 64], ACT.Exp, scale=-1.0,
                                             bias=bT[:, c * 64 + 63:c * 64 + 64]), m)
            dec = sm[:, 120:124]
            m4 = act(lambda: S.activation(dec, bT[:, 63:256:64], ACT.Exp), m)
            yield
            gq, gk = gqk[:, 0:256], gqk[:, 256:512]
            dve(lambda: V.scalar_tensor_tensor(out=eb, in0=gq, scalar=32 ** -0.5, in1=eb, op0=ALU.mult, op1=ALU.mult), m1, g_m[0])
            dve(lambda: V.tensor_tensor(en, gk, en, ALU.mult), m2)
            m_qk = dve(lambda: V.tensor_tensor(kend, gk, kend, ALU.mult), m4)
            yield
            AT = sc_g[:, 0:1024].rearrange("p (h t c) -> p h t c", h=4, t=2)
            m_at = []
            for h in range(4):
                while not room(1):
                    yield
                b = take()
                for t in range(2):
                    last = mm(banks[b][:, t * 128:(t + 1) * 128], en[32 * h:32 * h + 32, t * 128:(t + 1) * 128],
                              eb[32 * h:32 * h + 32, t * 128:(t + 1) * 128], True, True, m_qk, bank_free[b], inc=True)
                m = act(lambda b=b, h=h: S.copy(AT[:, h, :, :], banks[b][:, 0:256].rearrange("p (t c) -> p t c", t=2)), last)
                free(b, m)
                m = pool(lambda h=h: G.affine_select(out=AT[:, h, :, :], in_=AT[:, h, :, :], compare_op=ALU.is_ge, fill=0.0,
                                                     base=0, pattern=[[0, 2], [1, 128]], channel_multiplier=-1), m)
                a4 = AT[:, h, :, 64:128]
                m = pool(lambda a4=a4: G.affine_select(out=a4, in_=a4, compare_op=ALU.is_ge, fill=0.0,
                                                       base=-64, pattern=[[0, 2], [0, 64]], channel_multiplier=1), m)
                m_at.append(m)
            while not room(1):
                yield
            b = take()
            for t in range(2):
                last = pe(lambda t=t, b=b: TE.transpose(banks[b][:, t * 128:(t + 1) * 128], kend[:, t * 128:(t + 1) * 128], ident),
                          m_qk, bank_free[b])
            keN = gt[:, 1792:2048]
            m_ke = act(lambda b=b: S.copy(keN, banks[b][:, 0:256]), last)
            free(b, m_ke)
            yield
            St = sc_g[:, 1024:1024 + 3 * 256].rearrange("p (c e) -> p c e", c=3)
            m_S = []
            hm2 = hmask.rearrange("p (h o) -> p h o", o=1)[:, 0:4, :].broadcast_to((128, 4, 64))
            for c in range(3):
                r = slice(64 * (c % 2), 64 * (c % 2) + 64)
                while not room(1):
                    yield
                b = take()
                last = mm(banks[b][:, 0:256], keN[r, (c // 2) * 128:(c // 2) * 128 + 128], gv[r, (c // 2) * 256:(c // 2) * 256 + 256],
                          True, True, m_ke, m_gv, bank_free[b], inc=True)
                m = dve(lambda b=b, c=c: V.tensor_tensor(St[:, c, :].rearrange("p (h e) -> p h e", h=4),
                                                         banks[b][:, 0:256].rearrange("p (h e) -> p h e", h=4), hm2, ALU.mult), last)
                free(b, m)
                if c:
                    m = dve(lambda c=c: V.scalar_tensor_tensor(out=St[:, c, :], in0=St[:, c - 1, :], scalar=dec[:, c:c + 1],
                                                               in1=St[:, c, :], op0=ALU.mult, op1=ALU.add), m)
                m_S.append(m)
            yield
            oT = gt[:, 2048:2560].rearrange("p (a b) -> p a b", a=2)
            for pr in range(2):
                while not room(1):
                    yield
                b = take()
                for t in range(2):
                    for j in range(2):
                        h = 2 * pr + j
                        mm(banks[b][64 * j:64 * j + 64, t * 128:(t + 1) * 128], gv[:, t * 256 + 64 * h:t * 256 + 64 * h + 64],
                           AT[:, h, t, :], t == 0, False, m_at[h], m_gv, bank_free[b])
                for c in range(1, 4):
                    last = mm(banks[b][:, c * 64:(c + 1) * 64], St[:, c - 1, pr * 128:(pr + 1) * 128],
                              eb[:, c * 64:(c + 1) * 64], False, True, m_S[c - 1], inc=True)
                m_o = act(lambda b=b, pr=pr: S.copy(oT[:, pr, :], banks[b][:, 0:256]), last)
                free(b, m_o)
            yield
            oF = gt[:, 2048:2560]
            sqg = gt[:, 0:512]
            m = act(lambda: S.activation(sqg, oF, ACT.Square), m_o)
            while not room(1):
                yield
            b = take()
            last = mm(banks[b][:, :], bd64, sqg, True, True, m, bank_free[b], inc=True)
            ms = sc_g[:, 1024:1536]
            rr = sc_g[:, 0:512]
            m = dve(lambda: V.tensor_scalar(ms, banks[b][:, :], 1.0 / 64, EPS, ALU.mult, ALU.add), last)
            free(b, m)
            m = act(lambda: S.activation(sqg, ms, ACT.Sqrt), m)
            yield
            m = dve(lambda: V.reciprocal(rr, sqg), m)
            m = newton(rr, ms, sqg, m)
            yield
            m = dve(lambda: V.scalar_tensor_tensor(out=oF, in0=oF, scalar=vec("gla_norm_g", 0), in1=rr, op0=ALU.mult, op1=ALU.mult), m)
            m = dve(lambda: V.tensor_tensor(oF, oF, goT, ALU.mult), m, m_go)
            gla_m.append(cut(flat(Ym[:, 0, 6:8, :]), flat(Ym[:, 1, 6:8, :]), oF, m))

        spawn(gla_job())

        lin("w2_cc", 2, hk, mh3, copy_to(ccT, z_m))
        m_cc = z_m[-1]
        uv = uT.rearrange("p (a b) -> p a b", a=2)
        m_z = pool(lambda: G.memset(uv[:, :, 0:2], 0.0), m_pv)
        m_u = []

        def ch(c, b, m):
            m_u.append(dve(lambda: V.tensor_tensor(uv[:, :, 2:258], tri3(banks[b][:, :], 2), tri3(ccT, 2), ALU.mult), m, m_cc))
            free(b, m_u[-1])

        lin("w2_ch", 2, hk, mh3, ch)

        def cb(c, b, m):
            for j in range(2):
                t_ = ctmp[:, j * 256:(j + 1) * 256]
                n = dve(lambda j=j, t_=t_: V.tensor_scalar(t_, uv[:, j, 2:258], vec("sc_w", 2 * 2 + j), vec("sc_b", j), ALU.mult, ALU.add),
                        m_u[-1], m_z)
                for tap in (1, 0):
                    n = dve(lambda j=j, t_=t_, tap=tap: V.scalar_tensor_tensor(
                        out=t_, in0=uv[:, j, tap:tap + 256], scalar=vec("sc_w", 2 * tap + j), in1=t_,
                        op0=ALU.mult, op1=ALU.add), n)
            n = dve(lambda: V.tensor_tensor(ctmp, banks[b][:, :], ctmp, ALU.mult), n, m)
            free(b, n)
            m_u.append(cut(flat(Ym[:, 0, 0:2, :]), flat(Ym[:, 1, 0:2, :]), ctmp, n))

        lin("w2_cb", 2, hk, mh3, cb)
        m_conv = m_u[-1]
        drain()

        def m_cat(k):
            return m_conv if k < 2 else gla_m[0] if k >= 6 else mb_done[k - 2]

        m_x.clear()
        sums = sumsq()
        lin("w2_o", 8, of(Ym), m_cat, resid(None, sums))
        drain()
        h4 = norm(xT, sums, lambda j: vec("norm_xattn_g", j), dst=H)
        xqT = ctmp
        x_q = []
        lin("w2_xq", 2, hk, lambda k: h4[k], copy_to(xqT, x_q))
        xo_done = {}
        spawn(attend(4, tri3(xqT, 2), tri3(xkT, 2), tri3(xv, 2), Ym, 0, lambda: [x_q[-1], x_m[-1]],
                     None, lambda: [], lambda t: 2, sm[:, 80:104], 0.125, sc_b, m_x[-1], xo_done))
        drain()
        m_x.clear()
        sums = sumsq()
        lin("w2_xo", 8, of(Ym), lambda k: xo_done[k], resid(None, sums), kt=2)
        drain()
        ph2.close()
        act_t = sb("act_t", [128, 2, 22, T], F32R, where=ph)
        tmp = sb("ftmp", [128, 3, 768], where=ph)
        h5 = norm(xT, sums, lambda j: vec("norm_ffn_g", j), dst=H)
        m_act = []

        def ffn(c, b, m):
            a, g, e = (tmp[:, c % 3, i * 256:(i + 1) * 256] for i in range(3))
            fr = m_act[c - 3] if c >= 3 else m_x[-1]
            bank = banks[b]
            for j, d in ((0, a), (1, g)):
                i = 2 * c + j
                z = bank[:, j * T:(j + 1) * T]
                mk = act(lambda d=d, z=z, i=i: S.activation(d, z, ACT.Identity, bias=vec("f_b", i), scale=vec("f_w", 2 * 44 + i)), m, fr)
            for j, d in ((0, a), (1, g)):
                i = 2 * c + j
                z = bank[:, j * T:(j + 1) * T]
                n = dve(lambda d=d, z=z, i=i: V.scalar_tensor_tensor(out=d[:, 1:256], in0=z[:, 0:255], scalar=vec("f_w", 44 + i),
                                                                     in1=d[:, 1:256], op0=ALU.mult, op1=ALU.add), mk)
                n = dve(lambda d=d, z=z, i=i: V.scalar_tensor_tensor(out=d[:, 2:256], in0=z[:, 0:254], scalar=vec("f_w", i),
                                                                     in1=d[:, 2:256], op0=ALU.mult, op1=ALU.add), n)
                if j == 0:
                    ea = act(lambda: S.activation(e, a, ACT.Silu), n)
            free(b, n)
            n = dve(lambda: V.tensor_tensor(e, e, g, ALU.mult), n, ea)
            m_act.append(cut(act_t[:, 0, c, :], act_t[:, 1, c, :], e, n))

        lin("w_up", 44, hk, lambda k: h5[k], ffn)
        m_x.clear()
        sums = sumsq()
        lin("w_dn", 8, of(act_t), lambda k: m_act[k], resid(None, sums), kt=22)
        drain()
        h6 = norm(xT, sums, lambda j: vec("final_norm_g", j), keep=xT)
        done_ = []
        for j in range(8):
            done_.append(q.load("sync", out[:, j, :], xT[:, j, :], h6[j]))
        assert taken[0] == len(queue) == len(ready)

        block = ctx.enter_context(nc.Block())

        @block.sync
        def _(e):
            q.emit("sync", e)
            for _, s_, v_ in done_:
                e.wait_ge(s_, v_)

        @block.tensor
        def _(e):
            q.emit("tensor", e)

        @block.vector
        def _(e):
            q.emit("vector", e)

        @block.scalar
        def _(e):
            q.emit("scalar", e)

        @block.gpsimd
        def _(e):
            q.emit("gpsimd", e)
        ph.close()


def bucket(n):
    me = 16
    nf = np.maximum(n, 1).astype(np.float32)
    large = me + (np.log(nf / np.float32(me)) / np.float32(math.log(128 / me)) * np.float32(16)).astype(np.int32)
    return np.where(n < me, n, np.minimum(large, 31))


def constants():
    p = np.arange(128)
    f = np.float32
    cst = np.concatenate([
        np.eye(128), np.ones((128, 128)), (p[:, None] > p[None, :]), (p[None, :] > p[:, None]),
        (p[:, None] // 64 == p[None, :] // 64), np.broadcast_to(p[None, :], (128, 128))], 1).astype(f)
    oh = np.zeros((32, 384), f)
    for col in range(384):
        n = 255 - col
        if n >= 0:
            oh[bucket(np.array(n)), col] = 1.0
    same = (p[:, None] // 64 == p[None, :] // 64) & (p[:, None] <= p[None, :])
    hm = np.zeros((128, 128), f)
    for h in range(4):
        hm[32 * h:32 * h + 32, h] = 1.0
    gc = np.concatenate([same.astype(f), hm], 1)
    bmm = np.full((128, 8, 384), NEG, f)
    for h in range(8):
        slope = f(2.0 ** -(h + 1))
        for t in range(2):
            q_, k_ = 128 * t + p[:, None], np.arange(128 * (t + 1))[None, :]
            v = np.where(q_ >= k_, -(slope * (q_ - k_).astype(f)), NEG)
            bmm[:, h, (0 if t == 0 else 128):(128 if t == 0 else 384)] = v
    return cst, oh, gc, bmm


def tiles(w, kt, per):
    K, N = w.shape
    a = w.reshape(kt, 128, N // 128, 128).transpose(2, 1, 0, 3).reshape(N // 128 // per, per, 128, kt * 128)
    return np.ascontiguousarray(a.transpose(0, 2, 1, 3).reshape(N // 128 // per, 128, per * kt * 128))


def rows(w, width):
    kk = NC // width
    a = w.reshape(8 // kk, kk, 128, width).transpose(0, 2, 1, 3)
    return np.ascontiguousarray(a.reshape(8 // kk, 128, NC))


def cols(v):
    v = v.reshape(-1)
    return v.reshape(-1, 128).T


def lay_out(i):
    f = {k: np.asarray(v) for k, v in i.items()}
    A = {}
    w = f["w_in"][0]
    o = np.cumsum([0, 512, 512, 512, 512, 64, 8, 512, 512, 512, 1024, 1024])
    part = [w[:, o[n]:o[n + 1]] for n in range(11)]
    A["w_ada"] = tiles(f["w_ada"][0], 8, 2)
    A["w_qa"], A["w_ka"], A["w_qi"] = tiles(part[0], 8, 2), tiles(part[1], 8, 2), tiles(part[3], 8, 2)
    A["w_ki"] = tiles(np.concatenate([part[4], part[4]], 1), 8, 1)
    A["w_wi"] = np.ascontiguousarray(part[5].reshape(8, 128, 8).transpose(1, 0, 2).reshape(128, 64))
    A["w_va"], A["w_vb"] = rows(part[2], 512), rows(part[8], 512)
    A["w_qb"], A["w_kb"] = tiles(part[6], 8, 2), tiles(part[7], 8, 2)
    A["w_g"] = tiles(np.concatenate([part[9], part[10]], 1), 8, 2)
    A["w_pa"], A["w_pb"] = tiles(f["w_proj_a"][0], 4, 4), tiles(f["w_proj_b"][0], 4, 4)
    A["w_o"] = tiles(f["w_out"][0], 8, 2)
    A["w_pq"] = tiles(f["peer_wq"][0], 8, 2)
    A["sub_keys"] = np.ascontiguousarray(f["peer_sub_keys"][0].reshape(16, 128, 128).transpose(2, 0, 1).reshape(128, 2048))
    A["u"] = np.ascontiguousarray(
        f["peer_u"][0].reshape(64, 2, 128, 8, 128).transpose(0, 4, 1, 3, 2).reshape(64, 128, 2048))
    A["v"] = np.ascontiguousarray(f["peer_v"][0].reshape(64, 2, 128, 1024).transpose(0, 2, 1, 3).reshape(64, 128, 2048))
    w = f["w_in_2"][0]
    o = np.cumsum([0, 256, 256, 256, 512, 512, 512, 128, 128, 256, 256, 16])
    p2 = [w[:, o[n]:o[n + 1]] for n in range(11)]
    A["w2_cb"], A["w2_cc"], A["w2_ch"] = (tiles(p2[n], 8, 2) for n in range(3))
    A["w2_mq"], A["w2_mk"], A["w2_mv"] = tiles(p2[3], 8, 2), tiles(p2[4], 8, 2), rows(p2[5], 512)
    A["w2_gk"] = tiles(np.concatenate([p2[6], p2[7]], 1), 8, 2)
    A["w2_gv"], A["w2_go"] = rows(p2[8], 256), tiles(p2[9], 8, 2)
    A["w2_lr"] = np.ascontiguousarray(p2[10].reshape(8, 128, 16).transpose(1, 0, 2).reshape(1, 128, 128))
    A["w2_o"] = tiles(f["w_out_2"][0], 8, 2)
    A["w2_xq"] = tiles(f["xattn_wq_2"][0], 8, 2)
    kv = f["xattn_wkv_2"][0]
    A["w2_xk"], A["w2_xv"] = tiles(kv[:, 0:256], 8, 2), rows(kv[:, 256:512], 256)
    A["w2_xo"] = tiles(f["xattn_wo_2"][0], 2, 8)
    pad = lambda a, n: np.concatenate([a, np.zeros((a.shape[0], n - a.shape[1]), a.dtype)], 1)

    def ag(a):
        x, y = pad(a[:, :2752], 2816).reshape(-1, 22, 1, 128), pad(a[:, 2752:], 2816).reshape(-1, 22, 1, 128)
        return np.concatenate([x, y], 2).reshape(a.shape[0], 5632)

    A["w_up"] = tiles(ag(f["ffn_w_up_2"][0]), 8, 2)
    dn = pad(f["ffn_w_down_2"][0].T, 2816).T
    A["w_dn"] = np.ascontiguousarray(
        dn.reshape(22, 128, 8, 128).transpose(2, 0, 1, 3).reshape(22, 8, 128, 128).transpose(0, 2, 1, 3).reshape(22, 128, 1024))
    A["xT"] = np.ascontiguousarray(f["x"][0].T.reshape(8, 128, 256).transpose(1, 0, 2))
    A["memT"] = np.ascontiguousarray(f["mem_2"][0].T.reshape(8, 128, 256).transpose(1, 0, 2))
    A["rel_bias"] = f["rel_bias"]
    A["w_gate"] = f["gla_w_gate_2"][0]
    A["b_gate"] = f["gla_b_gate_2"]
    parts = [("c", cols(f["c"])), ("b_ada", cols(f["b_ada"])), ("norm1_g", cols(f["norm1_g"])),
             ("norm2_g", cols(f["norm2_g"])), ("final_g", cols(f["final_g"])), ("norm_mix_g", cols(f["norm_mix_g_2"])),
             ("norm_xattn_g", cols(f["norm_xattn_g_2"])), ("norm_mem_g", cols(f["norm_mem_g_2"])),
             ("norm_ffn_g", cols(f["norm_ffn_g_2"])), ("final_norm_g", cols(f["final_norm_g_2"])),
             ("sc_w", cols(f["sc_conv_w_2"])), ("sc_b", cols(f["sc_conv_b_2"])),
             ("gla_norm_g", np.concatenate([f["gla_norm_g_2"], f["gla_norm_g_2"]], 1).T),
             ("f_w", cols(ag(f["ffn_conv_w_2"][0]))), ("f_b", cols(ag(f["ffn_conv_b_2"])))]
    voff, n = {}, 0
    for name, a in parts:
        voff[name] = n
        n += a.shape[1]
    A["vecs"] = np.ascontiguousarray(np.concatenate([a for _, a in parts], 1))
    A["cst"], A["oh"], A["gcst"], A["bmm"] = constants()
    return A, voff


def kernel(**inputs):
    import concourse.bacc as bacc
    from concourse.bass_utils import run_bass_kernel_spmd

    arrays, voff = lay_out(inputs)
    nc = bacc.Bacc("TRN2", target_bir_lowering=False, num_devices=1)
    A, feeds = {}, {}
    for name, a in arrays.items():
        A[name] = nc.dram_tensor(f"in_{name}", a.shape, mybir.dt.from_np(a.dtype), kind="ExternalInput").ap()
        feeds[f"in_{name}"] = a
    A["voff"] = voff
    scratch = nc.dram_tensor("skew", (8, 128, 384), F32, kind="Internal").ap()
    out = nc.dram_tensor("out_0", (128, 8, 256), F32, kind="ExternalOutput").ap()
    build(nc, A, out, scratch)
    r = run_bass_kernel_spmd(nc, [feeds], core_ids=[0])
    y = r.results[0]["out_0"]
    return np.ascontiguousarray(np.asarray(y).transpose(2, 1, 0).reshape(1, 256, 1024))
```

```python
import math
from contextlib import ExitStack

import numpy as np

import concourse.bass as bass
from concourse import mybir
from concourse.alu_op_type import AluOpType as ALU

ACT = mybir.ActivationFunctionType
F32 = mybir.dt.float32
U32 = mybir.dt.uint32
F32R = mybir.dt.float32r
AX = mybir.AxisListType.X

T = 256
NC = 2048
UNIT = 1024
NEG = -1.0e30
LOW = -3.0e38
GONE = -3.4e38
EPS = 1e-6


class Queues:

    def __init__(self, nc, ctx):
        self.nc = nc
        self.ctx = ctx
        self.names = ["tensor", "vector", "scalar", "gpsimd", "sync"]
        self.items = {n: [] for n in self.names}
        self.sems = {n: ctx.enter_context(nc.semaphore(f"done_{n}")) for n in self.names}
        self.count = {n: 0 for n in self.names}
        self.nload = 0

    def do(self, eng, fn, *after, inc=True, apart=False):
        if eng != "tensor" and not apart:
            after = after + ((eng, self.sems[eng], self.count[eng]),)
        self.items[eng].append((after, fn, self.sems[eng] if inc else None, 1))
        if inc:
            self.count[eng] += 1
        return (eng, self.sems[eng], self.count[eng])

    def load(self, eng, out, in_, *after):
        self.nload += 1
        sem = self.ctx.enter_context(self.nc.semaphore(f"dma{self.nload}"))
        return self.dma(eng, out, in_, sem, 1, *after)

    def dma(self, eng, out, in_, sem, nth, *after):
        e = self.engine(eng)
        self.items[eng].append((after, lambda: e.dma_start(out, in_), sem, 16))
        return (f"dma {id(sem)}", sem, 16 * nth)

    def engine(self, n):
        return {"tensor": self.nc.tensor, "vector": self.nc.vector, "scalar": self.nc.scalar,
                "gpsimd": self.nc.gpsimd, "sync": self.nc.sync}[n]

    def emit(self, eng, handle):
        seen = {}
        for after, fn, sem, by in self.items[eng]:
            for m in after:
                if m is None:
                    continue
                who, s, v = m
                if v > 0 and seen.get(who, 0) < v:
                    handle.wait_ge(s, v)
                    seen[who] = v
            ins = fn()
            if sem is not None:
                ins.then_inc(sem, by)


def build(nc, A, out, scratch):
    with ExitStack() as ctx:
        q = Queues(nc, ctx)
        V, S, G, TE = nc.vector, nc.scalar, nc.gpsimd, nc.tensor

        def sb(name, shape, dt=F32, where=ctx):
            return where.enter_context(nc.sbuf_tensor(name, shape, dt))

        ringb = sb("ringb", [128, 4, UNIT])
        split = sb("split", [128, 3, 2, UNIT], F32R)
        xT = sb("xT", [128, 8, T])
        H = sb("H", [128, 2, 8, T], F32R)
        cst = sb("cst", [128, 768])
        vecs = sb("vecs", [128, A["vecs"].shape[1]])
        mod = sb("mod", [128, 48])
        sm = sb("sm", [128, 160])
        cond = sb("cond", [128, 8])
        rT = sb("rT", [128, 5, T])
        banks = [ctx.enter_context(nc.psum_tensor(f"bank{i}", [128, 512], F32)) for i in range(8)]
        bank_free = [None] * 8
        bank_at = [0]
        held = set()

        def take():
            assert len(held) < 8
            while bank_at[0] % 8 in held:
                bank_at[0] += 1
            i = bank_at[0] % 8
            bank_at[0] += 1
            held.add(i)
            return i

        def free(b, mark):
            bank_free[b] = mark
            held.discard(b)

        def room(n=1):
            return 8 - len(held) >= n + 2

        ident = cst[:, 0:128]
        ones = cst[:, 128:256]
        tri_gt = cst[:, 256:384]
        up_strict = cst[:, 384:512]
        bd64 = cst[:, 512:640]
        iota = cst[:, 640:768]

        def dve(fn, *after, **k):
            return q.do("vector", fn, *after, **k)

        def act(fn, *after, **k):
            return q.do("scalar", fn, *after, **k)

        def pool(fn, *after, **k):
            return q.do("gpsimd", fn, *after, **k)

        def pe(fn, *after, **k):
            return q.do("tensor", fn, *after, **k)

        def mm(o, l, r, start, stop, *after, inc=False):
            return pe(lambda: TE.matmul(o, l, r, start=start, stop=stop, skip_group_check=True), *after, inc=inc)

        def mm3(o, l, r, start, stop, *after, inc=False):
            mm(o, l[0], r[0], start, False, *after)
            mm(o, l[0], r[1], False, False)
            return mm(o, l[1], r[0], False, stop, inc=inc)

        jobs = []

        def spawn(gen):
            jobs.append(gen)

        def pump(conc=3):
            for g in list(jobs[:conc]):
                if next(g, "end") == "end":
                    jobs.remove(g)

        def drain():
            while jobs:
                pump()

        slot_ap, slot_sem, slot_uses, slot_free = [], [], [], []
        sets = {}

        def add_slots(name, aps):
            sets[name] = list(range(len(slot_ap), len(slot_ap) + len(aps)))
            for ap in aps:
                slot_sem.append(ctx.enter_context(nc.semaphore(f"slot{len(slot_ap)}")))
                slot_ap.append(ap)
                slot_uses.append(0)
                slot_free.append(())

        add_slots("near", [ringb[:, i, :] for i in range(2)])
        add_slots("ab", [ringb[:, i, :] for i in (2, 3)])
        sets["four"] = sets["near"] + sets["ab"]
        AB = ringb[:, 2:4, :].rearrange("p a b -> p (a b)")
        queue, loaded, ready, turn = [], [], [], {}
        limit = [0]
        ahead = [1]
        share = [0]
        part = {}
        bufs = [(split[:, i, 0, :], split[:, i, 1, :]) for i in range(3)]
        buf_free = [(i, None) for i in range(3)]
        closed = set()

        def add_bufs(t, n, *after):
            for i in range(n):
                buf_free.append((len(bufs), after[0] if after else None))
                bufs.append((t[:, i, 0, :], t[:, i, 1, :]))

        def close_bufs():
            closed.update(range(3, len(bufs)))
            buf_free[:] = [x for x in buf_free if x[0] not in closed]

        def plan(name, n, where, kind="split", width=UNIT):
            for i in range(n):
                j = part.get(name, 0)
                part[name] = j + 1
                queue.append((name, j, width, where, kind))

        def fetch():
            if len(loaded) == limit[0]:
                return False
            name, j, width, where, kind = queue[len(loaded)]
            ss = sets[where]
            s = ss[turn.get(where, 0) % len(ss)]
            if slot_free[s] is None:
                return False
            turn[where] = turn.get(where, 0) + 1
            slot_uses[s] += 1
            w = A[name].shape[2]
            per = max(w // UNIT, 1)
            src = A[name][j // per][:, (j % per) * UNIT:(j % per) * UNIT + width]
            raw = slot_ap[s][:, 0:width]
            m = q.dma("sync", raw, src, slot_sem[s], slot_uses[s], *slot_free[s])
            slot_free[s] = None
            loaded.append((raw, m, s))
            return True

        copied = []

        def prepare_hi():
            name, j, width, where, kind = queue[len(copied)]
            raw, m, s = loaded[len(copied)]
            if kind == "raw":
                copied.append(None)
                return
            b, free_at = buf_free.pop(0)
            hi, lo = bufs[b]
            mh = act(lambda: S.copy(hi[:, 0:width], raw), m, free_at, apart=True)
            copied.append((b, mh, free_at))

        def prepare_lo():
            name, j, width, where, kind = queue[len(ready)]
            raw, m, s = loaded[len(ready)]
            if kind == "raw":
                ready.append((raw, m, s))
                return
            b, mh, free_at = copied[len(ready)]
            hi, lo = bufs[b]
            if share[0] and len(ready) % share[0] == 0:
                ml = pool(lambda: G.tensor_tensor(lo[:, 0:width], raw, hi[:, 0:width].bitcast(F32), ALU.subtract),
                          mh, free_at, apart=True)
            else:
                ml = dve(lambda: V.tensor_tensor(lo[:, 0:width], raw, hi[:, 0:width].bitcast(F32), ALU.subtract),
                         mh, free_at, apart=True)
            slot_free[s] = (ml,)
            ready.append(((hi, lo), ml, b))

        taken = [0]

        def unit(name, conc=3):
            while name != "w_ada" and queue[taken[0]][0] == "w_ada":
                ada_step()
            n = taken[0]
            taken[0] += 1
            assert queue[n][0] == name, (queue[n], name)
            while fetch():
                pass
            stage(n)
            while len(ready) <= n:
                prepare_lo()
            pump(conc)
            data, m, s = ready[n]

            def done(mark):
                if queue[n][4] == "raw":
                    slot_free[s] = (mark,)
                elif s not in closed:
                    buf_free.append((s, mark))
            return data, m, done

        def stage(n):
            while fetch():
                pass
            while len(ready) < len(copied):
                prepare_lo()
            while len(copied) < min(len(loaded), n + ahead[0]) and (buf_free or queue[len(copied)][4] == "raw"):
                prepare_hi()

        l_vecs = q.load("scalar", vecs[:, :], A["vecs"])
        l_cst = q.load("scalar", cst[:, :], A["cst"])
        l_x = q.load("scalar", xT[:, :, :], A["xT"])
        VO = A["voff"]

        def vec(name, j, n=1):
            o = VO[name] + j
            return vecs[:, o:o + n]

        def tri3(ap, n):
            return ap.rearrange("p (a b) -> p a b", a=n)

        def flat(ap):
            return ap.rearrange("p a b -> p (a b)")

        m_cond = act(lambda: S.activation(cond[:, :], vec("c", 0, 8), ACT.Silu), l_vecs)

        m_mod = []
        ada_at = {"k": 0, "g": 0, "free": [None, None], "sum": None}

        def ada_sum():
            if ada_at["sum"]:
                g, acc, m = ada_at["sum"]
                ada_at["sum"] = None
                b = take()
                for j in range(8):
                    last = mm(banks[b][:, j:j + 1], acc[:, j * 128:(j + 1) * 128], ones[:, 0:1], True, True,
                              m, l_cst, bank_free[b], inc=(j == 7))
                ada_at["free"][g % 2] = last
                m_mod.append(dve(lambda: V.tensor_tensor(mod[:, 8 * g:8 * g + 8], banks[b][:, 0:8], vec("b_ada", 8 * g, 8), ALU.add),
                                 last, l_vecs))
                free(b, m_mod[-1])

        def ada_step():
            ada_sum()
            k, g = ada_at["k"], ada_at["g"]
            acc = ada_at["acc"][:, g % 2, :]
            w, lw, done = unit("w_ada", 0)
            if k == 0:
                m = dve(lambda: V.tensor_scalar(acc, w, cond[:, 0:1], None, ALU.mult), lw, m_cond, ada_at["free"][g % 2])
            else:
                m = dve(lambda: V.scalar_tensor_tensor(out=acc, in0=w, scalar=cond[:, k:k + 1], in1=acc,
                                                       op0=ALU.mult, op1=ALU.add), lw)
            done(m)
            ada_at["k"] = (k + 1) % 8
            if k == 7:
                ada_at["sum"] = (g, acc, m)
                ada_at["g"] = g + 1

        def newton(r, ms, t, m):
            m = dve(lambda: V.tensor_tensor(t, r, r, ALU.mult), m)
            m = dve(lambda: V.tensor_tensor(t, t, ms, ALU.mult), m)
            m = dve(lambda: V.tensor_scalar(t, t, -0.5, 1.5, ALU.mult, ALU.add), m)
            return dve(lambda: V.tensor_tensor(r, r, t, ALU.mult), m)

        t_free = [None] * 4

        def sumsq():
            st = {"b": take(), "k": 0, "n": 0}

            def square(src, m):
                k = st["n"]
                st["n"] += 1
                t = rT[:, (2, 3, 4, 0)[k % 4], :]
                m = act(lambda: S.activation(t, src, ACT.Square), m, t_free[k % 4], apart=True)
                return t, m

            def total(t, m):
                k = st["k"]
                st["k"] += 1
                t_free[k % 4] = st["last"] = mm(banks[st["b"]][:, 0:T], ones, t, k == 0, k == 7, m, l_cst,
                                                bank_free[st["b"]], inc=True)

            st.update(square=square, total=total, add=lambda src, m: total(*square(src, m)))
            return st

        def root(st):
            assert st["k"] == 8
            b = st["b"]
            ms, r, t0 = rT[:, 0, :], rT[:, 1, :], rT[:, 4, :]
            a = dve(lambda: V.tensor_scalar(ms, banks[b][:, 0:T], 1.0 / 1024, EPS, ALU.mult, ALU.add), st["last"])
            free(b, a)
            m = act(lambda: S.activation(t0, ms, ACT.Sqrt), a)
            m = dve(lambda: V.reciprocal(r, t0), m)
            st["r"] = t_free[2] = t_free[3] = newton(r, ms, t0, m)
            return st["r"]

        def norm(src, st, gain, m_free=(), shift=None, m_shift=(), dst=None, keep=None):
            m = st.get("r") or root(st)
            r = rT[:, 1, :]
            if keep is not None:
                return [dve(lambda j=j: V.scalar_tensor_tensor(out=keep[:, j, :], in0=src[:, j, :], scalar=gain(j), in1=r,
                                                               op0=ALU.mult, op1=ALU.mult), m, l_vecs, apart=True)
                        for j in range(8)]
            outs = []
            for _ in norm_steps(outs, m, src, gain, m_free, shift, m_shift, dst):
                pass
            return outs

        def norm_steps(outs, m, src, gain, m_free, shift, m_shift, dst):
            r, scaled = rT[:, 1, :], {}

            def scale(j):
                t = rT[:, 2 + j % 3, :]
                scaled[j] = dve(lambda: V.scalar_tensor_tensor(out=t, in0=src[:, j, :], scalar=gain(j), in1=r,
                                                               op0=ALU.mult, op1=ALU.mult), m, l_vecs, t_free[j % 3], *m_free, apart=True)

            scale(0)
            scale(1)
            for j in range(8):
                t, hi, lo = rT[:, 2 + j % 3, :], dst[:, 0, j, :], dst[:, 1, j, :]
                if shift:
                    n = act(lambda hi=hi, t=t, j=j: S.activation(hi, t, ACT.Identity, bias=shift(j)), scaled[j], *m_shift, apart=True)
                else:
                    n = act(lambda hi=hi, t=t: S.copy(hi, t), scaled[j], apart=True)
                if j + 2 < 8:
                    scale(j + 2)
                if shift:
                    n = dve(lambda hi=hi, lo=lo, t=t, j=j: V.scalar_tensor_tensor(
                        out=lo, in0=t, scalar=shift(j), in1=hi.bitcast(F32), op0=ALU.add, op1=ALU.subtract), n, apart=True)
                else:
                    n = dve(lambda hi=hi, lo=lo, t=t: V.tensor_tensor(lo, t, hi.bitcast(F32), ALU.subtract), n, apart=True)
                t_free[j % 3] = n
                outs.append(n)
                yield

        def cut(hi, lo, src, *after):
            m = act(lambda: S.copy(hi, src), *after)
            return dve(lambda: V.tensor_tensor(lo, src, hi.bitcast(F32), ALU.subtract), m)

        def lin(name, ncols, rhs, m_rhs, evac, kt=8, conc=3, c0=0):
            at = {"left": 0}
            for p in range(c0 // 2, ncols // 2):
                b = None
                for j in range(2):
                    for k in range(kt):
                        if at["left"] == 0:
                            w, lw, done = unit(name, conc)
                            at.update(w=w, lw=lw, done=done, left=8)
                        if b is None:
                            b = take()
                        o = (8 - at["left"]) * 128
                        at["left"] -= 1
                        wh, wl = at["w"]
                        last = mm3(banks[b][:, j * T:(j + 1) * T], (wh[:, o:o + 128], wl[:, o:o + 128]), rhs(k),
                                   k == 0, k == kt - 1, at["lw"], m_rhs(k), bank_free[b],
                                   inc=(k == kt - 1 or at["left"] == 0))
                        if at["left"] == 0:
                            at["done"](last)
                evac(p, b, last)

        def lin_nat(name, lhs, m_lhs, width, evac):
            b2 = None
            kk = UNIT // width
            for c in range(8 // kk):
                w, lw, done = unit(name)
                b2 = b2 or [take(), take()]
                for ki in range(kk):
                    k = c * kk + ki
                    for t in range(2):
                        last = mm3(banks[b2[t]][:, 0:width], lhs(k, t),
                                   (w[0][:, ki * width:(ki + 1) * width], w[1][:, ki * width:(ki + 1) * width]),
                                   k == 0, k == 7, lw, m_lhs(k), bank_free[b2[t]], inc=True)
                done(last)
            for t in range(2):
                evac(t, b2[t], last)

        def of(X):
            return lambda k: (X[:, 0, k, :], X[:, 1, k, :])

        def of_t(X):
            return lambda k, t: (X[:, 0, k, t * 128:(t + 1) * 128], X[:, 1, k, t * 128:(t + 1) * 128])

        hk, hkt = of(H), of_t(H)

        def copy_to(dst, store):
            def evac(c, b, m):
                n = act(lambda: S.copy(dst[:, c * 512:(c + 1) * 512], banks[b][:, :]), m)
                store.append(n)
                free(b, n)
            return evac

        def nat_to(dst, width, store):
            def evac(t, b, m):
                n = act(lambda: S.copy(dst[:, t * width:(t + 1) * width], banks[b][:, 0:width]), m)
                store.append(n)
                free(b, n)
            return evac

        def attend(heads, qT, kT, vN, Y, y0, marks, bm, m_bm, W_of, st_all, scale, sc, m_free, ydone):
            lfree = [m_free] * 3
            ptfree = [m_free] * 3
            state = {"z": [0, 1, 2], "y": {}, "live": 0}

            def item(pair, t, par):
                while not state["z"] or (pair not in state["y"] and state["live"]):
                    yield
                z = state["z"].pop(0)
                L, PT = sc[:, z * 512:(z + 1) * 512], sc[:, 1536 + z * 512:1536 + (z + 1) * 512]
                nk = W_of(t)
                W = 128 * nk
                hs = [4 * pair + par, 4 * pair + par + 2]
                rows = slice(64 * par, 64 * par + 64)
                while not room(1 if pair in state["y"] else 3):
                    yield
                if pair not in state["y"]:
                    yb = [take(), take()]
                    state["y"][pair] = [yb, [bank_free[i] for i in yb], 0]
                    state["live"] = 1
                b = take()
                for i, h in enumerate(hs):
                    last = mm(banks[b][:, i * 256:i * 256 + W], qT[rows, h // 2, t * 128:(t + 1) * 128],
                              kT[rows, h // 2, 0:W], True, True, *marks(), bank_free[b], inc=(i == 1))
                Lz = tri3(L, 2)[:, :, 0:W]
                bz = tri3(banks[b][:, :], 2)[:, :, 0:W]
                st = st_all[:, 8 * z:8 * z + 8]
                if bm:
                    m = dve(lambda: V.scalar_tensor_tensor(out=Lz, in0=bz, scalar=scale, in1=bm(hs[0], t, W),
                                                           op0=ALU.mult, op1=ALU.add), last, *lfree[z], *m_bm(), apart=True)
                    free(b, m)
                    m = dve(lambda: V.tensor_reduce(st[:, 0:2], Lz, AX, ALU.max, negate=True), m)
                    src, esc = Lz, 1.0
                else:
                    m = dve(lambda: V.tensor_reduce(st[:, 2:4], bz, AX, ALU.max), last, *lfree[z], apart=True)
                    m = dve(lambda: V.tensor_scalar(st[:, 0:2], st[:, 2:4], -scale, None, ALU.mult), m)
                    src, esc = bz, scale
                for i in range(2):
                    e = act(lambda i=i: S.activation(Lz[:, i, :], src[:, i, :], ACT.Exp, bias=st[:, i:i + 1], scale=esc,
                                                     accum_out=st[:, 4 + i:5 + i]), m, *lfree[z], apart=True)
                if not bm:
                    free(b, e)
                m = dve(lambda: V.reciprocal(st[:, 6:8], st[:, 4:6]), e)
                for i in range(2):
                    x = dve(lambda i=i: V.tensor_scalar(Lz[:, i, :], Lz[:, i, :], st[:, 6 + i:7 + i], None, ALU.mult), m, apart=True)
                yield
                yield
                while not room(1):
                    yield
                b = take()
                for i in range(2):
                    for k in range(nk):
                        last = pe(lambda i=i, k=k: TE.transpose(
                            banks[b][:, i * 256 + k * 128:i * 256 + k * 128 + 128],
                            Lz[:, i, k * 128:(k + 1) * 128], ident), x, bank_free[b])
                lfree[z] = (last,)
                PTz = tri3(PT, 2)
                m = act(lambda b=b: S.copy(PTz[:, :, 0:W], tri3(banks[b][:, :], 2)[:, :, 0:W]), last, *ptfree[z], apart=True)
                free(b, m)
                yield
                yb, fr, _ = state["y"][pair]
                for i, h in enumerate(hs):
                    for k in range(nk):
                        last = mm(banks[yb[i]][64 * par:64 * par + 64, t * 128:(t + 1) * 128],
                                  vN[:, k, 64 * h:64 * h + 64], PTz[:, i, k * 128:(k + 1) * 128],
                                  (k == 0), k == nk - 1, m, fr[i], inc=True)
                ptfree[z] = (last,)
                state["z"].append(z)
                state["y"][pair][2] += 1
                if state["y"][pair][2] == 4:
                    state["live"] = 0
                    for i in range(2):
                        j = 2 * pair + i
                        m = cut(Y[:, 0, y0 + j, :], Y[:, 1, y0 + j, :], banks[yb[i]][:, 0:T], last)
                        free(yb[i], m)
                        ydone[j] = m

            items = [(pair, t, par) for pair in range(heads // 4) for t in range(2) for par in range(2)]

            def run():
                lanes = []
                left = list(items)
                while left or lanes:
                    if len(lanes) < 3 and left:
                        if not lanes or lanes[-1][1] > 0:
                            lanes.append([item(*left.pop(0)), 0])
                    for ln in list(lanes):
                        ln[1] += 1
                        if next(ln[0], "end") == "end":
                            lanes.remove(ln)
                    yield
            return run()

        def parted(w, where, kind="split", width=UNIT):
            for nm, k in w:
                plan(nm, k, where, kind, width)

        plan("w_ada", 16, "far", "raw")
        parted([("w_qi", 4), ("w_ki", 1), ("w_wi", 1), ("w_qb", 4), ("w_kb", 4), ("w_vb", 4)], "far")
        for nm, k in [("w_qa", 4), ("w_ka", 4), ("w_va", 4), ("w_g", 16), ("w_pb", 4)]:
            for i in range(k):
                plan(nm, 1, "far")
                plan("w_ada", 1, "far", "raw")
        parted([("w_pa", 4), ("w_o", 8)], "far")
        parted([("w_pq", 16), ("u", 128)], "four")
        plan("v", 2, "near")
        plan("v", 102, "four")
        plan("w2_xk", 2, "four")
        plan("w2_xv", 2, "four")
        plan("v", 24, "four")
        parted([("w2_mq", 4), ("w2_mk", 4), ("w2_mv", 4), ("w2_gk", 2), ("w2_gv", 2), ("w2_lr", 1), ("w2_go", 2), ("w2_cc", 2), ("w2_ch", 2),
                ("w2_cb", 2), ("w2_o", 8), ("w2_xq", 2), ("w2_xo", 2)], "far2")
        plan("w_up", 44, "far2")
        plan("w_dn", 22, "far2")

        limit[0] = [k[0] for k in queue].index("v") + 2

        ph = ExitStack()
        far = sb("far", [128, 3, UNIT], where=ph)
        add_slots("far", [far[:, i, :] for i in range(3)])
        sets["far"] = sets["four"] + sets["far"]
        PA = sb("PA", [128, 20672], where=ph)
        Yb = sb("Yb", [128, 2, 4, T], F32R, where=ph)
        Ya = sb("Ya", [128, 2, 4, T], F32R, where=ph)
        off = [0]
        base = [PA]

        def scr(n):
            a = off[0]
            off[0] += n
            assert off[0] <= base[0].shape[1], off[0]
            return base[0][:, a:a + n]

        zbuf = sb("zbuf", [128, 2, 3, 384], where=ph)
        split1 = sb("split1", [128, 1, 2, UNIT], F32R, where=ph)
        add_bufs(split1, 1)
        ada_at["acc"] = sb("ada_acc", [128, 2, UNIT], where=ph)
        qiT, kiT = tri3(scr(1024), 4), scr(256)
        qaT, kaT, va = scr(1024), scr(1024), scr(1024)
        qbT, kbT, vb = scr(1024), scr(1024), scr(1024)
        sg = tri3(scr(4096), 16)
        bm = tri3(scr(3072), 8)
        madd = scr(384)
        relw = scr(2304)
        relb, wk = relw[:, 0:2048], relw[:, 2048:2304]
        sc_a = scr(3072)

        sums = sumsq()
        for j in range(8):
            sums["add"](xT[:, j, :], l_x)
        for c in range(16):
            ada_step()
            if c == 8:
                root(sums)
        ahead[0] = 4
        stage(taken[0])
        stage(taken[0])
        ada_sum()
        m_mod1 = m_mod[1]
        m = dve(lambda: V.tensor_scalar(sm[:, 32:40], mod[:, 8:16], 1.0, None, ALU.add), m_mod1)
        m_A1 = dve(lambda: V.tensor_tensor(sm[:, 24:32], sm[:, 32:40], vec("norm1_g", 0, 8), ALU.mult), m)
        h1 = norm(xT, sums, lambda j: sm[:, 24 + j:25 + j], [m_A1], shift=lambda j: mod[:, j:j + 1], m_shift=[m_mod1], dst=H)
        mh = lambda k: h1[k]

        ohs = sc_a[0:32, :]
        l_oh = q.load("scalar", ohs[:, 0:384], A["oh"])
        l_rb = q.load("scalar", ohs[:, 384:392], A["rel_bias"])
        reps, stores, l_bm, bias_end = [], [], [], []
        rbs = flat(sg)

        def bias_job():
            for h in range(8):
                o = 512 + 128 * h
                reps.append(dve(lambda h=h, o=o: V.tensor_copy(ohs[:, o:o + 128], ohs[:, 384 + h:385 + h].broadcast_to((32, 128))),
                                l_rb))
            for h in range(8):
                o = 512 + 128 * h
                b = take()
                rb = rbs[:, 384 * h:384 * h + 384]
                m = mm(banks[b][:, 0:384], ohs[:, o:o + 128], ohs[:, 0:384], True, True, reps[h], l_oh, bank_free[b], inc=True)
                w = dve(lambda b=b, rb=rb: V.tensor_copy(rb, banks[b][:, 0:384]), m)
                free(b, w)
                stores.append(q.load("gpsimd", scratch[h], rb, w))
                yield
            bias_end.append(m)
            for h in range(8):
                fl = scratch[h].rearrange("p n -> (p n)")
                src = fl[127:127 + 128 * 383].rearrange("(p n) -> p n", n=383)
                l_bm.append(q.load("gpsimd", bm[:, h, 128:384], src[:, 0:256], stores[h]))

        spawn(bias_job())

        qi_m = []
        lin("w_qi", 4, hk, mh, copy_to(flat(qiT), qi_m))
        w, lw, done = unit("w_ki")
        b = take()
        for k in range(8):
            last = mm3(banks[b][:, 0:T], (w[0][:, k * 128:(k + 1) * 128], w[1][:, k * 128:(k + 1) * 128]), hk(k),
                       k == 0, k == 7, lw, bank_free[b], inc=(k == 7))
        done(last)
        m_ki = act(lambda b=b: S.copy(kiT, banks[b][:, 0:T]), last)
        free(b, m_ki)
        w, lw, done = unit("w_wi")
        b = take()
        for k in range(8):
            last = mm3(banks[b][:, 0:T], (w[0][:, k * 128:(k + 1) * 128], w[1][:, k * 128:(k + 1) * 128]), hk(k),
                       k == 0, k == 7, lw, bank_free[b], inc=(k == 7))
        done(last)
        wiT = wk
        m = act(lambda b=b: S.copy(wiT, banks[b][:, 0:T]), last)
        free(b, m)
        b = take()
        for t in range(2):
            last = pe(lambda b=b, t=t: TE.transpose(banks[b][:, 128 * t:128 * t + 128], wiT[:, 128 * t:128 * t + 128], ident),
                      m, bank_free[b])
        m_wi = dve(lambda b=b: V.tensor_scalar(tri3(sm[:, 48:64], 2), tri3(banks[b][:, 0:256], 2)[:, :, 0:8], (64 ** -0.5) * (8 ** -0.5), None, ALU.mult), last)
        free(b, m_wi)

        m_bm, index_end = [], []

        def index_job():
            m_rel_free = None
            for t in range(2):
                W = 128 * (t + 1)
                rel = relb.rearrange("p (a b) -> p a b", a=8)[:, :, 0:W]
                for par in range(2):
                    for g in range(2):
                        while not room(1):
                            yield
                        b = take()
                        hs = [par + 4 * g, par + 4 * g + 2]
                        rows = slice(64 * par, 64 * par + 64)
                        for i, h in enumerate(hs):
                            last = mm(banks[b][:, i * 256:i * 256 + W], qiT[rows, h // 2, t * 128:(t + 1) * 128],
                                      kiT[rows, 0:W], True, True, qi_m[-1], m_ki, bank_free[b], inc=(i == 1))
                        mr = act(lambda b=b, h=hs[0], rel=rel, W=W: S.activation(
                            rel[:, h:h + 3:2, :], tri3(banks[b][:, :], 2)[:, :, 0:W], ACT.Relu), last, m_rel_free)
                        free(b, mr)
                yield
                acc = wk[:, 0:W]
                m = dve(lambda rel=rel, acc=acc, t=t: V.tensor_scalar(acc, rel[:, 0, :], sm[:, 48 + 8 * t:49 + 8 * t], None, ALU.mult),
                        mr, m_wi)
                for h in range(1, 8):
                    m = dve(lambda rel=rel, acc=acc, t=t, h=h: V.scalar_tensor_tensor(
                        out=acc, in0=rel[:, h, :], scalar=sm[:, 48 + 8 * t + h:49 + 8 * t + h], in1=acc,
                        op0=ALU.mult, op1=ALU.add), m)
                m_rel_free = m
                m = pool(lambda acc=acc, W=W, t=t: G.affine_select(out=acc, in_=acc, compare_op=ALU.is_ge, fill=LOW, base=128 * t,
                                                                  pattern=[[-1, W]], channel_multiplier=1), m)
                yield
                for r in range(8):
                    m = dve(lambda acc=acc: V.max(sm[:, 64:72], acc), m)
                    m = dve(lambda acc=acc: V.match_replace(acc, sm[:, 64:72], acc, GONE), m)
                    if r % 2:
                        yield
                a, e = (0, 128) if t == 0 else (128, 384)
                md = madd[:, a:e]
                m = dve(lambda acc=acc, md=md: V.tensor_scalar(md, acc, -3.2e38, NEG, ALU.is_gt, ALU.mult), m)
                index_end.append(m)
                m_madd = pool(lambda md=md, W=W, t=t: G.affine_select(out=md, in_=md, compare_op=ALU.is_ge, fill=NEG, base=128 * t,
                                                                     pattern=[[-1, W]], channel_multiplier=1), m)
            m0 = pool(lambda: G.tensor_tensor(bm[:, :, 0:128], bm[:, :, 256:384],
                                              madd[:, 0:128].rearrange("p (a b) -> p a b", a=1).broadcast_to((128, 8, 128)), ALU.add),
                      m_madd, *l_bm)
            m_bm.append(pool(lambda: G.tensor_tensor(bm[:, :, 128:384], bm[:, :, 128:384],
                                                     madd[:, 128:384].rearrange("p (a b) -> p a b", a=1).broadcast_to((128, 8, 256)),
                                                     ALU.add), m0))

        spawn(index_job())

        qa_m, ka_m, va_m, qb_m, kb_m, vb_m = [], [], [], [], [], []
        lin("w_qb", 4, hk, mh, copy_to(qbT, qb_m))
        lin("w_kb", 4, hk, mh, copy_to(kbT, kb_m))
        lin_nat("w_vb", hkt, mh, 512, nat_to(vb, 512, vb_m))

        qb3, kb3, vb3 = tri3(qbT, 4), tri3(kbT, 4), tri3(vb, 2)
        yb_done = {}
        zs = [flat(zbuf[:, i, :, :]) for i in range(2)] + [relw[:, 0:1152], relw[:, 1152:2304]]
        zs = [[z[:, i * 384:(i + 1) * 384] for i in range(3)] for z in zs]
        up2 = up_strict.rearrange("p (o i) -> p o i", o=1).broadcast_to((128, 2, 128))

        def diagonals(z):
            return tri3(z, 3)[:, 0:3:2, :]

        def stick_job():
            while len(index_end) < 2:
                yield
            done_z = [tuple(index_end[-1:])] * 4
            for wave in range(2):
                while not room(4):
                    yield
                bs = [take() for _ in range(4)]
                ms = [None] * 4
                for i, b in enumerate(bs):
                    h = 4 * wave + i
                    r = slice(64 * (h % 2), 64 * (h % 2) + 64)
                    mm(banks[b][:, 0:256], kb3[r, h // 2, 0:128], qb3[r, h // 2, :], True, True,
                       qb_m[-1], kb_m[-1], bank_free[b])
                    last = mm(banks[b][:, 256:384], kb3[r, h // 2, 128:256], qb3[r, h // 2, 128:256], True, True, inc=True)
                    ms[i] = act(lambda b=b, i=i: S.activation(zs[i][0], banks[b][:, 0:384], ACT.Abs, scale=0.125),
                                last, *done_z[i], apart=True)
                yield
                mins = [dve(lambda b=b, i=i: V.tensor_scalar(zs[i][1], banks[b][:, 0:384], 0.125, 0.0, ALU.mult, ALU.min),
                            ms[i], *done_z[i], apart=True) for i, b in enumerate(bs)]
                ms = [act(lambda i=i: S.activation(zs[i][0], zs[i][0], ACT.Exp, scale=-1.0), ms[i], apart=True) for i in range(4)]
                yield
                ms = [act(lambda i=i: S.activation(zs[i][0], zs[i][0], ACT.Ln, bias=1.0), ms[i], apart=True) for i in range(4)]
                yield
                ms = [dve(lambda i=i: V.tensor_tensor(zs[i][1], zs[i][1], zs[i][0], ALU.subtract), mins[i], ms[i], apart=True)
                      for i in range(4)]
                yield
                for i, b in enumerate(bs):
                    ms[i] = dve(lambda b=b, i=i: V.scalar_tensor_tensor(out=zs[i][2], in0=banks[b][:, 0:384], scalar=-0.125, in1=zs[i][1],
                                                                        op0=ALU.mult, op1=ALU.add), ms[i], *done_z[i], apart=True)
                    free(b, ms[i])
                    ms[i] = pool(lambda i=i: G.tensor_tensor(diagonals(zs[i][2]), diagonals(zs[i][2]), up2, ALU.mult), ms[i], l_cst,
                                 apart=True)
                yield
                yield
                for i in range(4):
                    while not room(1):
                        yield
                    b = take()
                    z2 = zs[i][2]
                    mm(banks[b][:, 0:256], tri_gt, z2[:, 0:256], True, False, ms[i], bank_free[b])
                    mm(banks[b][:, 128:256], ones, z2[:, 256:384], False, True)
                    last = mm(banks[b][:, 256:384], tri_gt, z2[:, 256:384], False, True, inc=True)
                    ms[i] = dve(lambda b=b, i=i: V.tensor_tensor(zs[i][1], zs[i][1], banks[b][:, 0:384], ALU.add), last)
                    free(b, ms[i])
                    if i % 2:
                        yield
                for i in range(4):
                    m = act(lambda i=i: S.activation(zs[i][1], zs[i][1], ACT.Exp), ms[i], apart=True)
                    ms[i] = pool(lambda i=i: G.tensor_tensor(diagonals(zs[i][1]), diagonals(zs[i][1]), up2, ALU.mult), m, apart=True)
                yield
                yield
                for p in range(2):
                    while not room(1):
                        yield
                    yb = take()
                    fr = bank_free[yb]
                    for i in (2 * p, 2 * p + 1):
                        h = 4 * wave + i
                        z1 = zs[i][1]
                        o = banks[yb][64 * (h % 2):64 * (h % 2) + 64, :]
                        mm(o[:, 0:256], vb3[:, 0, 64 * h:64 * h + 64], z1[:, 0:256], True, False, ms[i], vb_m[-1], fr)
                        last = mm(o[:, 128:256], vb3[:, 1, 64 * h:64 * h + 64], z1[:, 256:384], False, True, inc=True)
                        done_z[i] = (last,)
                    j = 2 * wave + p
                    m = cut(Yb[:, 0, j, :], Yb[:, 1, j, :], banks[yb][:, 0:256], last)
                    free(yb, m)
                    yb_done[j] = m
                    yield

        spawn(stick_job())

        lin("w_qa", 4, hk, mh, copy_to(qaT, qa_m))
        lin("w_ka", 4, hk, mh, copy_to(kaT, ka_m))
        lin_nat("w_va", hkt, mh, 512, nat_to(va, 512, va_m))

        def bm_a(h, t, W):
            a = 0 if t == 0 else 128
            return bm[:, h:h + 3:2, a:a + W]

        ya_done = {}

        def attend_a():
            while not m_bm:
                yield
            yield from attend(8, tri3(qaT, 4), tri3(kaT, 4), tri3(va, 2), Ya, 0, lambda: [qa_m[-1], ka_m[-1], va_m[-1]],
                              bm_a, lambda: m_bm, lambda t: t + 1, sm[:, 80:104], 0.125, sc_a, (m_bm[-1], bias_end[0]), ya_done)

        spawn(attend_a())

        sg_m = []

        def gate(c, b, m):
            d = flat(sg[:, 2 * c:2 * c + 2, :])
            sg_m.append(act(lambda: S.activation(d, banks[b][:, :], ACT.Sigmoid), m, *stores))
            free(b, sg_m[-1])

        lin("w_g", 16, hk, mh, gate)
        M = H
        m_mg = [None] * 8

        def merge_b(c, b, m):
            g = flat(sg[:, 8 + 2 * c:8 + 2 * c + 2, :])
            n = dve(lambda: V.tensor_tensor(g, banks[b][:, :], g, ALU.mult), m, sg_m[-1])
            free(b, n)

        def merge_a(c, b, m):
            g = flat(sg[:, 2 * c:2 * c + 2, :])
            gb = flat(sg[:, 8 + 2 * c:8 + 2 * c + 2, :])
            n = dve(lambda: V.tensor_tensor(g, banks[b][:, :], g, ALU.mult), m)
            free(b, n)
            n = dve(lambda: V.tensor_tensor(g, g, gb, ALU.add), n)
            n = cut(flat(M[:, 0, 2 * c:2 * c + 2, :]), flat(M[:, 1, 2 * c:2 * c + 2, :]), g, n)
            m_mg[2 * c] = m_mg[2 * c + 1] = n

        lin("w_pb", 8, of(Yb), lambda k: yb_done[k], merge_b, kt=4)
        drain()
        while queue[taken[0]][0] == "w_ada":
            ada_step()
        close_bufs()
        lin("w_pa", 8, of(Ya), lambda k: ya_done[k], merge_a, kt=4)

        ada_sum()
        m_x = []

        def resid(col, sums):
            def evac(c, b, m):
                for j in range(2):
                    i = 2 * c + j
                    if col is None:
                        n = dve(lambda i=i, j=j: V.tensor_tensor(xT[:, i, :], banks[b][:, j * T:(j + 1) * T], xT[:, i, :], ALU.add), m)
                    else:
                        n = dve(lambda i=i, j=j: V.scalar_tensor_tensor(out=xT[:, i, :], in0=banks[b][:, j * T:(j + 1) * T],
                                                                        scalar=mod[:, col + i:col + i + 1], in1=xT[:, i, :],
                                                                        op0=ALU.mult, op1=ALU.add), m)
                    marks[i] = n
                free(b, n)
                m_x.append(n)

                def later():
                    while sums["n"] - sums["k"] > 2:
                        yield
                    sq = [sums["square"](xT[:, i, :], marks[i]) for i in (2 * c, 2 * c + 1)]
                    yield
                    for t, m in sq:
                        sums["total"](t, m)
                spawn(later())
            marks = {}
            return evac

        sums = sumsq()
        lin("w_o", 8, of(M), lambda k: m_mg[k], resid(16, sums))
        drain()
        ph.close()

        ph = ExitStack()
        PR = sb("PR", [128, 128 * 256], where=ph)
        m = dve(lambda: V.tensor_scalar(sm[:, 32:40], mod[:, 32:40], 1.0, None, ALU.add), m_mod[-1])
        m_A2 = dve(lambda: V.tensor_tensor(sm[:, 24:32], sm[:, 32:40], vec("norm2_g", 0, 8), ALU.mult), m)
        h2 = norm(xT, sums, lambda j: sm[:, 24 + j:25 + j], [m_A2], shift=lambda j: mod[:, 24 + j:25 + j], m_shift=[m_mod[-1]], dst=H)
        mh2 = lambda k: h2[k]

        o96 = 96 * 256
        SC = PR[:, o96:o96 + 4096].rearrange("p (t c n) -> p t c n", t=2, c=16)
        o = o96 + 4096
        cand = PR[:, o:o + 256]
        tv = PR[:, o + 512:o + 1024].rearrange("p (t c k) -> p t c k", t=2, c=16)
        ti = PR[:, o + 1024:o + 1536].rearrange("p (t c k) -> p t c k", t=2, c=16)
        tf = PR[:, o + 1536:o + 2048].rearrange("p (t c k) -> p t c k", t=2, c=16)
        eq = PR[:, o + 2048:o + 4096]
        qh = [PR[:, 22528 + i * 512:22528 + (i + 1) * 512] for i in range(3)]
        cv2 = PR[:, o + 256:o + 512].rearrange("p (t n) -> p t n", t=2)
        cp2 = sb("cp", [128, 2, 128], U32, where=ph)
        cpa = sb("cpa", [128, 128], U32, where=ph)
        cpf = sb("cpf", [128, 2, 128], where=ph)
        rt = sb("rt", [128, 3, 256], where=ph)
        cpn = rT[:, 4, :]
        skt = PR[:, 80 * 256:80 * 256 + 2048]
        l_sk = q.load("scalar", skt, A["sub_keys"], m_x[-1])
        qh_free = [None] * 3
        m_s = {}

        def peer_q(c, b, m):
            z = qh[c % 3]
            e = act(lambda: S.copy(z, banks[b][:, :]), m, qh_free[c % 3])
            free(b, e)

            def later():
                yield
                b = take()
                for t in range(2):
                    for j in range(2):
                        last = mm(banks[b][:, (2 * t + j) * 128:(2 * t + j + 1) * 128],
                                  z[:, j * T + t * 128:j * T + (t + 1) * 128],
                                  skt[:, (2 * c + j) * 128:(2 * c + j + 1) * 128], True, True, e, l_sk, bank_free[b], inc=True)
                qh_free[c % 3] = last
                x = act(lambda: S.copy(SC[:, :, 2 * c:2 * c + 2, :], banks[b][:, :].rearrange("p (t j n) -> p t j n", t=2, j=2)), last)
                free(b, x)
                m_s[c] = x
            spawn(later())

        lin("w_pq", 16, hk, mh2, peer_q)
        drain()
        rt_m = []
        share[0] = 3

        def lanes(*chains):
            ms = [None] * len(chains)
            for n, step in enumerate(zip(*chains)):
                for i, (fn, *after) in enumerate(step):
                    ms[i] = dve(fn, ms[i], *after, apart=n > 0)
            return ms

        def route_job():
            for t in range(2):
                ti_u = ti[:, t, :, :].bitcast(U32)

                def top(c):
                    s_, a, e = SC[:, t, c, :], slice(0, 8), slice(8, 16)
                    v_, i_ = tv[:, t, c, :], ti_u[:, c, :]
                    return [(lambda: V.max(v_[:, a], s_), m_s[c // 2]),
                            (lambda: V.max_index(i_[:, a], v_[:, a], s_),),
                            (lambda: V.match_replace(s_, v_[:, a], s_, GONE),),
                            (lambda: V.max(v_[:, e], s_),),
                            (lambda: V.max_index(i_[:, e], v_[:, e], s_),)]

                for c in range(0, 16, 2):
                    m = lanes(top(c), top(c + 1))[1]
                    yield
                    yield
                prev = dve(lambda ti_u=ti_u, t=t: V.tensor_copy(tf[:, t, :, :], ti_u), m)
                cv, cp = cv2[:, t, :], cp2[:, t, :]

                def pairs(h, cand, cv=cv, cp=cp):
                    a0 = tv[:, t, 2 * h, :].rearrange("p (k o) -> p k o", o=1).broadcast_to((128, 16, 16))
                    a1 = tv[:, t, 2 * h + 1, :].rearrange("p (o k) -> p o k", o=1).broadcast_to((128, 16, 16))
                    cs = slice(16 * h, 16 * h + 8)
                    ct = slice(16 * h + 8, 16 * h + 16)
                    return [(lambda: V.tensor_tensor(cand.rearrange("p (a b) -> p a b", a=16), a0, a1, ALU.add),),
                            (lambda: V.max(cv[:, cs], cand),),
                            (lambda: V.max_index(cp[:, cs], cv[:, cs], cand),),
                            (lambda: V.match_replace(cand, cv[:, cs], cand, GONE),),
                            (lambda: V.max(cv[:, ct], cand),),
                            (lambda: V.max_index(cp[:, ct], cv[:, ct], cand),)]

                for h in range(0, 8, 2):
                    prev = lanes(pairs(h, cand), pairs(h + 1, eq[:, 0:256]))[1]
                    yield
                    yield
                    yield
                cv3 = cv.rearrange("p (h k) -> p h k", h=8)
                g3 = eq[:, 0:128].rearrange("p (h k) -> p h k", h=8)
                m = dve(lambda cv3=cv3, g3=g3: V.tensor_tensor(g3, cv3, cv3[:, :, 0:1].broadcast_to((128, 8, 16)), ALU.subtract), prev)
                m = act(lambda: S.activation(eq[:, 0:128], eq[:, 0:128], ACT.Exp), m)
                yield
                m = dve(lambda g3=g3: V.tensor_reduce(sm[:, 104:112], g3, AX, ALU.add), m)
                m = dve(lambda: V.reciprocal(sm[:, 112:120], sm[:, 104:112]), m)
                mg_ = dve(lambda g3=g3, cv3=cv3: V.tensor_tensor(
                    cv3, g3, sm[:, 112:120].rearrange("p (h o) -> p h o", o=1).broadcast_to((128, 8, 16)), ALU.mult), m)
                m = dve(lambda cp=cp: V.tensor_scalar(cpa[:, :], cp, 4, None, ALU.logical_shift_right), mg_)
                m = dve(lambda: V.tensor_copy(cpf[:, 0, :], cpa[:, :]), m)
                m = dve(lambda cp=cp: V.tensor_scalar(cpa[:, :], cp, 15, None, ALU.bitwise_and), m)
                m = dve(lambda: V.tensor_copy(cpf[:, 1, :], cpa[:, :]), m)
                yield
                e4 = eq.rearrange("p (h k i) -> p h k i", h=8, k=16)
                e3 = eq.rearrange("p (a i) -> p a i", i=16)
                io = iota[:, 0:16].rearrange("p (o i) -> p o i", o=1).broadcast_to((128, 128, 16))
                for s2 in range(2):
                    ps_ = cpf[:, s2, :].rearrange("p (a o) -> p a o", o=1).broadcast_to((128, 128, 16))
                    m = dve(lambda ps_=ps_: V.tensor_tensor(e3, io, ps_, ALU.is_equal), m)
                    yield
                    for h in range(8):
                        tk = tf[:, t, 2 * h + s2, :].rearrange("p (o i) -> p o i", o=1).broadcast_to((128, 16, 16))
                        mx = pool(lambda h=h, tk=tk: G.tensor_tensor(e4[:, h, :, :], e4[:, h, :, :], tk, ALU.mult), m)
                        if h % 2:
                            yield
                    m = dve(lambda s2=s2: V.tensor_reduce(cpf[:, s2, :], e3, AX, ALU.add), mx)
                    yield
                yield
                b = take()
                pe(lambda b=b, cv=cv: TE.transpose(banks[b][:, 256:384], cv, ident), m, bank_free[b])
                for s2 in range(2):
                    last = pe(lambda s2=s2, b=b: TE.transpose(banks[b][:, s2 * 128:(s2 + 1) * 128], cpf[:, s2, :], ident), m)
                m = dve(lambda b=b, t=t: V.tensor_copy(rt[:, :, t * 128:(t + 1) * 128],
                                                       banks[b][:, 0:384].rearrange("p (a b) -> p a b", a=3)), last)
                free(b, m)
                rt_m.append(m)

        spawn(route_job())

        P3 = PR[:, :].rearrange("p (i t) -> p i t", t=T)
        gelu = {}

        def pre(c, b, m):
            if c >= 48:
                assert len(rt_m) == 2
            gelu["m"] = act(lambda: S.activation(flat(P3[:, 2 * c:2 * c + 2, :]), banks[b][:, :], ACT.Gelu),
                            m, rt_m[-1] if c >= 48 else None)
            free(b, gelu["m"])

        lin("u", 128, hk, mh2, pre)
        while fetch():
            pass
        drain()

        tb = [AB[:, 0:1024], AB[:, 1024:2048], flat(rT[:, 0:4, :])]
        ab_free = [m for s in sets["ab"] for m in slot_free[s]]
        tb_free = [None] * 3
        made = {}

        m_neg = dve(lambda: V.tensor_scalar(cpn, rt[:, 1, :], -1.0, None, ALU.mult), *rt_m)

        def tables(g):
            z, fr = tb[g % 3], tb_free[g % 3]
            a4 = z[:, 0:512].rearrange("p (t i) -> p t i", t=4)

            def per_token(row):
                return rt[:, row, 4 * g:4 * g + 4].rearrange("p (t o) -> p t o", o=1).broadcast_to((128, 4, 128))

            m = dve(lambda: V.tensor_tensor(a4, iota.rearrange("p (o i) -> p o i", o=1).broadcast_to((128, 4, 128)),
                                            per_token(0), ALU.is_equal), fr, *rt_m, *ab_free, apart=True)
            m_a = pool(lambda: G.tensor_tensor(a4, a4, per_token(2), ALU.mult), m, fr, apart=True)
            for i in range(3):
                t = 4 * g + i
                y = z[:, 512 + i * 128:512 + (i + 1) * 128]
                m = act(lambda y=y, t=t: S.activation(y, iota, ACT.Abs, bias=cpn[:, t:t + 1]), m_neg, fr, *ab_free, apart=True)
            y2 = z[:, 512:896]
            m = act(lambda: S.activation(y2, y2, ACT.Relu, scale=-1.0, bias=1.0), m)
            made[g, 0] = made[g, 1] = made[g, 2] = (m_a, m)
            for i in (3,):
                t = 4 * g + i
                y = z[:, 512 + i * 128:512 + (i + 1) * 128]
                m = dve(lambda y=y, t=t: V.tensor_scalar(y, iota, rt[:, 1, t:t + 1], None, ALU.is_equal), fr, apart=True)
                made[g, i] = (m_a, m)

        tables(0)
        tables(1)
        for g in range(64):
            z = tb[g % 3]
            b = take()
            for i in range(4):
                last = mm(banks[b][:, i * 128:(i + 1) * 128], z[:, 512 + i * 128:512 + (i + 1) * 128],
                          z[:, i * 128:(i + 1) * 128], True, True, *made[g, i], bank_free[b], inc=True)
            tb_free[g % 3] = last
            if g < 62:
                tables(g + 2)
            d = P3[:, :, 4 * g:4 * g + 4].rearrange("p i t -> p t i")
            m_G = dve(lambda d=d, b=b: V.tensor_tensor(d, banks[b][:, :].rearrange("p (t i) -> p t i", t=4), d, ALU.mult),
                      last, gelu["m"], apart=True)
            free(b, m_G)
        for s in sets["ab"]:
            slot_free[s] = (last,)
        limit[0] = [k[3] for k in queue].index("far2")

        Hf = H[:, :, :, :].rearrange("p a b c -> p (a b c)")
        cf = [(Hf[:, i * 512:i * 512 + 256], Hf[:, i * 512 + 256:i * 512 + 512]) for i in range(8)]
        cf_free = [None] * 8
        cfm = {}

        def coef(i):
            hi, lo = cf[i % 8]
            m = act(lambda: S.copy(hi, P3[:, i, :]), m_G, cf_free[i % 8], apart=True)
            cfm[i] = dve(lambda: V.tensor_tensor(lo, P3[:, i, :], hi.bitcast(F32), ALU.subtract), m, apart=True)

        ph.close()
        ph = ExitStack()
        far2 = sb("far2", [128, 6, UNIT], where=ph)
        add_slots("far2", [far2[:, i, :] for i in range(6)])
        ph2 = ExitStack()
        Ym = sb("Ym", [128, 2, 8, T], F32R, where=ph2)
        PB = sb("PB", [128, 20480], where=ph2)
        off[0] = 0
        base[0] = PB
        memT = tri3(scr(2048), 8)
        xkT, xv = scr(512), scr(512)
        x_m = []

        fb = [take() for _ in range(4)]
        for i in range(4):
            coef(i)
        for i in range(128):
            if i == 72:
                m_low = cfm[i]
                for s in sets["far2"]:
                    slot_free[s] = (m_low,)
                sets["far2"] = sets["far2"] + sets["four"]
                limit[0] = len(queue)
                l_mem = q.load("scalar", memT, A["memT"], m_low)
                mem_s = sumsq()
            if 76 <= i < 84:
                mem_s["add"](memT[:, i - 76, :], l_mem)
            if i == 86:
                hm = []
                spawn(norm_steps(hm, root(mem_s), memT, lambda j: vec("norm_mem_g", j), [m_low], None, (), Ym))
            if i == 104:
                lin("w2_xk", 2, of(Ym), lambda k: hm[k], copy_to(xkT, x_m))
                lin_nat("w2_xv", of_t(Ym), lambda k: hm[k], 256, nat_to(xv, 256, x_m))
            w, lw, done = unit("v")
            if i + 4 < 128:
                coef(i + 4)
            hi, lo = cf[i % 8]
            for t in range(2):
                for d in range(2):
                    ts_, ds_ = slice(t * 128, (t + 1) * 128), slice(d * 512, (d + 1) * 512)
                    last = mm3(banks[fb[2 * t + d]][:, :], (hi[:, ts_], lo[:, ts_]), (w[0][:, ds_], w[1][:, ds_]),
                               i == 0, i == 127, lw, cfm[i], bank_free[fb[2 * t + d]], inc=(t == 1 and d == 1))
            cf_free[i % 8] = last
            done(last)
        m_pv = last

        fn = scr(2048)
        m_f = []
        for i in range(4):
            if i % 2:
                m = act(lambda i=i: S.copy(fn[:, i * 512:(i + 1) * 512], banks[fb[i]][:, :]), m_pv)
            else:
                m = dve(lambda i=i: V.tensor_copy(fn[:, i * 512:(i + 1) * 512], banks[fb[i]][:, :]), m_pv)
            free(fb[i], m)
            m_f.append(m)
        m_x.clear()
        sums = sumsq()
        ev = resid(40, sums)
        for d in range(4):
            b = take()
            for j in range(2):
                for t in range(2):
                    c = 2 * d + j
                    src = fn[:, t * 1024 + c * 128:t * 1024 + (c + 1) * 128]
                    last = pe(lambda b=b, j=j, t=t, src=src: TE.transpose(
                        banks[b][:, j * T + t * 128:j * T + (t + 1) * 128], src, ident), *m_f, bank_free[b])
            ev(d, b, last)
        bmm = tri3(scr(3072), 8)
        l_bmm = q.load("scalar", bmm, A["bmm"], m_pv)
        mqT, mkT, mv = scr(1024), scr(1024), scr(1024)
        ccT = scr(512)
        uT = scr(2 * 258)
        ctmp = scr(512)
        gqk = scr(512)
        goT = scr(512)
        gv = scr(512)
        lrT = scr(256)
        sc_b = scr(3072)
        gt = scr(2560)

        drain()
        x3 = norm(xT, sums, lambda j: vec("final_g", j), keep=xT)
        sums = sumsq()
        for j in range(8):
            sums["add"](xT[:, j, :], x3[j])
        h3 = norm(xT, sums, lambda j: vec("norm_mix_g", j), dst=H)
        mh3 = lambda k: h3[k]
        l_g = q.load("scalar", gt[0:16, 1280:1408], A["w_gate"], m_pv)
        l_gb = q.load("scalar", gt[0:1, 1408:1536], A["b_gate"], m_pv)
        l_gc = q.load("scalar", gt[:, 1536:1792], A["gcst"], m_pv)

        z_m = []
        lin("w2_mq", 4, hk, mh3, copy_to(mqT, z_m))
        lin("w2_mk", 4, hk, mh3, copy_to(mkT, z_m))
        lin_nat("w2_mv", hkt, mh3, 512, nat_to(mv, 512, z_m))
        m_mo = z_m[-1]

        def bm_m(h, t, W):
            a = 0 if t == 0 else 128
            return bmm[:, h:h + 3:2, a:a + W]

        mb_done = {}
        spawn(attend(8, tri3(mqT, 4), tri3(mkT, 4), tri3(mv, 2), Ym, 2, lambda: [m_mo],
                     bm_m, lambda: [l_bmm], lambda t: t + 1, sm[:, 80:104], 0.125, sc_b, (m_mo,), mb_done))

        g_m = []
        lin("w2_gk", 2, hk, mh3, copy_to(gqk, g_m))
        lin_nat("w2_gv", hkt, mh3, 256, nat_to(gv, 256, g_m))
        m_gv = g_m[-1]
        w, lw, done = unit("w2_lr")
        b = take()
        for k in range(8):
            last = mm3(banks[b][:, 0:T], (w[0][:, k * 128:(k + 1) * 128], w[1][:, k * 128:(k + 1) * 128]), hk(k),
                       k == 0, k == 7, lw, bank_free[b], inc=(k == 7))
        done(last)
        m_lr = act(lambda b=b: S.copy(lrT[0:16, :], banks[b][0:16, 0:T]), last)
        free(b, m_lr)

        def go(c, b, m):
            n = act(lambda: S.activation(goT, banks[b][:, :], ACT.Silu), m)
            free(b, n)
            g_m.append(n)

        lin("w2_go", 2, hk, mh3, go)
        m_go = g_m[-1]
        gla_m = []
        sc_g = sb("sc_g", [128, 1792], where=ph2)

        def gla_job():
            tri64 = gt[:, 1536:1664]
            hmask = gt[:, 1664:1792]
            la = gt[:, 0:256]
            while not room(1):
                yield
            b = take()
            for t in range(2):
                o_ = banks[b][:, t * 128:(t + 1) * 128]
                mm(o_, lrT[0:16, t * 128:(t + 1) * 128], gt[0:16, 1280:1408], True, False, m_lr, l_g, bank_free[b])
                last = mm(o_, ones[0:1, :], gt[0:1, 1408:1536], False, True, l_gb, inc=True)
            zg = banks[b][:, 0:256]
            mab = m = act(lambda: S.activation(la, zg, ACT.Abs), last)
            m = act(lambda: S.activation(la, la, ACT.Exp, scale=-1.0), m)
            m = act(lambda: S.activation(la, la, ACT.Ln, bias=1.0), m)
            n = dve(lambda: V.tensor_scalar(gt[:, 256:512], zg, 0.0, None, ALU.min), mab)
            free(b, n)
            n = dve(lambda: V.tensor_tensor(la, gt[:, 256:512], la, ALU.subtract), n, m)
            n = dve(lambda: V.tensor_scalar(la, la, 1.0 / 16.0, None, ALU.mult), n)
            yield
            while not room(1):
                yield
            b = take()
            for t in range(2):
                last = mm(banks[b][:, t * 128:(t + 1) * 128], la[:, t * 128:(t + 1) * 128], tri64, True, True, n, l_gc,
                          bank_free[b], inc=True)
            bT = gt[:, 256:512]
            m = act(lambda b=b: S.copy(bT, banks[b][:, 0:256]), last)
            free(b, m)
            eb, en, kend = gt[:, 512:768], gt[:, 768:1024], gt[:, 1024:1280]
            m1 = act(lambda: S.activation(eb, bT, ACT.Exp), m)
            m2 = act(lambda: S.activation(en, bT, ACT.Exp, scale=-1.0), m)
            for c in range(4):
                act(lambda c=c: S.activation(kend[:, c * 64:(c + 1) * 64], bT[:, c * 64:(c + 1) * 64], ACT.Exp, scale=-1.0,
                                             bias=bT[:, c * 64 + 63:c * 64 + 64]), m)
            dec = sm[:, 120:124]
            m4 = act(lambda: S.activation(dec, bT[:, 63:256:64], ACT.Exp), m)
            yield
            gq, gk = gqk[:, 0:256], gqk[:, 256:512]
            dve(lambda: V.scalar_tensor_tensor(out=eb, in0=gq, scalar=32 ** -0.5, in1=eb, op0=ALU.mult, op1=ALU.mult), m1, g_m[0])
            dve(lambda: V.tensor_tensor(en, gk, en, ALU.mult), m2)
            m_qk = dve(lambda: V.tensor_tensor(kend, gk, kend, ALU.mult), m4)
            yield
            AT = sc_g[:, 0:1024].rearrange("p (h t c) -> p h t c", h=4, t=2)
            m_at = []
            for h in range(4):
                while not room(1):
                    yield
                b = take()
                for t in range(2):
                    last = mm(banks[b][:, t * 128:(t + 1) * 128], en[32 * h:32 * h + 32, t * 128:(t + 1) * 128],
                              eb[32 * h:32 * h + 32, t * 128:(t + 1) * 128], True, True, m_qk, bank_free[b], inc=True)
                m = act(lambda b=b, h=h: S.copy(AT[:, h, :, :], banks[b][:, 0:256].rearrange("p (t c) -> p t c", t=2)), last)
                free(b, m)
                m = pool(lambda h=h: G.affine_select(out=AT[:, h, :, :], in_=AT[:, h, :, :], compare_op=ALU.is_ge, fill=0.0,
                                                     base=0, pattern=[[0, 2], [1, 128]], channel_multiplier=-1), m)
                a4 = AT[:, h, :, 64:128]
                m = pool(lambda a4=a4: G.affine_select(out=a4, in_=a4, compare_op=ALU.is_ge, fill=0.0,
                                                       base=-64, pattern=[[0, 2], [0, 64]], channel_multiplier=1), m)
                m_at.append(m)
            while not room(1):
                yield
            b = take()
            for t in range(2):
                last = pe(lambda t=t, b=b: TE.transpose(banks[b][:, t * 128:(t + 1) * 128], kend[:, t * 128:(t + 1) * 128], ident),
                          m_qk, bank_free[b])
            keN = gt[:, 1792:2048]
            m_ke = act(lambda b=b: S.copy(keN, banks[b][:, 0:256]), last)
            free(b, m_ke)
            yield
            St = sc_g[:, 1024:1024 + 3 * 256].rearrange("p (c e) -> p c e", c=3)
            m_S = []
            hm2 = hmask.rearrange("p (h o) -> p h o", o=1)[:, 0:4, :].broadcast_to((128, 4, 64))
            for c in range(3):
                r = slice(64 * (c % 2), 64 * (c % 2) + 64)
                while not room(1):
                    yield
                b = take()
                last = mm(banks[b][:, 0:256], keN[r, (c // 2) * 128:(c // 2) * 128 + 128], gv[r, (c // 2) * 256:(c // 2) * 256 + 256],
                          True, True, m_ke, m_gv, bank_free[b], inc=True)
                m = dve(lambda b=b, c=c: V.tensor_tensor(St[:, c, :].rearrange("p (h e) -> p h e", h=4),
                                                         banks[b][:, 0:256].rearrange("p (h e) -> p h e", h=4), hm2, ALU.mult), last)
                free(b, m)
                if c:
                    m = dve(lambda c=c: V.scalar_tensor_tensor(out=St[:, c, :], in0=St[:, c - 1, :], scalar=dec[:, c:c + 1],
                                                               in1=St[:, c, :], op0=ALU.mult, op1=ALU.add), m)
                m_S.append(m)
            yield
            oT = gt[:, 2048:2560].rearrange("p (a b) -> p a b", a=2)
            for pr in range(2):
                while not room(1):
                    yield
                b = take()
                for t in range(2):
                    for j in range(2):
                        h = 2 * pr + j
                        mm(banks[b][64 * j:64 * j + 64, t * 128:(t + 1) * 128], gv[:, t * 256 + 64 * h:t * 256 + 64 * h + 64],
                           AT[:, h, t, :], t == 0, False, m_at[h], m_gv, bank_free[b])
                for c in range(1, 4):
                    last = mm(banks[b][:, c * 64:(c + 1) * 64], St[:, c - 1, pr * 128:(pr + 1) * 128],
                              eb[:, c * 64:(c + 1) * 64], False, True, m_S[c - 1], inc=True)
                m_o = act(lambda b=b, pr=pr: S.copy(oT[:, pr, :], banks[b][:, 0:256]), last)
                free(b, m_o)
            yield
            oF = gt[:, 2048:2560]
            sqg = gt[:, 0:512]
            m = act(lambda: S.activation(sqg, oF, ACT.Square), m_o)
            while not room(1):
                yield
            b = take()
            last = mm(banks[b][:, :], bd64, sqg, True, True, m, bank_free[b], inc=True)
            ms = sc_g[:, 1024:1536]
            rr = sc_g[:, 0:512]
            m = dve(lambda: V.tensor_scalar(ms, banks[b][:, :], 1.0 / 64, EPS, ALU.mult, ALU.add), last)
            free(b, m)
            m = act(lambda: S.activation(sqg, ms, ACT.Sqrt), m)
            yield
            m = dve(lambda: V.reciprocal(rr, sqg), m)
            m = newton(rr, ms, sqg, m)
            yield
            m = dve(lambda: V.scalar_tensor_tensor(out=oF, in0=oF, scalar=vec("gla_norm_g", 0), in1=rr, op0=ALU.mult, op1=ALU.mult), m)
            m = dve(lambda: V.tensor_tensor(oF, oF, goT, ALU.mult), m, m_go)
            gla_m.append(cut(flat(Ym[:, 0, 6:8, :]), flat(Ym[:, 1, 6:8, :]), oF, m))

        spawn(gla_job())

        lin("w2_cc", 2, hk, mh3, copy_to(ccT, z_m))
        m_cc = z_m[-1]
        uv = uT.rearrange("p (a b) -> p a b", a=2)
        m_z = pool(lambda: G.memset(uv[:, :, 0:2], 0.0), m_pv)
        m_u = []

        def ch(c, b, m):
            m_u.append(dve(lambda: V.tensor_tensor(uv[:, :, 2:258], tri3(banks[b][:, :], 2), tri3(ccT, 2), ALU.mult), m, m_cc))
            free(b, m_u[-1])

        lin("w2_ch", 2, hk, mh3, ch)

        def cb(c, b, m):
            for j in range(2):
                t_ = ctmp[:, j * 256:(j + 1) * 256]
                n = dve(lambda j=j, t_=t_: V.tensor_scalar(t_, uv[:, j, 2:258], vec("sc_w", 2 * 2 + j), vec("sc_b", j), ALU.mult, ALU.add),
                        m_u[-1], m_z)
                for tap in (1, 0):
                    n = dve(lambda j=j, t_=t_, tap=tap: V.scalar_tensor_tensor(
                        out=t_, in0=uv[:, j, tap:tap + 256], scalar=vec("sc_w", 2 * tap + j), in1=t_,
                        op0=ALU.mult, op1=ALU.add), n)
            n = dve(lambda: V.tensor_tensor(ctmp, banks[b][:, :], ctmp, ALU.mult), n, m)
            free(b, n)
            m_u.append(cut(flat(Ym[:, 0, 0:2, :]), flat(Ym[:, 1, 0:2, :]), ctmp, n))

        lin("w2_cb", 2, hk, mh3, cb)
        m_conv = m_u[-1]
        drain()

        def m_cat(k):
            return m_conv if k < 2 else gla_m[0] if k >= 6 else mb_done[k - 2]

        m_x.clear()
        sums = sumsq()
        lin("w2_o", 8, of(Ym), m_cat, resid(None, sums))
        drain()
        h4 = norm(xT, sums, lambda j: vec("norm_xattn_g", j), dst=H)
        xqT = ctmp
        x_q = []
        lin("w2_xq", 2, hk, lambda k: h4[k], copy_to(xqT, x_q))
        xo_done = {}
        spawn(attend(4, tri3(xqT, 2), tri3(xkT, 2), tri3(xv, 2), Ym, 0, lambda: [x_q[-1], x_m[-1]],
                     None, lambda: [], lambda t: 2, sm[:, 80:104], 0.125, sc_b, (m_x[-1],), xo_done))
        drain()
        m_x.clear()
        sums = sumsq()
        lin("w2_xo", 8, of(Ym), lambda k: xo_done[k], resid(None, sums), kt=2)
        drain()
        x_end = m_x[-1]
        ph2.close()
        act_t = sb("act_t", [128, 2, 22, T], F32R, where=ph)
        split4 = sb("split4", [128, 4, 2, UNIT], F32R, where=ph)
        add_bufs(split4, 4, x_end)
        ahead[0] = 7
        share[0] = 3
        tmp = sb("ftmp", [128, 4, 768], where=ph)
        h5 = norm(xT, sums, lambda j: vec("norm_ffn_g", j), dst=H)
        m_act = {}

        def ffn(c, b, m):
            a, g, e = (tmp[:, c % 4, i * 256:(i + 1) * 256] for i in range(3))
            fr = m_act[c - 4] if c >= 4 else m_x[-1]
            bank = banks[b]
            parts = [(d, bank[:, j * T:(j + 1) * T], 2 * c + j) for j, d in ((0, a), (1, g))]
            mk = [act(lambda d=d, z=z, i=i: S.activation(d, z, ACT.Identity, bias=vec("f_b", i), scale=vec("f_w", 2 * 44 + i)),
                      m, fr, apart=True) for d, z, i in parts]

            def later():
                yield
                n = [dve(lambda d=d, z=z, i=i: V.scalar_tensor_tensor(out=d[:, 1:256], in0=z[:, 0:255], scalar=vec("f_w", 44 + i),
                                                                      in1=d[:, 1:256], op0=ALU.mult, op1=ALU.add),
                         mk[1], apart=True) for x, (d, z, i) in enumerate(parts)]
                n = [dve(lambda d=d, z=z, i=i: V.scalar_tensor_tensor(out=d[:, 2:256], in0=z[:, 0:254], scalar=vec("f_w", i),
                                                                      in1=d[:, 2:256], op0=ALU.mult, op1=ALU.add),
                         n[x], apart=True) for x, (d, z, i) in enumerate(parts)]
                free(b, n[1])
                ea = act(lambda: S.activation(e, a, ACT.Silu), n[0], fr, apart=True)
                yield
                x = dve(lambda: V.tensor_tensor(e, e, g, ALU.mult), n[1], ea, apart=True)
                hi, lo = act_t[:, 0, c, :], act_t[:, 1, c, :]
                yield
                x = act(lambda: S.copy(hi, e), x, apart=True)
                yield
                m_act[c] = dve(lambda: V.tensor_tensor(lo, e, hi.bitcast(F32), ALU.subtract), x, apart=True)

            spawn(later())

        lin("w_up", 44, hk, lambda k: h5[k], ffn, conc=6)
        m_x.clear()
        sums = sumsq()
        pump(6)
        pump(6)
        lin("w_dn", 8, of(act_t), lambda k: m_act[k], resid(None, sums), kt=22)
        drain()
        h6 = norm(xT, sums, lambda j: vec("final_norm_g", j), keep=xT)
        done_ = []
        for j in range(8):
            done_.append(q.load("sync", out[:, j, :], xT[:, j, :], h6[j]))
        assert taken[0] == len(queue) == len(ready)

        block = ctx.enter_context(nc.Block())

        @block.sync
        def _(e):
            q.emit("sync", e)
            for _, s_, v_ in done_:
                e.wait_ge(s_, v_)

        @block.tensor
        def _(e):
            q.emit("tensor", e)

        @block.vector
        def _(e):
            q.emit("vector", e)

        @block.scalar
        def _(e):
            q.emit("scalar", e)

        @block.gpsimd
        def _(e):
            q.emit("gpsimd", e)
        ph.close()


def bucket(n):
    me = 16
    nf = np.maximum(n, 1).astype(np.float32)
    large = me + (np.log(nf / np.float32(me)) / np.float32(math.log(128 / me)) * np.float32(16)).astype(np.int32)
    return np.where(n < me, n, np.minimum(large, 31))


def constants():
    p = np.arange(128)
    f = np.float32
    cst = np.concatenate([
        np.eye(128), np.ones((128, 128)), (p[:, None] > p[None, :]), (p[None, :] > p[:, None]),
        (p[:, None] // 64 == p[None, :] // 64), np.broadcast_to(p[None, :], (128, 128))], 1).astype(f)
    oh = np.zeros((32, 384), f)
    for col in range(384):
        n = 255 - col
        if n >= 0:
            oh[bucket(np.array(n)), col] = 1.0
    same = (p[:, None] // 64 == p[None, :] // 64) & (p[:, None] <= p[None, :])
    hm = np.zeros((128, 128), f)
    for h in range(4):
        hm[32 * h:32 * h + 32, h] = 1.0
    gc = np.concatenate([same.astype(f), hm], 1)
    bmm = np.full((128, 8, 384), NEG, f)
    for h in range(8):
        slope = f(2.0 ** -(h + 1))
        for t in range(2):
            q_, k_ = 128 * t + p[:, None], np.arange(128 * (t + 1))[None, :]
            v = np.where(q_ >= k_, -(slope * (q_ - k_).astype(f)), NEG)
            bmm[:, h, (0 if t == 0 else 128):(128 if t == 0 else 384)] = v
    return cst, oh, gc, bmm


def tiles(w, kt, per):
    K, N = w.shape
    a = w.reshape(kt, 128, N // 128, 128).transpose(2, 1, 0, 3).reshape(N // 128 // per, per, 128, kt * 128)
    return np.ascontiguousarray(a.transpose(0, 2, 1, 3).reshape(N // 128 // per, 128, per * kt * 128))


def rows(w, width):
    kk = NC // width
    a = w.reshape(8 // kk, kk, 128, width).transpose(0, 2, 1, 3)
    return np.ascontiguousarray(a.reshape(8 // kk, 128, NC))


def cols(v):
    v = v.reshape(-1)
    return v.reshape(-1, 128).T


def lay_out(i):
    f = {k: np.asarray(v) for k, v in i.items()}
    A = {}
    w = f["w_in"][0]
    o = np.cumsum([0, 512, 512, 512, 512, 64, 8, 512, 512, 512, 1024, 1024])
    part = [w[:, o[n]:o[n + 1]] for n in range(11)]
    A["w_ada"] = np.ascontiguousarray(f["w_ada"][0].reshape(8, 128, 6, 1024).transpose(2, 0, 1, 3).reshape(48, 128, 1024))
    A["w_qa"], A["w_ka"], A["w_qi"] = tiles(part[0], 8, 2), tiles(part[1], 8, 2), tiles(part[3], 8, 2)
    A["w_ki"] = tiles(np.concatenate([part[4], part[4]], 1), 8, 1)
    pad = lambda a, n: np.concatenate([a, np.zeros((a.shape[0], n - a.shape[1]), a.dtype)], 1)
    A["w_wi"] = tiles(pad(part[5], 128), 8, 1)
    A["w_va"], A["w_vb"] = rows(part[2], 512), rows(part[8], 512)
    A["w_qb"], A["w_kb"] = tiles(part[6], 8, 2), tiles(part[7], 8, 2)
    A["w_g"] = tiles(np.concatenate([part[9], part[10]], 1), 8, 2)
    A["w_pa"], A["w_pb"] = tiles(f["w_proj_a"][0], 4, 4), tiles(f["w_proj_b"][0], 4, 4)
    A["w_o"] = tiles(f["w_out"][0], 8, 2)
    A["w_pq"] = tiles(f["peer_wq"][0], 8, 2)
    A["sub_keys"] = np.ascontiguousarray(f["peer_sub_keys"][0].reshape(16, 128, 128).transpose(2, 0, 1).reshape(128, 2048))
    A["u"] = np.ascontiguousarray(
        f["peer_u"][0].reshape(64, 2, 128, 8, 128).transpose(0, 4, 1, 3, 2).reshape(64, 128, 2048))
    A["v"] = np.ascontiguousarray(f["peer_v"][0].reshape(64, 2, 128, 1024).transpose(0, 2, 1, 3).reshape(64, 128, 2048))
    w = f["w_in_2"][0]
    o = np.cumsum([0, 256, 256, 256, 512, 512, 512, 128, 128, 256, 256, 16])
    p2 = [w[:, o[n]:o[n + 1]] for n in range(11)]
    A["w2_cb"], A["w2_cc"], A["w2_ch"] = (tiles(p2[n], 8, 2) for n in range(3))
    A["w2_mq"], A["w2_mk"], A["w2_mv"] = tiles(p2[3], 8, 2), tiles(p2[4], 8, 2), rows(p2[5], 512)
    A["w2_gk"] = tiles(np.concatenate([p2[6], p2[7]], 1), 8, 2)
    A["w2_gv"], A["w2_go"] = rows(p2[8], 256), tiles(p2[9], 8, 2)
    A["w2_lr"] = tiles(pad(p2[10], 128), 8, 1)
    A["w2_o"] = tiles(f["w_out_2"][0], 8, 2)
    A["w2_xq"] = tiles(f["xattn_wq_2"][0], 8, 2)
    kv = f["xattn_wkv_2"][0]
    A["w2_xk"], A["w2_xv"] = tiles(kv[:, 0:256], 8, 2), rows(kv[:, 256:512], 256)
    A["w2_xo"] = tiles(f["xattn_wo_2"][0], 2, 8)

    def ag(a):
        x, y = pad(a[:, :2752], 2816).reshape(-1, 22, 1, 128), pad(a[:, 2752:], 2816).reshape(-1, 22, 1, 128)
        return np.concatenate([x, y], 2).reshape(a.shape[0], 5632)

    A["w_up"] = tiles(ag(f["ffn_w_up_2"][0]), 8, 2)
    dn = pad(f["ffn_w_down_2"][0].T, 2816).T
    A["w_dn"] = np.ascontiguousarray(
        dn.reshape(22, 128, 8, 128).transpose(2, 0, 1, 3).reshape(22, 8, 128, 128).transpose(0, 2, 1, 3).reshape(22, 128, 1024))
    A["xT"] = np.ascontiguousarray(f["x"][0].T.reshape(8, 128, 256).transpose(1, 0, 2))
    A["memT"] = np.ascontiguousarray(f["mem_2"][0].T.reshape(8, 128, 256).transpose(1, 0, 2))
    A["rel_bias"] = f["rel_bias"]
    A["w_gate"] = f["gla_w_gate_2"][0]
    A["b_gate"] = f["gla_b_gate_2"]
    parts = [("c", cols(f["c"])), ("b_ada", cols(f["b_ada"])), ("norm1_g", cols(f["norm1_g"])),
             ("norm2_g", cols(f["norm2_g"])), ("final_g", cols(f["final_g"])), ("norm_mix_g", cols(f["norm_mix_g_2"])),
             ("norm_xattn_g", cols(f["norm_xattn_g_2"])), ("norm_mem_g", cols(f["norm_mem_g_2"])),
             ("norm_ffn_g", cols(f["norm_ffn_g_2"])), ("final_norm_g", cols(f["final_norm_g_2"])),
             ("sc_w", cols(f["sc_conv_w_2"])), ("sc_b", cols(f["sc_conv_b_2"])),
             ("gla_norm_g", np.concatenate([f["gla_norm_g_2"], f["gla_norm_g_2"]], 1).T),
             ("f_w", cols(ag(f["ffn_conv_w_2"][0]))), ("f_b", cols(ag(f["ffn_conv_b_2"])))]
    voff, n = {}, 0
    for name, a in parts:
        voff[name] = n
        n += a.shape[1]
    A["vecs"] = np.ascontiguousarray(np.concatenate([a for _, a in parts], 1))
    A["cst"], A["oh"], A["gcst"], A["bmm"] = constants()
    return A, voff


def kernel(**inputs):
    import concourse.bacc as bacc
    from concourse.bass_utils import run_bass_kernel_spmd

    arrays, voff = lay_out(inputs)
    nc = bacc.Bacc("TRN2", target_bir_lowering=False, num_devices=1)
    A, feeds = {}, {}
    for name, a in arrays.items():
        A[name] = nc.dram_tensor(f"in_{name}", a.shape, mybir.dt.from_np(a.dtype), kind="ExternalInput").ap()
        feeds[f"in_{name}"] = a
    A["voff"] = voff
    scratch = nc.dram_tensor("skew", (8, 128, 384), F32, kind="Internal").ap()
    out = nc.dram_tensor("out_0", (128, 8, 256), F32, kind="ExternalOutput").ap()
    build(nc, A, out, scratch)
    r = run_bass_kernel_spmd(nc, [feeds], core_ids=[0])
    y = r.results[0]["out_0"]
    return np.ascontiguousarray(np.asarray(y).transpose(2, 1, 0).reshape(1, 256, 1024))
```
